# Optimizing a Trainium2 kernel written in Bass

```python
import jax, jax.numpy as jnp
from jax import lax
import numpy as np

D_MODEL = 1024
BATCH = 1
SEQ = 512
DEPTH = 1
DEC_BATCH = 8
DEC_SEQ = 16
PAST_LEN = 1024

CHUNK = 64
Q_BLOCK = 128
MLA_HEADS = 8
NOPE_DIM = 64
ROPE_DIM = 32
V_DIM = 64
Q_LORA = 384
KV_LORA = 256
ROPE_THETA = 10000.0
ATTN_SCALE = (NOPE_DIM + ROPE_DIM) ** -0.5
ML_HEADS = 4
ML_DIM = 128
ML_WIDTH = ML_HEADS * ML_DIM
CONV_W = 4
MIX_WIDTH = MLA_HEADS * V_DIM + ML_WIDTH
IN_SIZES = (Q_LORA, KV_LORA, ROPE_DIM, ML_WIDTH, ML_WIDTH, ML_WIDTH, ML_WIDTH, 2 * ML_HEADS)
IN_SPLITS = tuple(int(v) for v in np.cumsum(IN_SIZES)[:-1])
IN_COLS = int(sum(IN_SIZES))
N_EXPERTS = 32
TOP_K = 4
D_FF = 1024
SWIGLU_LIMIT = 7.0
SWIGLU_ALPHA = 1.702
MOE_BLOCK = 128
ALPHA_RES = (2.0 * DEPTH) ** 0.25
BETA_INIT = (8.0 * DEPTH) ** -0.25
EPS = 1e-5

kernel_name = 'mla_mlstm_moe_streaming_step'

def layer_norm(x, g, b):
    xf = x.astype(jnp.float32)
    mu = jnp.mean(xf, -1, keepdims=True)
    var = jnp.mean(jnp.square(xf - mu), -1, keepdims=True)
    return ((xf - mu) * lax.rsqrt(var + EPS) * g + b).astype(x.dtype)

def rms_norm(x, g):
    xf = x.astype(jnp.float32)
    return (xf * lax.rsqrt(jnp.mean(xf * xf, -1, keepdims=True) + EPS) * g).astype(x.dtype)

def rope(x, pos):
    half = ROPE_DIM // 2
    inv = ROPE_THETA ** (-jnp.arange(half, dtype=jnp.float32) / half)
    ang = (pos.astype(jnp.float32)[:, None] * inv).reshape((pos.shape[0],) + (1,) * (x.ndim - 3) + (half,))
    cos, sin = jnp.cos(ang), jnp.sin(ang)
    x1, x2 = x[..., :half].astype(jnp.float32), x[..., half:].astype(jnp.float32)
    return jnp.concatenate([x1 * cos - x2 * sin, x1 * sin + x2 * cos], -1).astype(x.dtype)

def ada(c, w, b):
    e = jax.nn.silu(c) @ w + b
    return jnp.split(e[:, None, :], 6, axis=-1)

def mixer_inputs(u, pos, p):
    B, T, _ = u.shape
    z = u @ p['w_in']
    cq, ckv, kr, mq, mk, mv, mo, mif = jnp.split(z, IN_SPLITS, axis=-1)
    q = (rms_norm(cq, p['q_norm_g']) @ p['w_uq']).reshape(B, T, MLA_HEADS, NOPE_DIM + ROPE_DIM)
    q_rope = rope(q[..., NOPE_DIM:], pos)
    q_lat = jnp.einsum('bthn,lhn->bthl', q[..., :NOPE_DIM], p['w_uk'])
    ckv = rms_norm(ckv, p['kv_norm_g'])
    kr = rope(kr, pos)
    gates = (mif + p['b_if']).astype(jnp.float32)
    ig = gates[..., :ML_HEADS]
    lf = jax.nn.log_sigmoid(gates[..., ML_HEADS:])
    return q_lat, q_rope, ckv, kr, jnp.concatenate([mq, mk], -1), mv, mo, ig, lf

def mla_attend(q_lat, q_rope, ckv, kr, q_pos, k_pos):
    s = (jnp.einsum('bqhl,bkl->bhqk', q_lat, ckv, preferred_element_type=jnp.float32)
         + jnp.einsum('bqhr,bkr->bhqk', q_rope, kr, preferred_element_type=jnp.float32)) * ATTN_SCALE
    visible = (k_pos[None, :] // CHUNK) <= (q_pos[:, None] // CHUNK)
    pr = jax.nn.softmax(jnp.where(visible, s, -jnp.inf), axis=-1)
    return jnp.einsum('bhqk,bkl->bqhl', pr.astype(ckv.dtype), ckv)

def mla_prompt(q_lat, q_rope, ckv, kr, pos):
    B, S, H, L = q_lat.shape
    nb = S // Q_BLOCK

    def blocks(a):
        return jnp.swapaxes(a.reshape((B, nb, Q_BLOCK) + a.shape[2:]), 0, 1)

    def one(args):
        ql, qr, qp = args
        return mla_attend(ql, qr, ckv, kr, qp, pos)

    o = lax.map(one, (blocks(q_lat), blocks(q_rope), pos.reshape(nb, Q_BLOCK)))
    return jnp.swapaxes(o, 0, 1).reshape(B, S, H, L)

def mlstm_qkv(qk_pre, conv_buf, mv, p):
    B, T, _ = qk_pre.shape
    xpad = jnp.concatenate([conv_buf.astype(qk_pre.dtype), qk_pre], 1)
    qk = sum(xpad[:, j:j + T] * p['conv_w'][j] for j in range(CONV_W)) + p['conv_b']
    qk = jax.nn.silu(qk.astype(jnp.float32))
    q = qk[..., :ML_WIDTH].reshape(B, T, ML_HEADS, ML_DIM)
    k = qk[..., ML_WIDTH:].reshape(B, T, ML_HEADS, ML_DIM) * (ML_DIM ** -0.5)
    v = mv.astype(jnp.float32).reshape(B, T, ML_HEADS, ML_DIM)
    return q, k, v, xpad[:, -(CONV_W - 1):]

def mlstm_chunk(carry, inp):
    C, n, m = carry
    q, k, v, ig, lf = inp
    L = q.shape[1]
    F = jnp.cumsum(lf, axis=1)
    m_t = F + jnp.maximum(m[:, None], lax.cummax(ig - F, axis=1))
    carry_w = jnp.exp(m[:, None] + F - m_t)
    causal = jnp.tril(jnp.ones((L, L), bool))[None, :, :, None]
    logd = F[:, :, None] - F[:, None, :] + ig[:, None, :] - m_t[:, :, None]
    w = jnp.exp(jnp.where(causal, logd, -jnp.inf)) * jnp.einsum('bthd,bshd->btsh', q, k)
    num = carry_w[..., None] * jnp.einsum('bthd,bhde->bthe', q, C) + jnp.einsum('btsh,bshe->bthe', w, v)
    den = carry_w * jnp.einsum('bthd,bhd->bth', q, n) + jnp.sum(w, axis=2)
    h = num / jnp.maximum(jnp.abs(den), jnp.exp(-m_t))[..., None]
    m_new = m_t[:, -1]
    ws = jnp.exp(ig + F[:, -1:] - F - m_new[:, None])
    decay = jnp.exp(m + F[:, -1] - m_new)
    C_new = decay[..., None, None] * C + jnp.einsum('bsh,bshd,bshe->bhde', ws, k, v)
    n_new = decay[..., None] * n + jnp.einsum('bsh,bshd->bhd', ws, k)
    return (C_new, n_new, m_new), h

def mlstm_prompt(q, k, v, ig, lf):
    B, S, H, Dh = q.shape
    nc = S // CHUNK

    def chunks(a):
        return jnp.swapaxes(a.reshape((B, nc, CHUNK) + a.shape[2:]), 0, 1)

    init = (jnp.zeros((B, H, Dh, Dh), jnp.float32), jnp.zeros((B, H, Dh), jnp.float32),
            jnp.zeros((B, H), jnp.float32))
    (C, n, m), h = lax.scan(mlstm_chunk, init, (chunks(q), chunks(k), chunks(v), chunks(ig), chunks(lf)))
    return jnp.swapaxes(h, 0, 1).reshape(B, S, H, Dh), C, n, m

def mixer_out(o_lat, h, mo, p):
    B, T = o_lat.shape[:2]
    att = jnp.einsum('bthl,lhv->bthv', o_lat, p['w_uv']).reshape(B, T, MLA_HEADS * V_DIM)
    mu = jnp.mean(h, -1, keepdims=True)
    var = jnp.mean(jnp.square(h - mu), -1, keepdims=True)
    hn = (h - mu) * lax.rsqrt(var + EPS) * p['ml_norm_g'].reshape(ML_HEADS, ML_DIM)
    ml = jax.nn.sigmoid(mo.astype(jnp.float32)) * hn.reshape(B, T, ML_WIDTH)
    return jnp.concatenate([att, ml.astype(att.dtype)], -1) @ p['w_o']

def moe(t, p):
    n_tok = t.shape[0]
    n_asg = n_tok * TOP_K
    logits = jnp.einsum('nd,de->ne', t, p['router_w'], preferred_element_type=jnp.float32) + p['router_b']
    vals, idx = lax.top_k(logits, TOP_K)
    wts = jax.nn.softmax(vals, axis=-1).reshape(-1)
    exp_flat = idx.reshape(-1)
    tok_flat = jnp.arange(n_asg, dtype=jnp.int32) // TOP_K
    order = jnp.argsort(exp_flat)
    exp_s, w_s, tok_s = exp_flat[order], wts[order], tok_flat[order]
    counts = jnp.bincount(exp_flat, length=N_EXPERTS)
    padded = (counts + MOE_BLOCK - 1) // MOE_BLOCK * MOE_BLOCK
    starts = jnp.cumsum(counts) - counts
    pends = jnp.cumsum(padded)
    pstarts = pends - padded
    n_blocks = (n_asg + N_EXPERTS * (MOE_BLOCK - 1) + MOE_BLOCK - 1) // MOE_BLOCK
    n_rows = n_blocks * MOE_BLOCK
    dest = pstarts[exp_s] + jnp.arange(n_asg, dtype=jnp.int32) - starts[exp_s]
    row_tok = jnp.zeros((n_rows,), jnp.int32).at[dest].set(tok_s)
    row_w = jnp.zeros((n_rows,), jnp.float32).at[dest].set(w_s)
    block_exp = jnp.minimum(jnp.searchsorted(pends, jnp.arange(n_blocks) * MOE_BLOCK, side='right'),
                            N_EXPERTS - 1)

    def expert_block(args):
        e, toks, w = args
        hh = t[toks] @ p['w_up'][e] + p['b_up'][e]
        glu = jnp.minimum(hh[:, :D_FF], SWIGLU_LIMIT)
        lin = jnp.clip(hh[:, D_FF:], -SWIGLU_LIMIT, SWIGLU_LIMIT)
        y = (glu * jax.nn.sigmoid(SWIGLU_ALPHA * glu) * (lin + 1.0)) @ p['w_down'][e] + p['b_down'][e]
        return y.astype(jnp.float32) * w[:, None]

    y = lax.map(expert_block, (block_exp, row_tok.reshape(n_blocks, MOE_BLOCK), row_w.reshape(n_blocks, MOE_BLOCK)))
    out = jax.ops.segment_sum(y.reshape(n_rows, D_MODEL), row_tok, num_segments=n_tok)
    return out.astype(t.dtype)

def layer(xp, xs, cp, cs, ckv_past, kr_past, C0, n0, m0, conv0, p):
    Bp, S, _ = xp.shape
    Bs, T, _ = xs.shape
    past = ckv_past.shape[1]
    shp1, scp1, gp1, shp2, scp2, gp2 = ada(cp, p['w_ada'], p['b_ada'])
    shs1, scs1, gs1, shs2, scs2, gs2 = ada(cs, p['w_ada'], p['b_ada'])
    pos_p = jnp.arange(S)
    pos_s = past + jnp.arange(T)

    up = xp * (1.0 + scp1) + shp1
    ql, qr, ckv_p, kr_p, qk_p, mv_p, mo_p, ig_p, lf_p = mixer_inputs(up, pos_p, p)
    o_p = mla_prompt(ql, qr, ckv_p, kr_p, pos_p)
    q, k, v, conv_p = mlstm_qkv(qk_p, jnp.zeros((Bp, CONV_W - 1, 2 * ML_WIDTH), qk_p.dtype), mv_p, p)
    h_p, C_p, n_p, m_p = mlstm_prompt(q, k, v, ig_p, lf_p)
    xp = layer_norm(ALPHA_RES * xp + gp1 * mixer_out(o_p, h_p, mo_p, p), p['ln1_g'], p['ln1_b'])

    us = xs * (1.0 + scs1) + shs1
    ql, qr, ckv_s, kr_s, qk_s, mv_s, mo_s, ig_s, lf_s = mixer_inputs(us, pos_s, p)
    o_s = mla_attend(ql, qr, jnp.concatenate([ckv_past.astype(ckv_s.dtype), ckv_s], 1),
                     jnp.concatenate([kr_past.astype(kr_s.dtype), kr_s], 1), pos_s, jnp.arange(past + T))
    q, k, v, conv_s = mlstm_qkv(qk_s, conv0, mv_s, p)
    (C_s, n_s, m_s), h_s = mlstm_chunk((C0.astype(jnp.float32), n0.astype(jnp.float32), m0.astype(jnp.float32)),
                                       (q, k, v, ig_s, lf_s))
    xs = layer_norm(ALPHA_RES * xs + gs1 * mixer_out(o_s, h_s, mo_s, p), p['ln1_g'], p['ln1_b'])

    u2 = jnp.concatenate([(xp * (1.0 + scp2) + shp2).reshape(Bp * S, D_MODEL),
                          (xs * (1.0 + scs2) + shs2).reshape(Bs * T, D_MODEL)], 0)
    f = moe(u2, p)
    xp = layer_norm(ALPHA_RES * xp + gp2 * f[:Bp * S].reshape(Bp, S, D_MODEL), p['ln2_g'], p['ln2_b'])
    xs = layer_norm(ALPHA_RES * xs + gs2 * f[Bp * S:].reshape(Bs, T, D_MODEL), p['ln2_g'], p['ln2_b'])
    return xp, xs, (ckv_p, kr_p, C_p, n_p, m_p, conv_p, ckv_s, kr_s, C_s, n_s, m_s, conv_s)

def setup_inputs(seed: int = 0) -> dict:
    key = jax.random.key(seed)
    ks = jax.random.split(key, 40)
    L = DEPTH

    def nrm(k, shape, s=1.0):
        return s * jax.random.normal(k, shape, jnp.float32)

    b_if = jnp.concatenate([nrm(ks[14], (L, ML_HEADS), 0.1),
                            jnp.linspace(3.0, 6.0, ML_HEADS, dtype=jnp.float32)[None]
                            + nrm(ks[15], (L, ML_HEADS), 0.01)], -1)
    return {
        'x_prompt': nrm(ks[0], (BATCH, SEQ, D_MODEL)),
        'x_sample': nrm(ks[1], (DEC_BATCH, DEC_SEQ, D_MODEL)),
        'c_prompt': nrm(ks[2], (BATCH, D_MODEL)),
        'c_sample': nrm(ks[3], (DEC_BATCH, D_MODEL)),
        'cache_ckv': nrm(ks[4], (L, DEC_BATCH, PAST_LEN, KV_LORA)),
        'cache_kr': nrm(ks[5], (L, DEC_BATCH, PAST_LEN, ROPE_DIM)),
        'state_C': nrm(ks[6], (L, DEC_BATCH, ML_HEADS, ML_DIM, ML_DIM), 0.1),
        'state_n': nrm(ks[7], (L, DEC_BATCH, ML_HEADS, ML_DIM), 0.3),
        'state_m': 1.0 + nrm(ks[8], (L, DEC_BATCH, ML_HEADS), 0.5),
        'state_conv': nrm(ks[9], (L, DEC_BATCH, CONV_W - 1, 2 * ML_WIDTH)),
        'w_ada': nrm(ks[10], (L, D_MODEL, 6 * D_MODEL), D_MODEL ** -0.5),
        'b_ada': nrm(ks[11], (L, 6 * D_MODEL), 0.02),
        'w_in': nrm(ks[12], (L, D_MODEL, IN_COLS), D_MODEL ** -0.5),
        'b_if': b_if,
        'conv_w': nrm(ks[16], (L, CONV_W, 2 * ML_WIDTH), CONV_W ** -0.5),
        'conv_b': nrm(ks[17], (L, 2 * ML_WIDTH), 0.02),
        'q_norm_g': 1.0 + nrm(ks[18], (L, Q_LORA), 0.02),
        'w_uq': nrm(ks[19], (L, Q_LORA, MLA_HEADS * (NOPE_DIM + ROPE_DIM)), Q_LORA ** -0.5),
        'kv_norm_g': 1.0 + nrm(ks[20], (L, KV_LORA), 0.02),
        'w_uk': nrm(ks[21], (L, KV_LORA, MLA_HEADS, NOPE_DIM), KV_LORA ** -0.5),
        'w_uv': nrm(ks[22], (L, KV_LORA, MLA_HEADS, V_DIM), KV_LORA ** -0.5),
        'ml_norm_g': 1.0 + nrm(ks[23], (L, ML_WIDTH), 0.02),
        'w_o': nrm(ks[24], (L, MIX_WIDTH, D_MODEL), BETA_INIT * MIX_WIDTH ** -0.5),
        'ln1_g': 1.0 + nrm(ks[25], (L, D_MODEL), 0.02),
        'ln1_b': nrm(ks[26], (L, D_MODEL), 0.02),
        'router_w': nrm(ks[27], (L, D_MODEL, N_EXPERTS), D_MODEL ** -0.5),
        'router_b': nrm(ks[28], (L, N_EXPERTS), 0.01),
        'w_up': nrm(ks[29], (L, N_EXPERTS, D_MODEL, 2 * D_FF), D_MODEL ** -0.5),
        'b_up': nrm(ks[30], (L, N_EXPERTS, 2 * D_FF), 0.02),
        'w_down': nrm(ks[31], (L, N_EXPERTS, D_FF, D_MODEL), BETA_INIT * D_FF ** -0.5),
        'b_down': nrm(ks[32], (L, N_EXPERTS, D_MODEL), 0.02),
        'ln2_g': 1.0 + nrm(ks[33], (L, D_MODEL), 0.02),
        'ln2_b': nrm(ks[34], (L, D_MODEL), 0.02),
    }

def reference(x_prompt, x_sample, c_prompt, c_sample, cache_ckv, cache_kr, state_C, state_n, state_m,
              state_conv, w_ada, b_ada, w_in, b_if, conv_w, conv_b, q_norm_g, w_uq, kv_norm_g, w_uk, w_uv,
              ml_norm_g, w_o, ln1_g, ln1_b, router_w, router_b, w_up, b_up, w_down, b_down, ln2_g, ln2_b):
    xp, xs = x_prompt, x_sample
    per_layer = []
    for l in range(DEPTH):
        p = {'w_ada': w_ada[l], 'b_ada': b_ada[l], 'w_in': w_in[l], 'b_if': b_if[l], 'conv_w': conv_w[l],
             'conv_b': conv_b[l], 'q_norm_g': q_norm_g[l], 'w_uq': w_uq[l], 'kv_norm_g': kv_norm_g[l],
             'w_uk': w_uk[l], 'w_uv': w_uv[l], 'ml_norm_g': ml_norm_g[l], 'w_o': w_o[l], 'ln1_g': ln1_g[l],
             'ln1_b': ln1_b[l], 'router_w': router_w[l], 'router_b': router_b[l], 'w_up': w_up[l],
             'b_up': b_up[l], 'w_down': w_down[l], 'b_down': b_down[l], 'ln2_g': ln2_g[l], 'ln2_b': ln2_b[l]}
        xp, xs, st = layer(xp, xs, c_prompt, c_sample, cache_ckv[l], cache_kr[l], state_C[l], state_n[l],
                           state_m[l], state_conv[l], p)
        per_layer.append(st)
    (ckv_p, kr_p, C_p, n_p, m_p, conv_p,
     ckv_s, kr_s, C_s, n_s, m_s, conv_s) = [jnp.stack(a) for a in zip(*per_layer)]
    return (xp, xs, ckv_p, kr_p, C_p, n_p, m_p, conv_p, ckv_s, kr_s, C_s, n_s, m_s, conv_s)


_drawn_inputs = setup_inputs


def setup_inputs(seed=0):
    import zlib

    import numpy as np

    out = dict(_drawn_inputs(seed))
    spreads = {}
    factors = {'cache_ckv': 2.864,
     'cache_kr': 8.0,
     'q_norm_g': 8.0,
     'kv_norm_g': 2.91,
     'ml_norm_g': 7.992,
     'router_b': 4.172,
     'b_up': 8.0,
     'b_down': 8.0,
     'ln2_g': 2.848,
     'ln2_b': 2.852}
    for name, (base, spread) in spreads.items():
        noise = np.random.default_rng([zlib.crc32(name.encode()), seed]).standard_normal(out[name].shape)
        drawn = base * np.exp(spread * noise) if base else spread * noise
        out[name] = __import__('jax').numpy.asarray(drawn.astype(out[name].dtype))
    for name, factor in factors.items():
        out[name] = (out[name] * factor).astype(out[name].dtype)
    return out
```

```python
import numpy as np

import concourse.bass as bass
from concourse import mybir

F32 = mybir.dt.float32
I32 = mybir.dt.int32
U32 = mybir.dt.uint32
ALU = mybir.AluOpType
ACT = mybir.ActivationFunctionType
AX = mybir.AxisListType

P = 128
D = 1024
KD = D // P
SEQ = 512
DEC_B, DEC_T = 8, 16
PAST = 1024
NT = (SEQ + DEC_B * DEC_T) // P
NP_T = SEQ // P
TOK = NT * P
H, NOPE, ROPE, VD = 8, 64, 32, 64
QK = NOPE + ROPE
Q_LORA, KV_LORA = 384, 256
MH, MD = 4, 128
MW = MH * MD
IN_COLS = Q_LORA + KV_LORA + ROPE + 4 * MW + 2 * MH
ZC = Q_LORA + KV_LORA + ROPE
NE, TOPK, FF = 32, 4, 1024
ATTN_SCALE = float((NOPE + ROPE) ** -0.5)
ALPHA = float(2.0 ** 0.25)
EPS = 1e-5
LIMIT, SW_ALPHA = 7.0, 1.702
NEG = -1e30
MAX_BLOCKS = NE + TOK * TOPK // P

C_ID, C_TRI, C_ONE, C_NEGP, C_NEGS, C_NEGA = (i * P for i in range(6))
C_BIND = 6 * P
C_IOTA = C_BIND + DEC_B
C_ROPE = C_IOTA + P
C_TOK = C_ROPE + NT * ROPE
NCONST = C_TOK + NT
R_SEL4, R_RESET, R_SELC = 0, MH * P, MH * P + TOK
NROWS = R_SELC + 2 * P


def const_tables():
    c = np.zeros((P, NCONST), np.float32)
    p = np.arange(P)
    c[:, C_ID:C_ID + P] = np.eye(P)
    c[:, C_TRI:C_TRI + P] = p[:, None] < p[None, :]
    c[:, C_ONE:C_ONE + P] = 1.0
    c[:, C_NEGP:C_NEGP + P] = np.where(p[:, None] > p[None, :], NEG, 0)
    same = p[:, None] // DEC_T == p[None, :] // DEC_T
    c[:, C_NEGS:C_NEGS + P] = np.where(same & (p[:, None] <= p[None, :]), 0, NEG)
    c[:, C_NEGA:C_NEGA + P] = np.where((p[:, None] < 64) & (p[None, :] >= 64), NEG, 0)
    c[:, C_BIND:C_BIND + DEC_B] = p[:, None] // DEC_T == np.arange(DEC_B)
    c[:, C_IOTA:C_IOTA + P] = np.arange(P)
    half = ROPE // 2
    inv = np.float32(10000.0) ** (-np.arange(half, dtype=np.float32) / np.float32(half))
    for t in range(NT):
        pos = (t * P + p if t < NP_T else PAST + p % DEC_T).astype(np.float32)
        ang = pos[:, None] * inv
        c[:, C_ROPE + t * ROPE:C_ROPE + t * ROPE + half] = np.cos(ang)
        c[:, C_ROPE + t * ROPE + half:C_ROPE + (t + 1) * ROPE] = np.sin(ang)
        c[:, C_TOK + t] = t * P + p
    r = np.zeros((1 + DEC_B, NROWS), np.float32)
    for h in range(MH):
        r[h, R_SEL4 + h * P:R_SEL4 + (h + 1) * P] = 1.0
    tok = np.arange(TOK)
    r[:, R_RESET:R_RESET + TOK] = np.where(tok < SEQ, tok % P != 0, tok % DEC_T != 0)
    r[0, R_SELC:R_SELC + P] = 1.0
    for b in range(DEC_B):
        r[1 + b, R_SELC + P + b * DEC_T:R_SELC + P + (b + 1) * DEC_T] = 1.0
    return c, r


class Views:
    pass


class Chain:

    def __init__(self, sem):
        self.sem, self.n = sem, 0

    def __call__(self, eng, ins):
        ins.then_inc(self.sem, 1)
        self.n += 1
        eng.wait_ge(self.sem, self.n)


def bcast_rows(ap, n):
    return ap.partition_broadcast(n)


def make_views(nc, ctx):
    v = Views()
    arena = ctx.enter_context(nc.sbuf_tensor("arena", [P, 53100], F32))

    def cut(off, *dims):
        n = int(np.prod(dims))
        assert off + n <= 53100, (off, n)
        ap = arena[:, off:off + n]
        if len(dims) == 1:
            return ap
        names = "abcd"[:len(dims)]
        return ap.rearrange("p (%s) -> p %s" % (" ".join(names), " ".join(names)),
                            **{k: d for k, d in zip(names, dims)})
    v.cut = cut
    v.const = cut(0, NCONST)
    v.rows = cut(NCONST, NROWS)
    assert NCONST + NROWS <= 3000
    v.ident = v.const[:, C_ID:C_ID + P]
    v.ones = v.const[:, C_ONE:C_ONE + P]
    v.e9 = cut(3000, 6 * D)
    v.z = cut(9144, NT, ZC)
    v.so = cut(12504, NT, MW)
    v.qk = cut(15064, 8, TOK)
    v.va = cut(20184, NT, MH, MD + 1)
    v.mix = cut(22764, NT, D)
    v.gates = cut(52900, NT, 2 * MH)
    return v


def stage_project(nc, I, O, v, s, S):
    x = v.cut(22764, NT, D)
    uT = v.cut(27884, KD, TOK)
    RING = 3
    ring = v.cut(33004, RING, KD, 512)
    xpP = v.cut(45292, 8, SEQ + 3)
    xpS = v.cut(45292 + 8 * (SEQ + 3), 8, DEC_B, DEC_T + 3)
    c9 = v.cut(45292, 2, D)
    m0 = 45292 + 8 * 667
    scT = v.cut(m0, KD, 9)
    ssT = v.cut(m0 + 72, 2, KD, 9)
    cw = v.cut(m0 + 216, KD, 29)
    gq = v.cut(m0 + 448, Q_LORA + KV_LORA)
    bif = v.cut(m0 + 1088, 2 * MH)
    ss = v.cut(m0 + 1096, 4, 2 * NT)
    rt = v.cut(m0 + 1136, 4, NT, ROPE // 2)
    tail = v.tail = v.cut(m0 + 1456, KD, 27)
    assert m0 + 1456 + 216 <= 52900
    crow = ring[:, 2, 0:2, :].rearrange("p a b -> p (a b)")

    wada = I["w_ada"][0].rearrange("(k p) n -> p k n", p=P)
    win = I["w_in"][0].rearrange("(k p) n -> p k n", p=P)
    cut_in = [("q", ZC, 512), ("k", ZC + MW, 512), ("za", 0, 512), ("zb", 512, ZC - 512),
              ("g", IN_COLS - 2 * MH, 2 * MH), ("v", ZC + 2 * MW, 512), ("o", ZC + 3 * MW, 512)]
    stream = [(wada[:, :, n * 512:(n + 1) * 512], 512, "ada%d" % n) for n in range(12)]
    stream += [(win[:, :, a:a + n], n, k) for k, a, n in cut_in]
    accs, last_acc = [], {}
    for i, (kind, a, n) in enumerate(cut_in):
        if kind in "qk":
            accs += [(kind, 12 + i, ct, part) for ct in range(4) for part in ((0, 512), (512, TOK))]
        else:
            accs += [(kind, 12 + i, t, (0, n)) for t in range(NT)]
        last_acc[12 + i] = len(accs)
    NB = 4

    def out_count(kind, tile):
        return 1 + max(i for i, a in enumerate(accs) if a[0] == kind and a[2] == tile)

    with nc.Block() as block:
        @block.sync
        def _(sp):
            sp.dma_start(v.const, I["const"]).then_inc(s["const_in"], 16)
            sp.dma_start(v.rows[0:9, :], I["rows"]).then_inc(s["const_in"], 16)
            for i, (src, n, _) in enumerate(stream):
                if i == 2:
                    sp.wait_ge(s["crow_read"], 1)
                if RING <= i < 12 + RING:
                    sp.wait_ge(s["ada_acc"], i - RING + 1)
                if i >= 12 + RING:
                    sp.wait_ge(s["proj_acc"], last_acc[i - RING])
                sp.dma_start(ring[:, i % RING, :, 0:n], src).then_inc(s["ring_in"][i % RING], 16)

        @block.scalar
        def _(act):
            act.dma_start(c9[0:1, 0, :], I["c_prompt"]).then_inc(s["c_in"], 16)
            act.dma_start(c9[1:9, 0, :], I["c_sample"]).then_inc(s["c_in"], 16)
            act.dma_start(v.e9[0:9, :], bcast_rows(I["b_ada"][0], 9)).then_inc(s["bada_in"], 16)
            act.dma_start(crow[0:4, :], I["conv_w"][0]).then_inc(s["crow_in"], 16)
            act.dma_start(crow[4:5, :], I["conv_b"]).then_inc(s["crow_in"], 16)
            act.dma_start(crow[5:29, :], I["state_conv"][0].rearrange("b j n -> (b j) n")).then_inc(s["crow_in"], 16)
            for t in range(NP_T):
                act.dma_start(x[:, t, :], I["x_prompt"][0, t * P:(t + 1) * P, :]).then_inc(s["x_in"], 16)
            act.dma_start(x[:, NP_T, :], I["x_sample"].rearrange("b t d -> (b t) d")).then_inc(s["x_in"], 16)
            act.dma_start(gq[:, 0:Q_LORA], bcast_rows(I["q_norm_g"][0], P)).then_inc(s["gq_in"], 16)
            act.dma_start(gq[:, Q_LORA:], bcast_rows(I["kv_norm_g"][0], P)).then_inc(s["gq_in"], 16)
            act.dma_start(bif, bcast_rows(I["b_if"][0], P)).then_inc(s["gq_in"], 16)
            act.wait_ge(s["c_in"], 32)
            act.activation(c9[0:9, 1, :], c9[0:9, 0, :], ACT.Sigmoid).then_inc(s["c_sig"], 1)

            def evac(i):
                kind, _, t, (a, b) = accs[i]
                act.wait_ge(s["proj_acc"], i + 1)
                ps = S[1 + i % NB]
                if kind in "qk":
                    ct = t + (4 if kind == "k" else 0)
                    if i == 0:
                        act.wait_ge(s["pad_ready"], 2)
                    if a == 0:
                        dst, src = xpP[:, ct, 3:3 + SEQ], ps[:, 0:512]
                    else:
                        dst = xpS[:, ct, :, 3:3 + DEC_T]
                        src = ps[:, 0:P].rearrange("p (b t) -> p b t", b=DEC_B)
                elif kind == "za":
                    dst, src = v.z[:, t, 0:512], ps[:, 0:512]
                elif kind == "zb":
                    dst, src = v.z[:, t, 512:ZC], ps[:, 0:ZC - 512]
                elif kind == "g":
                    dst, src = v.gates[:, t, :], ps[:, 0:2 * MH]
                elif kind == "v":
                    dst = v.va[:, t, :, 0:MD]
                    src = ps[:, 0:MW].rearrange("p (h e) -> p h e", h=MH)
                else:
                    dst, src = v.so[:, t, :], ps[:, 0:MW]
                act.activation(dst, src, ACT.Sigmoid if kind == "o" else ACT.Copy).then_inc(s["proj_out"], 1)

            def sigmoids(cts):
                for ct in cts:
                    act.wait_ge(s["conv_done"], ct + 1)
                    act.activation(xpP[:, ct, 0:SEQ], v.qk[:, ct, 0:SEQ], ACT.Sigmoid).then_inc(s["conv_sig"], 1)
                    act.activation(xpS[:, ct, :, 0:DEC_T],
                                   v.qk[:, ct, SEQ:].rearrange("p (b t) -> p b t", b=DEC_B),
                                   ACT.Sigmoid).then_inc(s["conv_sig"], 1)

            n_g = last_acc[12 + 4]
            for i in range(n_g):
                evac(i)
            sigmoids(range(8))
            for i in range(n_g, len(accs)):
                if i == len(accs) - NT:
                    act.wait_ge(s["ss_ready"], 1)
                    act.activation(ss[:, 2, :], ss[:, 1, :], ACT.Sqrt).then_inc(s["ss_root"], 1)
                evac(i)

        @block.tensor
        def _(pe):
            pe.wait_ge(s["const_in"], 32)
            pe.wait_ge(s["crow_in"], 48)
            for k in range(KD):
                ins = pe.transpose(S[7][:, k * 29:(k + 1) * 29], crow[0:29, k * P:(k + 1) * P],
                                   v.ident[0:29, 0:29])
            ins.then_inc(s["crow_read"], 1)
            pe.wait_ge(s["c_silu"], 1)
            for k in range(KD):
                ins = pe.transpose(S[0][:, k * 9:(k + 1) * 9], c9[0:9, 0, k * P:(k + 1) * P],
                                   v.ident[0:9, 0:9])
            ins.then_inc(s["cT_acc"], 1)
            pe.wait_ge(s["cT_ready"], 1)

            def ada(n):
                pe.wait_ge(s["ring_in"][n % RING], 16 * (n // RING + 1))
                if n >= NB:
                    pe.wait_ge(s["ada_out"], n - NB + 1)
                for k in range(KD):
                    ins = pe.matmul(S[1 + n % NB][0:9, :], scT[:, k, :], ring[:, n % RING, k, :],
                                    start=(k == 0), stop=(k == KD - 1))
                ins.then_inc(s["ada_acc"], 1)

            for n in range(5):
                ada(n)
            pe.wait_ge(s["ada_out"], 4)
            for j in range(16):
                ins = pe.transpose(S[0][:, 128 + j * 9:137 + j * 9], v.e9[0:9, j * P:(j + 1) * P],
                                   v.ident[0:9, 0:9])
            ins.then_inc(s["ssT_acc"], 1)
            pe.wait_ge(s["x_in"], 16 * NT)
            for k in range(KD):
                if k >= 2:
                    pe.wait_ge(s["uT_out"], k - 1)
                for t in range(NP_T):
                    ins = pe.transpose(S[5 + k % 2][:, t * P:(t + 1) * P], x[:, t, k * P:(k + 1) * P], v.ident)
                ins.then_inc(s["xT_acc"], 1)
            for g in range(2):
                pe.wait_ge(s["cw_ready"], 1) if g == 0 else pe.wait_ge(s["uT_out"], KD - 1)
                for k in range(4):
                    ins = pe.transpose(S[7 - 2 * g][:, k * P:(k + 1) * P],
                                       x[:, NP_T, (4 * g + k) * P:(4 * g + k + 1) * P], v.ident)
                ins.then_inc(s["xT_acc"], 1)
            for n in range(5, 12):
                ada(n)
            pe.wait_ge(s["uT_out"], KD + 2)
            pe.wait_ge(s["ada_out"], 12)
            for i, (kind, piece, t, (a, b)) in enumerate(accs):
                slot = piece % RING
                pe.wait_ge(s["ring_in"][slot], 16 * (piece // RING + 1))
                if i >= NB:
                    pe.wait_ge(s["proj_out"], i - NB + 1)
                ps = S[1 + i % NB]
                for k in range(KD):
                    if kind in "qk":
                        ins = pe.matmul(ps[:, 0:b - a], ring[:, slot, k, t * P:(t + 1) * P], uT[:, k, a:b],
                                        start=(k == 0), stop=(k == KD - 1))
                    else:
                        ins = pe.matmul(ps[:, 0:b], uT[:, k, t * P:(t + 1) * P], ring[:, slot, k, 0:b],
                                        start=(k == 0), stop=(k == KD - 1))
                ins.then_inc(s["proj_acc"], 1)

        @block.vector
        def _(dve):
            link = lambda ins: s["dve"](dve, ins)
            dve.memset(v.va[:, :, :, MD:MD + 1], 1.0)
            dve.wait_ge(s["c_sig"], 1)
            dve.tensor_tensor(c9[0:9, 0, :], c9[0:9, 0, :], c9[0:9, 1, :], ALU.mult).then_inc(s["c_silu"], 1)
            dve.wait_ge(s["crow_read"], 1)
            dve.tensor_copy(cw, S[7][:, 0:KD * 29].rearrange("p (k n) -> p k n", k=KD)).then_inc(s["cw_ready"], 1)
            dve.wait_ge(s["cT_acc"], 1)
            dve.tensor_copy(scT, S[0][:, 0:KD * 9].rearrange("p (k n) -> p k n", k=KD)).then_inc(s["cT_ready"], 1)
            dve.memset(xpP[:, :, 0:3], 0.0).then_inc(s["pad_ready"], 1)
            dve.wait_ge(s["cw_ready"], 1)
            dve.tensor_copy(xpS[:, :, :, 0:3], cw[:, :, 5:29].rearrange("p k (b j) -> p k b j", j=3)
                            ).then_inc(s["pad_ready"], 1)
            dve.wait_ge(s["bada_in"], 16)

            def ada_out(n):
                dve.wait_ge(s["ada_acc"], n + 1)
                e = v.e9[0:9, n * 512:(n + 1) * 512]
                dve.tensor_tensor(e, S[1 + n % NB][0:9, :], e, ALU.add).then_inc(s["ada_out"], 1)

            for n in range(4):
                ada_out(n)
            dve.wait_ge(s["ssT_acc"], 1)
            link(dve.tensor_copy(ssT[:, 0], S[0][:, 128:200].rearrange("p (k n) -> p k n", k=KD)))
            link(dve.tensor_scalar(ssT[:, 1], S[0][:, 200:272].rearrange("p (k n) -> p k n", k=KD),
                                   1.0, None, ALU.add))
            ada_out(4)
            for k in range(KD):
                dve.wait_ge(s["xT_acc"], k + 1)
                dve.tensor_scalar(uT[:, k, 0:SEQ], S[5 + k % 2][:, :], ssT[:, 1, k, 0:1], ssT[:, 0, k, 0:1],
                                  ALU.mult, ALU.add).then_inc(s["uT_out"], 1)
            for g in range(2):
                dve.wait_ge(s["xT_acc"], KD + 1 + g)
                dst = uT[:, 4 * g:4 * g + 4, SEQ:].rearrange("p k (b t) -> p k b t", b=DEC_B)

                def per_batch(j):
                    return ssT[:, j, 4 * g:4 * g + 4, 1:9].unsqueeze(3).to_broadcast([P, 4, DEC_B, DEC_T])

                link(dve.tensor_tensor(dst, S[7 - 2 * g][:, :].rearrange("p (k b t) -> p k b t", k=4, b=DEC_B),
                                       per_batch(1), ALU.mult))
                dve.tensor_tensor(dst, dst, per_batch(0), ALU.add).then_inc(s["uT_out"], 1)
            for n in range(5, 12):
                ada_out(n)

            for ct in range(8):
                kind = "q" if ct < 4 else "k"
                dve.wait_ge(s["proj_out"], out_count(kind, ct % 4))
                accP, accS = v.qk[:, ct, 0:SEQ], v.qk[:, ct, SEQ:].rearrange("p (b t) -> p b t", b=DEC_B)
                dve.tensor_scalar(accP, xpP[:, ct, 0:SEQ], cw[:, ct, 0:1], cw[:, ct, 4:5], ALU.mult, ALU.add)
                link(dve.tensor_scalar(accS, xpS[:, ct, :, 0:DEC_T], cw[:, ct, 0:1], cw[:, ct, 4:5],
                                       ALU.mult, ALU.add))
                for j in range(1, 4):
                    dve.scalar_tensor_tensor(accP, xpP[:, ct, j:j + SEQ], cw[:, ct, j:j + 1], accP,
                                             ALU.mult, ALU.add)
                    ins = dve.scalar_tensor_tensor(accS, xpS[:, ct, :, j:j + DEC_T], cw[:, ct, j:j + 1], accS,
                                                   ALU.mult, ALU.add)
                    if j < 3:
                        link(ins)
                    else:
                        link(ins)
                dve.tensor_copy(tail[:, ct, 0:3], xpP[:, ct, SEQ:SEQ + 3])
                dve.tensor_copy(tail[:, ct, 3:27].rearrange("p (b j) -> p b j", j=3),
                                xpS[:, ct, :, DEC_T:DEC_T + 3]).then_inc(s["conv_done"], 1)
            sq = xrow = x[:, 0, 0:Q_LORA]
            for t in range(NT):
                dve.wait_ge(s["proj_out"], out_count("zb", t))
                link(dve.tensor_tensor_reduce(sq, v.z[:, t, 0:Q_LORA], v.z[:, t, 0:Q_LORA], 1.0, 0.0,
                                              ALU.mult, ALU.add, ss[:, 0, t:t + 1]))
                link(dve.tensor_tensor_reduce(sq[:, 0:KV_LORA], v.z[:, t, Q_LORA:Q_LORA + KV_LORA],
                                              v.z[:, t, Q_LORA:Q_LORA + KV_LORA], 1.0, 0.0,
                                              ALU.mult, ALU.add, ss[:, 0, NT + t:NT + t + 1]))
            link(dve.tensor_scalar(ss[:, 1, 0:NT], ss[:, 0, 0:NT], 1.0 / Q_LORA, EPS, ALU.mult, ALU.add))
            dve.tensor_scalar(ss[:, 1, NT:], ss[:, 0, NT:], 1.0 / KV_LORA, EPS, ALU.mult, ALU.add
                              ).then_inc(s["ss_ready"], 1)
            tab = v.const[:, C_ROPE:C_ROPE + NT * ROPE].rearrange("p (t n) -> p t n", t=NT)
            cos, sin = tab[:, :, 0:16], tab[:, :, 16:32]
            x1, x2 = v.z[:, :, ZC - 32:ZC - 16], v.z[:, :, ZC - 16:ZC]
            dve.tensor_tensor(rt[:, 0], x1, cos, ALU.mult)
            dve.tensor_tensor(rt[:, 1], x2, sin, ALU.mult)
            dve.tensor_tensor(rt[:, 2], x1, sin, ALU.mult)
            link(dve.tensor_tensor(rt[:, 3], x2, cos, ALU.mult))
            dve.tensor_tensor(x1, rt[:, 0], rt[:, 1], ALU.subtract)
            dve.tensor_tensor(x2, rt[:, 2], rt[:, 3], ALU.add)
            for ct in range(8):
                dve.wait_ge(s["conv_sig"], 2 * ct + 2)
                sc = 1.0 if ct < 4 else float(MD ** -0.5)
                dve.scalar_tensor_tensor(v.qk[:, ct, 0:SEQ], v.qk[:, ct, 0:SEQ], sc, xpP[:, ct, 0:SEQ],
                                         ALU.mult, ALU.mult)
                accS = v.qk[:, ct, SEQ:].rearrange("p (b t) -> p b t", b=DEC_B)
                link(dve.scalar_tensor_tensor(accS, accS, sc, xpS[:, ct, :, 0:DEC_T], ALU.mult, ALU.mult))
            dve.wait_ge(s["gq_in"], 48)
            dve.wait_ge(s["proj_out"], out_count("g", NT - 1))
            link(dve.tensor_tensor(v.gates, v.gates, bif.unsqueeze(1).to_broadcast([P, NT, 2 * MH]), ALU.add))
            dve.wait_ge(s["ss_root"], 1)
            link(dve.reciprocal(ss[:, 3, :], ss[:, 2, :]))
            for t in range(NT):
                zq, zk = v.z[:, t, 0:Q_LORA], v.z[:, t, Q_LORA:Q_LORA + KV_LORA]
                dve.scalar_tensor_tensor(zq, zq, ss[:, 3, t:t + 1], gq[:, 0:Q_LORA], ALU.mult, ALU.mult)
                dve.scalar_tensor_tensor(zk, zk, ss[:, 3, NT + t:NT + t + 1], gq[:, Q_LORA:], ALU.mult,
                                         ALU.mult)


def stage_mlstm(nc, I, O, v, s, S):
    W0 = 27884
    C = v.cut(W0, 36, MD + 1)
    o = W0 + 36 * (MD + 1)
    row = v.cut(o, 12, TOK)
    o += 12 * TOK
    seg = v.cut(o, 4, 4 + DEC_B)
    o += 48
    colv = v.cut(o, NT, 4, MH)
    o += NT * 16
    dec = v.cut(o, MH, 4 + DEC_B)
    o += 48
    Dx = v.cut(o, 2, P)
    Wt = v.cut(o + 256, 2, P)
    kw = v.cut(o + 512, 2, P)
    nd = v.cut(o + 768, 2, MD + 1)
    tmp = v.cut(o + 1026, 2, MD + 1)
    o += 1284
    qm = v.cut(o, DEC_B, P)
    vm = v.cut(o + 1024, DEC_B, MD + 1)
    o += 2056
    h = v.cut(o, NT * MH, MD)
    o += NT * MH * MD
    st = v.cut(o, NT * MH, 6)
    mv = v.cut(o + 120, NT * MH, 2)
    rs = v.cut(o + 160, 2, NT * MH)
    dn = v.cut(o + 200, NT * MH, 2)
    o += 240
    gml = v.cut(o, MW)
    o += MW
    nrow = v.cut(o, 2, MD)
    crow = v.cut(o + 256, D)
    o += 256 + D
    assert o <= 50628 + 1400
    Pm, Sm = slice(0, SEQ), slice(SEQ, TOK)
    IG, LF, T1, T2, FC, M, A, B, Q2, Q3, NM, IG2 = range(12)

    def r(i, sl=slice(0, TOK)):
        return row[0:4, i, sl]

    def seg12(i, sl=slice(0, 4 + DEC_B)):
        return seg[0:4, i, sl]

    def bat(ap):
        return ap.rearrange("p (b t) -> p b t", b=DEC_B)

    def til(ap):
        return ap.rearrange("p (b t) -> p b t", b=NP_T)

    units = [(t, hh) for t in range(NP_T) for hh in range(MH)] + [(NP_T, hh) for hh in range(MH)]
    NU = len(units)

    with nc.Block() as block:
        @block.sync
        def _(sp):
            for b in range(DEC_B):
                sp.dma_start(C[:, 4 + 4 * b:8 + 4 * b, 0:MD], I["state_C"][0, b].rearrange("h d e -> d h e")
                             ).then_inc(s["C_in"], 16)
            sp.dma_start(O["new_ckv_p"][0, 0].rearrange("(t p) n -> p t n", p=P),
                         v.z[:, 0:NP_T, Q_LORA:Q_LORA + KV_LORA]).then_inc(s["out1"], 16)
            sp.dma_start(O["new_ckv_s"][0].rearrange("b t n -> (b t) n"),
                         v.z[:, NP_T, Q_LORA:Q_LORA + KV_LORA]).then_inc(s["out1"], 16)
            sp.dma_start(O["new_kr_p"][0, 0].rearrange("(t p) n -> p t n", p=P),
                         v.z[:, 0:NP_T, ZC - ROPE:ZC]).then_inc(s["out1"], 16)
            sp.dma_start(O["new_kr_s"][0].rearrange("b t n -> (b t) n"), v.z[:, NP_T, ZC - ROPE:ZC]
                         ).then_inc(s["out1"], 16)
            sp.wait_ge(s["tail_ready"], 2)
            sp.dma_start(O["new_conv_p"][0, 0], crow[0:3, :]).then_inc(s["out1"], 16)
            sp.dma_start(O["new_conv_s"][0].rearrange("b j n -> (b j) n"), crow[3:27, :]).then_inc(s["out1"], 16)
            sp.wait_ge(s["m_ready"], 1)
            sp.dma_start(O["new_m_p"][0, 0:1].rearrange("b h -> h b"), row[0:4, M, SEQ - 1:SEQ]).then_inc(s["out1"], 16)
            sp.dma_start(O["new_m_s"][0].rearrange("b h -> h b"), seg[0:4, 3, 4:12],
                         allow_slow_non_contiguous=True).then_inc(s["out1"], 16)
            sp.wait_ge(s["C_new"], MH * NP_T)
            sp.dma_start(O["new_C_p"][0, 0].rearrange("h d e -> d h e"), C[:, 0:4, 0:MD]).then_inc(s["out1"], 16)
            sp.wait_ge(s["C_new"], MH * NP_T + MH)
            for b in range(DEC_B):
                sp.dma_start(O["new_C_s"][0, b].rearrange("h d e -> d h e"), C[:, 4 + 4 * b:8 + 4 * b, 0:MD]
                             ).then_inc(s["out1"], 16)
            sp.wait_ge(s["nT_ready"], 1)
            sp.dma_start(O["new_n_p"][0, 0], nrow[0:4, 1, :]).then_inc(s["out1"], 16)
            sp.dma_start(O["new_n_s"][0].rearrange("b h d -> (b h) d"), nrow[4:36, 1, :]).then_inc(s["out1"], 16)
            sp.wait_ge(s["out1"], 16 * (4 + 2 + 2 + 1 + DEC_B + 2))

        @block.scalar
        def _(act):
            act.dma_start(nrow[0:32, 0, :], I["state_n"][0].rearrange("b h d -> (b h) d")).then_inc(s["n_in"], 16)
            act.dma_start(seg[0:4, 0, 4:12], I["state_m"][0].rearrange("b h -> h b"),
                          allow_slow_non_contiguous=True).then_inc(s["m0_in"], 16)
            act.dma_start(gml, bcast_rows(I["ml_norm_g"][0], P)).then_inc(s["n_in"], 16)
            act.wait_ge(s["row_a"], 1)
            act.activation(r(T1), r(T2), ACT.Exp, scale=-1.0).then_inc(s["act_row"], 1)
            act.wait_ge(s["act_row"], 1)
            act.activation(r(T1), r(T1), ACT.Ln, bias=v.ones[0:4, 0:1]).then_inc(s["act_row"], 1)
            act.wait_ge(s["cols_acc"], 1)
            act.activation(dec, S[3][:, 0:48].rearrange("p (h n) -> p h n", h=MH), ACT.Exp).then_inc(s["cols_exp"], 1)
            act.activation(colv[:, :, 0, :], S[2][:, 0:80].rearrange("p (t q h) -> p t q h", q=4, h=MH)[:, :, 0],
                           ACT.Copy).then_inc(s["cols_exp"], 1)
            act.activation(colv[:, :, 1:4, :], S[2][:, 0:80].rearrange("p (t q h) -> p t q h", q=4, h=MH)[:, :, 1:4],
                           ACT.Exp).then_inc(s["cols_exp"], 1)
            act.wait_ge(s["cols_exp"], 3)
            for u, (t, hh) in enumerate(units):
                act.wait_ge(s["pre_acc"], u + 1)
                if u >= 2:
                    act.wait_ge(s["W_ready"], u - 1)
                act.activation(Dx[:, u % 2, :], S[u % 2][:, P:2 * P], ACT.Exp,
                               bias=colv[:, t, 0, hh:hh + 1]).then_inc(s["D_ready"], 1)
                act.wait_ge(s["num_acc"], u + 1)
                if u >= 2:
                    act.wait_ge(s["nd_ready"], u - 1)
                act.activation(tmp[:, u % 2, :], S[2 + u % 2][:, 129:258], ACT.Copy,
                               scale=colv[:, t, 1, hh:hh + 1]).then_inc(s["tmp_ready"], 1)
            act.wait_ge(s["var_ready"], 1)
            act.activation(rs[:, 1, :], rs[:, 0, :], ACT.Sqrt).then_inc(s["rs_root"], 1)

        @block.tensor
        def _(pe):
            for k in range(KD):
                ins = pe.transpose(S[4 + k // 4][0:27, (k % 4) * P:(k % 4 + 1) * P], v.tail[:, k, :], v.ident)
            ins.then_inc(s["tail_acc"], 1)
            for j in range(2):
                for t in range(NT):
                    bank, a = (2 * j, t * P) if t < NP_T else (2 * j + 1, 0)
                    ins = pe.transpose(S[bank][0:4, a:a + P], v.gates[:, t, 4 * j:4 * j + 4], v.ident)
                ins.then_inc(s["gate_acc"], 1)
            pe.wait_ge(s["n_in"], 32)
            pe.transpose(S[6][:, 0:32], nrow[0:32, 0, :], v.ident[0:32, 0:32]).then_inc(s["n_acc"], 1)
            pe.wait_ge(s["rows_done"], 1)
            for hh in range(MH):
                ins = pe.matmul(S[3][:, hh * 12:hh * 12 + 12], v.rows[0:4, R_SEL4 + hh * P:R_SEL4 + (hh + 1) * P],
                                seg12(2), start=True, stop=True)
            for t in range(NT):
                for q, src in enumerate((B, Q2, Q3, NM)):
                    c = (t * 4 + q) * 4
                    ins = pe.transpose(S[2][:, c:c + 4], row[0:4, src, t * P:(t + 1) * P], v.ident[0:4, 0:4])
            ins.then_inc(s["cols_acc"], 1)

            def pre(u):
                t, hh = units[u]
                if u >= 2:
                    pe.wait_ge(s["kw_ready"], u - 1)
                b = S[u % 2]
                pe.matmul(b[:, 0:P], v.qk[:, 4 + hh, t * P:(t + 1) * P], v.qk[:, hh, t * P:(t + 1) * P],
                          start=True, stop=True)
                pe.matmul(b[:, P:2 * P], v.rows[0:4, R_SEL4 + hh * P:R_SEL4 + (hh + 1) * P],
                          r(A, slice(t * P, (t + 1) * P)), start=True, stop=False)
                neg = C_NEGP if t < NP_T else C_NEGS
                pe.matmul(b[:, P:2 * P], v.ident, v.const[:, neg:neg + P], start=False, stop=True)
                pe.transpose(b[:, 2 * P:3 * P], v.qk[:, 4 + hh, t * P:(t + 1) * P], v.ident
                             ).then_inc(s["pre_acc"], 1)

            def products(u):
                t, hh = units[u]
                pe.wait_ge(s["kw_ready"], u + 1)
                if u == 0:
                    pe.wait_ge(s["cols_exp"], 3)
                if u >= 2:
                    pe.wait_ge(s["nd_ready"], u - 1)
                    pe.wait_ge(s["C_new"], u - 1)
                b = S[2 + u % 2]
                pe.matmul(b[:, 0:129], Wt[:, u % 2, :], v.va[:, t, hh, :], start=True, stop=True)
                if t < NP_T:
                    pe.wait_ge(s["C_new"], max(1, u - MH + 1)) if t else pe.wait_ge(s["C_zero"], 1)
                    pe.matmul(b[:, 129:258], v.qk[:, hh, t * P:(t + 1) * P], C[:, hh, :], start=True, stop=True)
                    pe.matmul(b[:, 258:387], kw[:, u % 2, :], v.va[:, t, hh, :], start=True, stop=True
                              ).then_inc(s["num_acc"], 1)
                else:
                    if hh == 0:
                        pe.wait_ge(s["C_in"], 16 * DEC_B)
                    if hh >= 1:
                        pe.wait_ge(s["C_new"], u)
                    for bb in range(DEC_B):
                        pe.matmul(b[:, 129:258], qm[:, bb, :], C[:, 4 + 4 * bb + hh, :],
                                  start=(bb == 0), stop=(bb == DEC_B - 1))
                    for j, (b0, b1) in enumerate(((0, 3), (3, 6), (6, 8))):
                        ins = pe.matmul(S[4 + j][:, 0:(b1 - b0) * 129], kw[:, u % 2, :], vm[:, b0:b1, :],
                                        start=True, stop=True)
                    ins.then_inc(s["num_acc"], 1)

            pre(0)
            for u in range(NU):
                if u + 1 < NU:
                    pre(u + 1)
                products(u)
            pe.wait_ge(s["n_cols"], 1)
            pe.transpose(S[7][0:36, 0:P], Dx[:, 0, 0:36], v.ident).then_inc(s["nT_acc"], 1)

        @block.vector
        def _(dve):
            link = lambda ins: s["dve"](dve, ins)
            dve.wait_ge(s["tail_acc"], 1)
            dve.tensor_copy(crow[0:27, 0:512], S[4][0:27, :]).then_inc(s["tail_ready"], 1)
            dve.tensor_copy(crow[0:27, 512:], S[5][0:27, :]).then_inc(s["tail_ready"], 1)
            dve.memset(C[:, 0:4, :], 0.0).then_inc(s["C_zero"], 1)
            dve.memset(qm, 0.0)
            dve.memset(seg12(0, slice(0, 1)), 0.0)
            dve.wait_ge(s["gate_acc"], 2)
            for j, dst in ((0, IG), (1, LF)):
                dve.tensor_copy(r(dst, Pm), S[2 * j][0:4, :])
                link(dve.tensor_copy(r(dst, Sm), S[2 * j + 1][0:4, 0:P]))
            dve.scalar_tensor_tensor(r(T2), r(LF), -1.0, r(LF), ALU.mult, ALU.max).then_inc(s["row_a"], 1)
            dve.wait_ge(s["act_row"], 2)
            link(dve.scalar_tensor_tensor(r(LF), r(LF), 0.0, r(T1), ALU.min, ALU.subtract))
            link(dve.tensor_tensor_scan(r(FC), v.rows[0:4, R_RESET:R_RESET + TOK], r(LF), 0.0, ALU.mult, ALU.add))
            link(dve.tensor_tensor_scan(r(M, Pm), r(LF, Pm), r(IG, Pm), 0.0, ALU.add, ALU.max))
            dve.tensor_copy(r(IG2, Sm), r(IG, Sm))
            link(dve.tensor_copy(r(T1, Sm), r(LF, Sm)))
            first, firstI = bat(r(T1, Sm))[:, :, 0:1], bat(r(IG2, Sm))[:, :, 0:1]
            dve.wait_ge(s["m0_in"], 16)
            m0c = seg12(0, slice(4, 12)).unsqueeze(2)
            link(dve.tensor_tensor(first, first, m0c, ALU.add))
            link(dve.tensor_tensor(firstI, firstI, first, ALU.max))
            link(dve.memset(first, NEG))
            link(dve.tensor_tensor_scan(r(M, Sm), r(T1, Sm), r(IG2, Sm), 0.0, ALU.add, ALU.max))
            dve.tensor_tensor(r(A), r(FC), r(M), ALU.subtract)
            dve.tensor_tensor(r(B), r(IG), r(FC), ALU.subtract)
            dve.tensor_scalar(r(NM), r(M), -1.0, None, ALU.mult)
            dve.tensor_copy(seg12(0, slice(1, 4)).unsqueeze(2), til(r(M, Pm))[:, 0:3, P - 1:P])
            link(dve.tensor_copy(seg12(3, slice(4, 12)).unsqueeze(2), bat(r(M, Sm))[:, :, DEC_T - 1:DEC_T]))
            dve.tensor_copy(seg12(1, slice(0, 4)).unsqueeze(2), til(r(A, Pm))[:, :, P - 1:P])
            link(dve.tensor_copy(seg12(1, slice(4, 12)).unsqueeze(2), bat(r(A, Sm))[:, :, DEC_T - 1:DEC_T]))
            dve.tensor_tensor(seg12(2), seg12(0), seg12(1), ALU.add).then_inc(s["m_ready"], 1)
            for i, src, dst in ((0, A, Q2), (1, B, Q3)):
                dve.tensor_tensor(til(r(dst, Pm)), til(r(src, Pm)),
                                  seg12(i, slice(0, 4)).unsqueeze(2).to_broadcast([4, NP_T, P]), ALU.add)
                ins = dve.tensor_tensor(bat(r(dst, Sm)), bat(r(src, Sm)),
                                        seg12(i, slice(4, 12)).unsqueeze(2).to_broadcast([4, DEC_B, DEC_T]), ALU.add)
            ins.then_inc(s["rows_done"], 1)
            dve.wait_ge(s["n_acc"], 1)
            link(dve.tensor_copy(C[:, 4:36, MD:MD + 1], S[6][:, 0:32].unsqueeze(2)))
            dve.wait_ge(s["cols_exp"], 3)
            dve.wait_ge(s["C_in"], 16 * DEC_B)

            def weights(u):
                t, hh = units[u]
                dve.wait_ge(s["pre_acc"], u + 1)
                if u >= 2:
                    dve.wait_ge(s["num_acc"], u - 1)
                dve.wait_ge(s["D_ready"], u + 1)
                dve.tensor_tensor(Wt[:, u % 2, :], S[u % 2][:, 0:P], Dx[:, u % 2, :], ALU.mult
                                  ).then_inc(s["W_ready"], 1)
                if t == NP_T:
                    if hh >= 1:
                        dve.wait_ge(s["num_acc"], u)
                    qd = qm.rearrange("p b n -> p (b n)")
                    for bb in range(DEC_B):
                        dve.tensor_copy(qd[:, bb * (P + DEC_T):bb * (P + DEC_T) + DEC_T],
                                        v.qk[:, hh, SEQ + bb * DEC_T:SEQ + (bb + 1) * DEC_T])
                    dve.tensor_tensor(vm, v.va[:, t, hh, :].unsqueeze(1).to_broadcast([P, DEC_B, MD + 1]),
                                      v.const[:, C_BIND:C_BIND + DEC_B].unsqueeze(2).to_broadcast(
                                          [P, DEC_B, MD + 1]), ALU.mult)
                dve.tensor_scalar(kw[:, u % 2, :], S[u % 2][:, 2 * P:3 * P], colv[:, t, 2, hh:hh + 1], None,
                                  ALU.mult).then_inc(s["kw_ready"], 1)

            def close(u):
                t, hh = units[u]
                dve.wait_ge(s["num_acc"], u + 1)
                dve.wait_ge(s["tmp_ready"], u + 1)
                b = S[2 + u % 2]
                link(dve.tensor_tensor(nd[:, u % 2, :], b[:, 0:129], tmp[:, u % 2, :], ALU.add))
                if t < NP_T:
                    dve.scalar_tensor_tensor(C[:, hh, :], C[:, hh, :], dec[:, hh, t:t + 1], b[:, 258:387],
                                             ALU.mult, ALU.add).then_inc(s["C_new"], 1)
                else:
                    for bb in range(DEC_B):
                        c = C[:, 4 + 4 * bb + hh, :]
                        ins = dve.scalar_tensor_tensor(c, c, dec[:, hh, 4 + bb:5 + bb],
                                                       S[4 + bb // 3][:, (bb % 3) * 129:(bb % 3 + 1) * 129],
                                                       ALU.mult, ALU.add)
                    ins.then_inc(s["C_new"], 1)
                den = nd[:, u % 2, MD:MD + 1]
                d2 = dn[:, 4 * t + hh, :]
                link(dve.scalar_tensor_tensor(d2[:, 0:1], den, -1.0, den, ALU.mult, ALU.max))
                link(dve.tensor_tensor(d2[:, 1:2], d2[:, 0:1], colv[:, t, 3, hh:hh + 1], ALU.max))
                link(dve.reciprocal(d2[:, 0:1], d2[:, 1:2]))
                dve.tensor_scalar(h[:, 4 * t + hh, :], nd[:, u % 2, 0:MD], d2[:, 0:1], None, ALU.mult
                                  ).then_inc(s["nd_ready"], 1)
                dve.wait_ge(s["nd_ready"], u + 1)
                dve.bn_stats(st[:, 4 * t + hh, :], h[:, 4 * t + hh, :])

            weights(0)
            for u in range(NU):
                if u + 1 < NU and units[u + 1][0] < NP_T:
                    weights(u + 1)
                close(u)
                if u + 1 < NU and units[u + 1][0] == NP_T:
                    weights(u + 1)
            link(dve.memset(rs, 0.0))
            dve.wait_ge(s["D_ready"], NU)
            dve.wait_ge(s["W_ready"], NU)
            dve.wait_ge(s["C_new"], NU)
            dve.tensor_copy(Dx[:, 0, 0:36].unsqueeze(2), C[:, :, MD:MD + 1]).then_inc(s["n_cols"], 1)
            for i in range(NT * MH):
                ins = dve.bn_aggr(mv[:, i, :], st[:, i, :])
            link(ins)
            dve.tensor_scalar(rs[:, 0, :], mv[:, :, 1], EPS, None, ALU.add).then_inc(s["var_ready"], 1)
            dve.wait_ge(s["rs_root"], 1)
            link(dve.reciprocal(rs[:, 0, :], rs[:, 1, :]))
            for t in range(NT):
                for hh in range(MH):
                    i = 4 * t + hh
                    dve.tensor_scalar(h[:, i, :], h[:, i, :], mv[:, i, 0:1], rs[:, 0, i:i + 1],
                                      ALU.subtract, ALU.mult)
                link(dve.tensor_tensor(v.so[:, t, :], v.so[:, t, :], gml, ALU.mult))
                dve.tensor_tensor(v.mix[:, t, MW:], h[:, 4 * t:4 * t + 4, :].rearrange("p h e -> p (h e)"),
                                  v.so[:, t, :], ALU.mult)
            dve.wait_ge(s["nT_acc"], 1)
            dve.tensor_copy(nrow[0:36, 1, :], S[7][0:36, 0:P]).then_inc(s["nT_ready"], 1)


def stage_prompt_attention(nc, I, O, v, s, S):
    v.qT = qT = v.cut(15064, H, TOK)
    v.wuv = wuv = v.cut(20184, 2, H * VD)
    kT = v.cut(27884, H, SEQ)
    vP = v.cut(31980, NP_T, H * VD)
    cqT = v.cut(34028, 3, TOK)
    v.ckT = ckT = v.cut(35948, 2, TOK)
    v.ukT = ukT = v.cut(37228, H, KV_LORA)
    qt = v.cut(39276, 2, H, QK)
    Pr = v.cut(40812, 2, SEQ)
    PT = v.cut(41836, 2, NP_T, P)
    v.cache = v.cut(42860, 2, KD, KV_LORA)
    v.krc = [v.cut(46956, KD, QK), v.cut(21208, KD, QK)]
    wuq = v.cut(48492, 3, H * QK)
    wuk = v.cut(50796, 2, H * NOPE)
    rot = v.cut(21976, 4, H, ROPE // 2)
    mx = v.cut(22488, 4, 2)
    v.newk = v.cut(48492, DEC_B, KV_LORA)
    yz = v.cut(13600, D)
    v.krnew = v.cut(22500, 1, P)
    nb = v.cut(22628, 2)
    units = [(t, h) for t in range(NP_T) for h in range(H)]
    NU = len(units)
    tab = v.const[:, C_ROPE:C_ROPE + NT * ROPE].rearrange("p (t n) -> p t n", t=NT)
    prep = [("cq", t) for t in range(NT)] + [("ck", t) for t in range(NT)] + [("uk", j) for j in range(4)]
    fill = [("k", h) for h in range(H)] + [("v", t) for t in range(NP_T)]
    for t in range(NT):
        prep += [("q", t, 0), ("q", t, 1)] + fill[3 * t:3 * t + 3] + [("qT", t, 0), ("qT", t, 1)]
    where = {k: i for i, k in enumerate(prep)}

    with nc.Block() as block:
        @block.sync
        def _(sp):
            sp.dma_start(wuq, I["w_uq"][0].rearrange("(k p) n -> p k n", p=P)).then_inc(s["wu_in"], 16)
            sp.dma_start(wuk, I["w_uk"][0].rearrange("(k p) h n -> p k (h n)", p=P)).then_inc(s["wu_in"], 16)
            sp.dma_start(wuv, I["w_uv"][0].rearrange("(k p) h n -> p k (h n)", p=P)).then_inc(s["wu_in"], 16)
            sp.wait_ge(s["yz_ready"], 1)
            sp.dma_start(v.d_y[NE * P:, :].rearrange("(b p) d -> p b d", p=P),
                         yz.unsqueeze(1).to_broadcast([P, MAX_BLOCKS - NE, D])).then_inc(s["yz_out"], 16)
            sp.wait_ge(s["krc_zero"], 1)
            for b in range(2):
                sp.dma_start(v.cache[:, b], I["cache_ckv"][0, b].rearrange("(k p) n -> p k n", p=P)
                             ).then_inc(s["cache_in"][b], 16)
                sp.dma_start(v.krc[b][:, :, NOPE:], I["cache_kr"][0, b].rearrange("(k p) n -> p k n", p=P)
                             ).then_inc(s["cache_in"][b], 16)

        @block.gpsimd
        def _(pool):
            pool.memset(yz, 0.0).then_inc(s["yz_ready"], 1)
            pool.memset(v.krc[0][:, :, 0:NOPE], 0.0)
            pool.memset(v.krc[1][:, :, 0:NOPE], 0.0).then_inc(s["krc_zero"], 1)
            for t in range(NT):
                pool.wait_ge(s["prep_out"], where[("q", t, 1)] + 1)
                x1, x2 = qt[:, t % 2, :, NOPE:NOPE + 16], qt[:, t % 2, :, NOPE + 16:]
                cos = tab[:, t, 0:16].unsqueeze(1).to_broadcast([P, H, 16])
                sin = tab[:, t, 16:32].unsqueeze(1).to_broadcast([P, H, 16])
                pool.tensor_tensor(rot[:, 0], x1, cos, ALU.mult)
                pool.tensor_tensor(rot[:, 1], x2, sin, ALU.mult)
                pool.tensor_tensor(rot[:, 2], x1, sin, ALU.mult)
                s["pool"](pool, pool.tensor_tensor(rot[:, 3], x2, cos, ALU.mult))
                pool.tensor_tensor(x1, rot[:, 0], rot[:, 1], ALU.subtract)
                pool.tensor_tensor(x2, rot[:, 2], rot[:, 3], ALU.add).then_inc(s["q_rot"], 1)
                pool.wait_ge(s["q_rot"], t + 1)

        @block.tensor
        def _(pe):
            pe.wait_ge(s["wu_in"], 48)
            for i, it in enumerate(prep):
                if i >= 8:
                    pe.wait_ge(s["prep_out"], i - 7)
                ps = S[i % 8]
                if it[0] == "cq":
                    for k in range(3):
                        ins = pe.transpose(ps[:, k * P:(k + 1) * P], v.z[:, it[1], k * P:(k + 1) * P], v.ident)
                elif it[0] == "ck":
                    for k in range(2):
                        pe.transpose(ps[:, k * P:(k + 1) * P],
                                     v.z[:, it[1], Q_LORA + k * P:Q_LORA + (k + 1) * P], v.ident)
                    ins = pe.transpose(ps[0:QK, 2 * P:3 * P], v.z[:, it[1], ZC - QK:ZC], v.ident)
                elif it[0] == "uk":
                    for h in (2 * it[1], 2 * it[1] + 1):
                        for k in range(2):
                            c = (h % 2) * KV_LORA + k * P
                            ins = pe.transpose(ps[0:NOPE, c:c + P], wuk[:, k, h * NOPE:(h + 1) * NOPE], v.ident)
                elif it[0] == "q":
                    _, t, half = it
                    pe.wait_ge(s["prep_out"], where[("cq", t)] + 1)
                    for k in range(3):
                        ins = pe.matmul(ps[:, 0:384], cqT[:, k, t * P:(t + 1) * P],
                                        wuq[:, k, half * 384:(half + 1) * 384], start=(k == 0), stop=(k == 2))
                elif it[0] == "k":
                    pe.wait_ge(s["prep_out"], where[("ck", NT - 1)] + 1)
                    for k in range(2):
                        ins = pe.matmul(ps[0:NOPE, :], wuk[:, k, it[1] * NOPE:(it[1] + 1) * NOPE],
                                        ckT[:, k, 0:SEQ], start=(k == 0), stop=(k == 1))
                elif it[0] == "v":
                    for k in range(2):
                        ins = pe.matmul(ps[:, :], ckT[:, k, it[1] * P:(it[1] + 1) * P], wuv[:, k, :],
                                        start=(k == 0), stop=(k == 1))
                else:
                    _, t, half = it
                    pe.wait_ge(s["q_rot"], t + 1)
                    for h in range(4):
                        ins = pe.transpose(ps[0:QK, h * P:(h + 1) * P], qt[:, t % 2, 4 * half + h, :], v.ident)
                ins.then_inc(s["prep_acc"], 1)
            pe.wait_ge(s["prep_out"], len(prep))

            def scores(u):
                t, h = units[u]
                n = (t + 1) * P
                if u >= 2:
                    pe.wait_ge(s["at_exp"], u - 1)
                pe.matmul(S[u % 2][:, 0:n], qT[0:QK, h, t * P:n], kT[0:QK, h, 0:n], start=True, stop=False,
                          skip_group_check=True)
                pe.matmul(S[u % 2][:, t * P:n], v.ident, v.const[:, C_NEGA:C_NEGA + P], start=False, stop=True,
                          skip_group_check=True).then_inc(s["at_S"], 1)

            def turn(u):
                t, h = units[u]
                pe.wait_ge(s["at_exp"], u + 1)
                if u >= 2:
                    pe.wait_ge(s["at_PT"], u - 1)
                for k in range(t + 1):
                    ins = pe.transpose(S[2 + u % 2][:, k * P:(k + 1) * P], Pr[:, u % 2, k * P:(k + 1) * P], v.ident)
                ins.then_inc(s["at_T"], 1)

            def weigh(u):
                t, h = units[u]
                pe.wait_ge(s["at_PT"], u + 1)
                if u >= 2:
                    pe.wait_ge(s["at_out"], u - 1)
                for k in range(t + 1):
                    ins = pe.matmul(S[4 + u % 2][:, 0:VD], PT[:, u % 2, k, :], vP[:, k, h * VD:(h + 1) * VD],
                                    start=(k == 0), stop=(k == t))
                ins.then_inc(s["at_O"], 1)

            scores(0)
            for u in range(NU + 1):
                if u + 1 < NU:
                    scores(u + 1)
                if u < NU:
                    turn(u)
                if u >= 1:
                    weigh(u - 1)

        @block.scalar
        def _(act):
            for i, it in enumerate(prep):
                act.wait_ge(s["prep_acc"], i + 1)
                ps = S[i % 8]
                if it[0] == "cq":
                    act.activation(cqT[:, :, it[1] * P:(it[1] + 1) * P],
                                   ps[:, 0:384].rearrange("p (k n) -> p k n", k=3), ACT.Copy).then_inc(s["prep_out"], 1)
                elif it[0] == "ck":
                    act.activation(ckT[:, :, it[1] * P:(it[1] + 1) * P],
                                   ps[:, 0:256].rearrange("p (k n) -> p k n", k=2), ACT.Copy)
                    n = H if it[1] < NP_T else 1
                    dst = kT[NOPE:QK, 0:n, it[1] * P:(it[1] + 1) * P] if it[1] < NP_T else v.krnew[NOPE:QK, :, :]
                    act.activation(dst, ps[NOPE:QK, 256:384].unsqueeze(1).to_broadcast([ROPE, n, P]), ACT.Copy
                                   ).then_inc(s["prep_out"], 1)
                elif it[0] == "uk":
                    act.activation(ukT[0:NOPE, 2 * it[1]:2 * it[1] + 2, :],
                                   ps[0:NOPE, :].rearrange("p (h n) -> p h n", h=2), ACT.Copy).then_inc(s["prep_out"], 1)
                elif it[0] == "q":
                    _, t, half = it
                    if t >= 2:
                        act.wait_ge(s["prep_acc"], where[("qT", t - 2, 1)] + 1)
                    act.activation(qt[:, t % 2, 4 * half:4 * half + 4, :],
                                   ps[:, 0:384].rearrange("p (h n) -> p h n", h=4), ACT.Copy).then_inc(s["prep_out"], 1)
                elif it[0] == "k":
                    act.activation(kT[0:NOPE, it[1], :], ps[0:NOPE, :], ACT.Copy).then_inc(s["prep_out"], 1)
                elif it[0] == "v":
                    act.activation(vP[:, it[1], :], ps[:, :], ACT.Copy).then_inc(s["prep_out"], 1)
                else:
                    _, t, half = it
                    act.activation(qT[0:QK, 4 * half:4 * half + 4, t * P:(t + 1) * P],
                                   ps[0:QK, :].rearrange("p (h n) -> p h n", h=4), ACT.Copy).then_inc(s["prep_out"], 1)

            for u, (t, h) in enumerate(units):
                act.wait_ge(s["at_max"], u + 1)
                if u >= 2:
                    act.wait_ge(s["at_T"], u - 1)
                    act.wait_ge(s["at_out"], u - 1)
                n = (t + 1) * P
                act.activation(Pr[:, u % 2, 0:n], S[u % 2][:, 0:n], ACT.Exp, bias=mx[:, 1, u % 2:u % 2 + 1],
                               scale=ATTN_SCALE, accum_out=mx[:, 2, u % 2:u % 2 + 1]).then_inc(s["at_exp"], 1)

        @block.vector
        def _(dve):
            link = lambda ins: s["dve"](dve, ins)

            def maximum(u):
                t, h = units[u]
                dve.wait_ge(s["at_S"], u + 1)
                link(dve.tensor_reduce(mx[:, 0, u % 2:u % 2 + 1], S[u % 2][:, 0:(t + 1) * P], AX.X, ALU.max))
                if u >= 2:
                    dve.wait_ge(s["at_exp"], u - 1)
                dve.tensor_scalar(mx[:, 1, u % 2:u % 2 + 1], mx[:, 0, u % 2:u % 2 + 1], -ATTN_SCALE, None,
                                  ALU.mult).then_inc(s["at_max"], 1)

            def close(u):
                t, h = units[u]
                dve.wait_ge(s["at_exp"], u + 1)
                link(dve.reciprocal(mx[:, 3, u % 2:u % 2 + 1], mx[:, 2, u % 2:u % 2 + 1]))
                dve.wait_ge(s["at_O"], u + 1)
                dve.tensor_scalar(v.mix[:, t, h * VD:(h + 1) * VD], S[4 + u % 2][:, 0:VD],
                                  mx[:, 3, u % 2:u % 2 + 1], None, ALU.mult).then_inc(s["at_out"], 1)

            maximum(0)
            for u in range(NU + 1):
                if u + 1 < NU:
                    maximum(u + 1)
                if u < NU:
                    dve.wait_ge(s["at_T"], u + 1)
                    if u >= 2:
                        dve.wait_ge(s["at_O"], u - 1)
                    n = (units[u][0] + 1) * P
                    dve.tensor_copy(PT[:, u % 2, 0:units[u][0] + 1, :],
                                    S[2 + u % 2][:, 0:n].rearrange("p (k n) -> p k n", n=P)).then_inc(s["at_PT"], 1)
                if u >= 1:
                    close(u - 1)


def stage_decode_attention(nc, I, O, v, s, S):
    KT = PAST // P
    NK = PAST + DEC_T
    cT = v.cut(27884, 2, PAST)
    kT = v.cut(29932, PAST)
    PT = v.cut(30956, KT + 1, P)
    olT = v.cut(32108, 2, H, DEC_B, DEC_T)
    ol = v.cut(34156, 2, KV_LORA)
    mx = v.cut(34668, 8, 2)
    qlT = v.cut(39276, 2, DEC_B, H, DEC_T)
    Pr = v.cut(41324, NK)
    qr = v.cut(12504, DEC_B, H, DEC_T)
    newk, krnew, ckT, qT, ukT, wuv = v.newk, v.krnew, v.ckT, v.qT, v.ukT, v.wuv
    B = DEC_B
    TG = 5

    with nc.Block() as block:
        @block.sync
        def _(sp):
            for b in range(B):
                sp.dma_start(newk[0:DEC_T, b, :],
                             v.z[b * DEC_T:(b + 1) * DEC_T, NP_T, Q_LORA:Q_LORA + KV_LORA]).then_inc(s["new_in"], 16)
            sp.wait_ge(s["yz_out"], 16)
            for b in range(2, B):
                sp.wait_ge(s["d_O"], b - 1)
                sp.dma_start(v.cache[:, b % 2], I["cache_ckv"][0, b].rearrange("(k p) n -> p k n", p=P)
                             ).then_inc(s["cache_in"][b % 2], 16)
                sp.dma_start(v.krc[b % 2][:, :, NOPE:], I["cache_kr"][0, b].rearrange("(k p) n -> p k n", p=P)
                             ).then_inc(s["cache_in"][b % 2], 16)

        @block.tensor
        def _(pe):
            n = 0
            for h in range(H):
                for k in range(2):
                    if n >= 4:
                        pe.wait_ge(s["ql_out"], n - 3)
                    pe.matmul(S[n % 4][:, 0:P], ukT[0:NOPE, h, k * P:(k + 1) * P], qT[0:NOPE, h, SEQ:],
                              start=True, stop=True).then_inc(s["ql_acc"], 1)
                    n += 1
            pe.wait_ge(s["ql_out"], n + 1)
            for b in range(B):
                pe.wait_ge(s["cache_in"][b % 2], 32 * (b // 2 + 1))
                for g in range(TG + 1):
                    m = (TG + 1) * b + g
                    if m >= 2:
                        pe.wait_ge(s["tr_out"], m - 1)
                    bank = S[3 + m % 2]
                    for j in range(4):
                        if g < 4:
                            k, half = (4 * g + j) % KT, (4 * g + j) // KT
                            ins = pe.transpose(bank[:, j * P:(j + 1) * P],
                                               v.cache[:, b % 2, k, half * P:(half + 1) * P], v.ident)
                        else:
                            ins = pe.transpose(bank[0:QK, j * P:(j + 1) * P],
                                               v.krc[b % 2][:, 4 * (g - 4) + j, :], v.ident)
                    ins.then_inc(s["tr_acc"], 1)
                pe.wait_ge(s["tr_out"], (TG + 1) * (b + 1))
                if b >= 1:
                    pe.wait_ge(s["d_exp"], b)
                for c, (lo, hi) in enumerate(((0, 512), (512, 1024), (1024, NK))):
                    w = hi - lo
                    for k in range(2):
                        rhs = cT[:, k, lo:hi] if c < 2 else ckT[:, k, SEQ + b * DEC_T:SEQ + (b + 1) * DEC_T]
                        pe.matmul(S[c][:, 0:w], qlT[:, k, b, :, :], rhs, start=(k == 0), stop=False)
                    rhs = kT[NOPE:QK, lo:hi] if c < 2 else krnew[NOPE:QK, 0, b * DEC_T:(b + 1) * DEC_T]
                    ins = pe.matmul(S[c][:, 0:w], qr[NOPE:QK, b, :, :], rhs,
                                    start=False, stop=True)
                ins.then_inc(s["d_S"], 1)
                pe.wait_ge(s["d_exp"], b + 1)
                for g in range(3):
                    bank = S[5 + g % 2]
                    if g == 2:
                        pe.wait_ge(s["p_out"], 3 * b + 1)
                    elif b >= 1:
                        pe.wait_ge(s["p_out"], 3 * b)
                    if g < 2:
                        for j in range(4):
                            k = 4 * g + j
                            ins = pe.transpose(bank[:, j * P:(j + 1) * P], Pr[:, k * P:(k + 1) * P], v.ident)
                    else:
                        ins = pe.transpose(bank[0:DEC_T, 0:P], Pr[:, PAST:NK], v.ident)
                    ins.then_inc(s["p_acc"], 1)
                pe.wait_ge(s["p_out"], 3 * (b + 1))
                if b == 0:
                    pe.wait_ge(s["new_in"], 16 * B)
                for k in range(KT):
                    pe.matmul(S[7][:, 0:KV_LORA], PT[:, k, :], v.cache[:, b % 2, k, :], start=(k == 0), stop=False)
                pe.matmul(S[7][:, 0:KV_LORA], PT[0:DEC_T, KT, :], newk[0:DEC_T, b, :], start=False, stop=True
                          ).then_inc(s["d_O"], 1)
                pe.wait_ge(s["ol_ready"], b + 1)
                for k in range(2):
                    ins = pe.transpose(S[7][:, 256 + k * P:256 + (k + 1) * P], ol[:, b % 2, k * P:(k + 1) * P], v.ident)
                ins.then_inc(s["ol_T"], 1)
                pe.wait_ge(s["ol_out"], b + 1)
            for h in range(H):
                for k in range(2):
                    ins = pe.matmul(S[0][:, h * VD:(h + 1) * VD], olT[:, k, h, :, :], wuv[:, k, h * VD:(h + 1) * VD],
                                    start=(k == 0), stop=(k == 1))
            ins.then_inc(s["datt_acc"], 1)

        @block.scalar
        def _(act):
            for b in range(B):
                for g in range(TG + 1):
                    m = (TG + 1) * b + g
                    act.wait_ge(s["tr_acc"], m + 1)
                    if g == 0 and b >= 1:
                        act.wait_ge(s["d_S"], b)
                    if g < 4:
                        half, c = g // 2, (g % 2) * 512
                        ins = act.activation(cT[:, half, c:c + 512], S[3 + m % 2][:, :], ACT.Copy)
                    else:
                        c = (g - 4) * 512
                        ins = act.activation(kT[NOPE:QK, c:c + 512], S[3 + m % 2][NOPE:QK, :], ACT.Copy)
                    ins.then_inc(s["tr_out"], 1)
                act.wait_ge(s["d_max"], b + 1)
                for c, (lo, hi) in enumerate(((0, 512), (512, 1024), (1024, NK))):
                    ins = act.activation(Pr[:, lo:hi], S[c][:, 0:hi - lo], ACT.Exp, bias=mx[:, 4, 0:1],
                                         scale=ATTN_SCALE, accum_out=mx[:, 5 + c, 0:1])
                ins.then_inc(s["d_exp"], 1)

        @block.vector
        def _(dve):
            link = lambda ins: s["dve"](dve, ins)
            n = 0
            for h in range(H):
                for k in range(2):
                    dve.wait_ge(s["ql_acc"], n + 1)
                    dve.tensor_copy(qlT[:, k, :, h, :],
                                    S[n % 4][:, 0:P].rearrange("p (b t) -> p b t", b=B)).then_inc(s["ql_out"], 1)
                    n += 1
            dve.tensor_copy(qr[NOPE:QK].rearrange("p b h t -> p h b t"),
                            qT[NOPE:QK, :, SEQ:].rearrange("p h (b t) -> p h b t", b=B)).then_inc(s["ql_out"], 1)
            for b in range(B):
                dve.wait_ge(s["d_S"], b + 1)
                for c, w in enumerate((512, 512, DEC_T)):
                    ins = dve.tensor_reduce(mx[:, c, 0:1], S[c][:, 0:w], AX.X, ALU.max)
                link(ins)
                link(dve.tensor_tensor(mx[:, 3, 0:1], mx[:, 0, 0:1], mx[:, 1, 0:1], ALU.max))
                link(dve.tensor_tensor(mx[:, 3, 0:1], mx[:, 3, 0:1], mx[:, 2, 0:1], ALU.max))
                dve.tensor_scalar(mx[:, 4, 0:1], mx[:, 3, 0:1], -ATTN_SCALE, None, ALU.mult).then_inc(s["d_max"], 1)
                for g in range(3):
                    dve.wait_ge(s["p_acc"], 3 * b + g + 1)
                    if g < 2:
                        ins = dve.tensor_copy(PT[:, 4 * g:4 * g + 4, :],
                                              S[5 + g % 2][:, :].rearrange("p (k n) -> p k n", n=P))
                    else:
                        ins = dve.tensor_copy(PT[0:DEC_T, KT, :], S[5 + g % 2][0:DEC_T, 0:P])
                    ins.then_inc(s["p_out"], 1)
                dve.wait_ge(s["d_exp"], b + 1)
                link(dve.tensor_tensor(mx[:, 0, 1:2], mx[:, 5, 0:1], mx[:, 6, 0:1], ALU.add))
                link(dve.tensor_tensor(mx[:, 0, 1:2], mx[:, 0, 1:2], mx[:, 7, 0:1], ALU.add))
                link(dve.reciprocal(mx[:, 1, 1:2], mx[:, 0, 1:2]))
                dve.wait_ge(s["d_O"], b + 1)
                dve.tensor_scalar(ol[:, b % 2, :], S[7][:, 0:KV_LORA], mx[:, 1, 1:2], None, ALU.mult
                                  ).then_inc(s["ol_ready"], 1)
                dve.wait_ge(s["ol_T"], b + 1)
                dve.tensor_copy(olT[:, :, :, b, :],
                                S[7][:, 256:512].rearrange("p (k h t) -> p k h t", k=2, h=H)).then_inc(s["ol_out"], 1)
            dve.wait_ge(s["datt_acc"], 1)
            dve.tensor_copy(v.mix[:, NP_T, 0:H * VD], S[0][:, :])


def stage_output_router(nc, I, O, v, s, S):
    wo = v.cut(27884, 2, KD, 512)
    x = v.cut(36076, NT, D)
    G = v.cut(41196, 4, 2, D)
    ln = v.cut(49388, 2, D)
    mixT = v.cut(47340, 2, KD, P)
    u2T = v.cut(11192, 2, KD, P)
    rw = v.cut(13240, KD, NE)
    rb = v.cut(13496, NE)
    u2 = v.cut(15064, 2, D)
    x1 = v.cut(17112, 2, D)
    tmp = v.cut(19160, 2, D)
    o = 13528
    bn = v.cut(o, 2, 2, 6)
    mv = v.cut(o + 24, NT, 2)
    rs = v.cut(o + 34, NT, 2)
    lg = v.cut(o + 44, NT, NE)
    mask = v.cut(o + 204, NT, NE)
    top = v.cut(o + 364, NT, 8)
    topf = v.cut(o + 404, NT, 8)
    ex = v.cut(o + 444, NT, TOPK)
    es = v.cut(o + 464, NT, 2)
    oh = v.cut(o + 474, NT, TOPK, NE)
    assert o + 1114 <= 15064
    cnt = v.cut(21208, 6, NE)
    gs = v.cut(21400, NT, NE)
    slotf = v.cut(21560, NT, TOPK)
    dummy = v.cut(21580, 2, NE)
    v.table = v.cut(2800, MAX_BLOCKS + 2).bitcast(U32)
    split = v.cut(21760, 2, NT, TOPK).bitcast(U32)
    splitf = v.cut(21800, 2, NT, TOPK)
    hotm = v.cut(21840, 4, P)
    hotd = v.cut(22352, 4, MAX_BLOCKS + 2)
    topi = v.cut(21720, NT, 8).bitcast(U32)
    v.slot = v.cut(2700, NT, TOPK).bitcast(U32)
    v.wts = v.cut(2720, NT, TOPK)
    v.cum = v.cut(2740, NE + 1).bitcast(I32)
    iota = v.const[:, C_IOTA:C_IOTA + P]
    PARTS = (2, 3, 4, 5)
    two = lambda b: v.psum[:, b:b + 2, :].rearrange("p a n -> p (a n)")

    with nc.Block() as block:
        @block.sync
        def _(sp):
            for j in range(2):
                sp.dma_start(wo[:, j], I["w_o"][0][:, j * 512:(j + 1) * 512].rearrange("(k p) n -> p k n", p=P)
                             ).then_inc(s["wo_in"], 16)
            sp.wait_ge(s["G_out"], 16)
            sp.dma_start(v.d_gate, G[:, 3]).then_inc(s["st_out"], 16)
            first_up = v.cut(3000, 2, KD, 512)
            for g in range(2):
                sp.dma_start(first_up[:, g], I["w_up"][0, 0].rearrange("(k p) n -> p k n", p=P)
                             [:, :, g * FF:g * FF + 512]).then_inc(s["up_in"][0][0], 16)
            for t in range(NT):
                sp.wait_ge(s["x1_ready"], t + 1)
                sp.dma_start(v.d_x1[t * P:(t + 1) * P, :], x1[:, t % 2]).then_inc(s["x1_out"][t % 2], 16)
                sp.wait_ge(s["u2_ready"], t + 1)
                sp.dma_start(v.d_u2[t * P:(t + 1) * P, :], u2[:, t % 2]).then_inc(s["u2_out"][t % 2], 16)
            sp.wait_ge(s["st_out"], 16)
            for par, n in ((0, (NT + 1) // 2), (1, NT // 2)):
                sp.wait_ge(s["x1_out"][par], 16 * n)
                sp.wait_ge(s["u2_out"][par], 16 * n)

        @block.scalar
        def _(act):
            act.dma_start(x[:, 0:NP_T, :], I["x_prompt"][0].rearrange("(t p) d -> p t d", p=P)).then_inc(s["x2_in"], 16)
            act.dma_start(x[:, NP_T, :], I["x_sample"].rearrange("b t d -> (b t) d")).then_inc(s["x2_in"], 16)
            act.dma_start(ln[:, 0], bcast_rows(I["ln1_g"][0], P)).then_inc(s["x2_in"], 16)
            act.dma_start(ln[:, 1], bcast_rows(I["ln1_b"][0], P)).then_inc(s["x2_in"], 16)
            act.dma_start(rw, I["router_w"][0].rearrange("(k p) n -> p k n", p=P)).then_inc(s["rw_in"], 16)
            act.dma_start(rb, bcast_rows(I["router_b"][0], P)).then_inc(s["rw_in"], 16)
            for i in range(16):
                part, who, half = i // 4, i // 2 % 2, i % 2
                act.wait_ge(s["G_acc"], i + 1)
                act.activation(G[:, part, who, half * 512:(half + 1) * 512], S[4 + i % 4][:, :], ACT.Copy
                               ).then_inc(s["G_out"], 1)

            def mix_T(t):
                for j in range(2):
                    act.wait_ge(s["mT_acc"], 2 * t + j + 1)
                    if t >= 2:
                        act.wait_ge(s["wo_acc"], t - 1)
                    act.activation(mixT[:, t % 2, 4 * j:4 * j + 4, :],
                                   S[j][:, :].rearrange("p (k n) -> p k n", n=P), ACT.Copy).then_inc(s["mT_out"], 1)

            act.wait_ge(s["st_out"], 16)
            mix_T(0)
            for t in range(NT):
                if t + 1 < NT:
                    mix_T(t + 1)
                act.wait_ge(s["var1"], t + 1)
                act.activation(rs[:, t, 1:2], rs[:, t, 0:1], ACT.Sqrt).then_inc(s["root1"], 1)
                for j in range(2):
                    act.wait_ge(s["uT2_acc"], 2 * t + j + 1)
                    if t >= 2:
                        act.wait_ge(s["lg_acc"], t - 1)
                    act.activation(u2T[:, t % 2, 4 * j:4 * j + 4, :],
                                   S[6 + j][:, :].rearrange("p (k n) -> p k n", n=P), ACT.Copy
                                   ).then_inc(s["uT2_out"], 1)
            for t in range(NT):
                act.wait_ge(s["top_neg"], t + 1)
                act.activation(ex[:, t, :], top[:, t, 0:TOPK], ACT.Exp, bias=es[:, t, 0:1],
                               accum_out=es[:, t, 1:2]).then_inc(s["ex_ready"], 1)

        @block.gpsimd
        def _(pool):
            pool.wait_ge(s["G_out"], 16)
            pool.tensor_scalar(G[:, 2], G[:, 2], 1.0, None, ALU.add).then_inc(s["sc2_ready"], 1)
            pool.wait_ge(s["sc2_ready"], 1)
            for t in range(NT):
                who = 0 if t < NP_T else 1
                pool.wait_ge(s["x1_ready"], t + 1)
                if t >= 2:
                    pool.wait_ge(s["u2_out"][t % 2], 16 * (t // 2))
                    pool.wait_ge(s["uT2_acc"], 2 * (t - 1))
                s["pool"](pool, pool.tensor_tensor(u2[:, t % 2], x1[:, t % 2], G[:, 2, who], ALU.mult))
                pool.tensor_tensor(u2[:, t % 2], u2[:, t % 2], G[:, 1, who], ALU.add).then_inc(s["u2_ready"], 1)

        @block.tensor
        def _(pe):
            for i in range(16):
                part, who, half = i // 4, i // 2 % 2, i % 2
                if i >= 4:
                    pe.wait_ge(s["G_out"], i - 3)
                c = PARTS[part] * D + half * 512
                pe.matmul(S[4 + i % 4][:, :], v.rows[0:9, R_SELC + who * P:R_SELC + (who + 1) * P],
                          v.e9[0:9, c:c + 512], start=True, stop=True).then_inc(s["G_acc"], 1)

            def mix_T(t):
                for j in range(2):
                    if t:
                        pe.wait_ge(s["mT_out"], 2 * t - 1 + j)
                    for k in range(4):
                        ins = pe.transpose(S[j][:, k * P:(k + 1) * P], v.mix[:, t, (4 * j + k) * P:(4 * j + k + 1) * P],
                                           v.ident)
                    ins.then_inc(s["mT_acc"], 1)

            def project(t):
                pe.wait_ge(s["mT_out"], 2 * t + 2)
                if t == 0:
                    pe.wait_ge(s["wo_in"], 32)
                    pe.wait_ge(s["G_out"], 16)
                if t >= 2:
                    pe.wait_ge(s["wo_read"], t - 1)
                for n in range(2):
                    for k in range(KD):
                        ins = pe.matmul(S[2 + 2 * (t % 2) + n][:, :], mixT[:, t % 2, k, :], wo[:, n, k, :],
                                        start=(k == 0), stop=(k == KD - 1))
                ins.then_inc(s["wo_acc"], 1)

            def router(t):
                pe.wait_ge(s["u2_ready"], t + 1)
                for j in range(2):
                    if t:
                        pe.wait_ge(s["lg_read"], t) if j == 0 else pe.wait_ge(s["uT2_out"], 2 * t)
                    for k in range(4):
                        ins = pe.transpose(S[6 + j][:, k * P:(k + 1) * P],
                                           u2[:, t % 2, (4 * j + k) * P:(4 * j + k + 1) * P], v.ident)
                    ins.then_inc(s["uT2_acc"], 1)
                pe.wait_ge(s["uT2_out"], 2 * t + 2)
                if t == 0:
                    pe.wait_ge(s["rw_in"], 32)
                for k in range(KD):
                    ins = pe.matmul(S[6][:, 0:NE], u2T[:, t % 2, k, :], rw[:, k, :], start=(k == 0), stop=(k == KD - 1))
                ins.then_inc(s["lg_acc"], 1)

            mix_T(0)
            for t in range(NT):
                if t + 1 < NT:
                    mix_T(t + 1)
                project(t)
                if t >= 1:
                    router(t - 1)
            router(NT - 1)
            pe.wait_ge(s["mask_ready"], NT)
            for t in range(NT):
                for tt in range(t):
                    pe.matmul(S[0][:, t * NE:(t + 1) * NE], v.ones, mask[:, tt, :], start=(tt == 0), stop=False)
                pe.matmul(S[0][:, t * NE:(t + 1) * NE], v.const[:, C_TRI:C_TRI + P], mask[:, t, :],
                          start=(t == 0), stop=True)
            for t in range(NT):
                ins = pe.matmul(S[1][:, 0:NE], v.ones, mask[:, t, :], start=(t == 0), stop=(t == NT - 1))
            ins.then_inc(s["pos_acc"], 1)
            for i in range(NT * TOPK):
                pe.wait_ge(s["hot_ready"], i + 1)
                ins = pe.matmul(S[2][:, 0:MAX_BLOCKS + 2], hotm[:, i % 4, :], hotd[:, i % 4, :],
                                start=(i == 0), stop=(i == NT * TOPK - 1))
                ins.then_inc(s["hot_acc"], 1)

        @block.vector
        def _(dve):
            link = lambda ins: s["dve"](dve, ins)
            dve.wait_ge(s["x2_in"], 64)
            dve.wait_ge(s["G_out"], 16)
            def norm(t):
                who = 0 if t < NP_T else 1
                dve.wait_ge(s["wo_acc"], t + 1)
                tm = tmp[:, t % 2]
                dve.tensor_tensor(tm, two(2 + 2 * (t % 2)), G[:, 0, who], ALU.mult).then_inc(s["wo_read"], 1)
                dve.wait_ge(s["wo_read"], t + 1)
                link(dve.scalar_tensor_tensor(x[:, t], x[:, t], ALPHA, tm, ALU.mult, ALU.add))
                for j in range(2):
                    ins = dve.bn_stats(bn[:, t % 2, j, :], x[:, t, j * 512:(j + 1) * 512])
                link(ins)
                link(dve.bn_aggr(mv[:, t, :], bn[:, t % 2]))
                dve.tensor_scalar(rs[:, t, 0:1], mv[:, t, 1:2], EPS, None, ALU.add).then_inc(s["var1"], 1)
                dve.wait_ge(s["root1"], t + 1)
                link(dve.reciprocal(rs[:, t, 0:1], rs[:, t, 1:2]))
                if t >= 2:
                    dve.wait_ge(s["x1_out"][t % 2], 16 * (t // 2))
                    dve.wait_ge(s["u2_ready"], t - 1)
                xo = x1[:, t % 2]
                link(dve.tensor_scalar(xo, x[:, t], mv[:, t, 0:1], rs[:, t, 0:1], ALU.subtract, ALU.mult))
                link(dve.tensor_tensor(xo, xo, ln[:, 0], ALU.mult))
                dve.tensor_tensor(xo, xo, ln[:, 1], ALU.add).then_inc(s["x1_ready"], 1)

            def choose(t):
                dve.wait_ge(s["lg_acc"], t + 1)
                dve.tensor_tensor(lg[:, t, :], S[6][:, 0:NE], rb, ALU.add).then_inc(s["lg_read"], 1)
                dve.wait_ge(s["lg_read"], t + 1)
                link(dve.max(top[:, t, :], lg[:, t, :]))
                dve.tensor_scalar(es[:, t, 0:1], top[:, t, 0:1], -1.0, None, ALU.mult).then_inc(s["top_neg"], 1)
                link(dve.max_index(topi[:, t, :], top[:, t, :], lg[:, t, :]))
                link(dve.tensor_copy(topf[:, t, :], topi[:, t, :]))
                for k in range(TOPK):
                    ins = dve.tensor_scalar(oh[:, t, k, :], iota[:, 0:NE], topf[:, t, k:k + 1], None, ALU.is_equal)
                link(ins)
                dve.tensor_tensor(dummy[:, 0], oh[:, t, 0], oh[:, t, 1], ALU.add)
                link(dve.tensor_tensor(dummy[:, 1], oh[:, t, 2], oh[:, t, 3], ALU.add))
                dve.tensor_tensor(mask[:, t, :], dummy[:, 0], dummy[:, 1], ALU.add).then_inc(s["mask_ready"], 1)
                dve.wait_ge(s["mask_ready"], t + 1)

            for t in range(NT):
                norm(t)
                if t >= 1:
                    choose(t - 1)
            choose(NT - 1)
            for t in range(NT):
                dve.wait_ge(s["ex_ready"], t + 1)
                link(dve.reciprocal(es[:, t, 0:1], es[:, t, 1:2]))
                dve.tensor_scalar(v.wts[:, t, :], ex[:, t, :], es[:, t, 0:1], None, ALU.mult)
            dve.wait_ge(s["pos_acc"], 1)
            c, nb, ns, inc = cnt[:, 0], cnt[:, 1], cnt[:, 2], cnt[:, 3]
            dve.memset(cnt[:, 4], 1.0)
            link(dve.tensor_copy(c, S[1][:, 0:NE]))
            link(dve.tensor_scalar(nb, c, float(P), 1.0, ALU.is_gt, ALU.add))
            for j in range(2, NT):
                link(dve.tensor_scalar(ns, c, float(P * j), None, ALU.is_gt))
                link(dve.tensor_tensor(nb, nb, ns, ALU.add))
            link(dve.tensor_tensor_scan(inc, cnt[:, 4], nb, 0.0, ALU.mult, ALU.add))
            link(dve.tensor_tensor(ns, inc, nb, ALU.subtract))
            link(dve.tensor_scalar(cnt[:, 5], ns, float(P), None, ALU.mult))
            dve.memset(v.cum[0:1, 0:1], 0)
            dve.tensor_copy(v.cum[0:1, 1:NE + 1], inc[0:1, :])
            for t in range(NT):
                ins = dve.tensor_tensor(gs[:, t, :], S[0][:, t * NE:(t + 1) * NE], cnt[:, 5], ALU.add)
            link(ins)
            for t in range(NT):
                for k in range(TOPK):
                    link(dve.tensor_tensor_reduce(dummy[:, 0], oh[:, t, k, :], gs[:, t, :], 1.0, 0.0,
                                                  ALU.mult, ALU.add, slotf[:, t, k:k + 1]))
            link(dve.tensor_copy(v.slot, slotf))
            dve.tensor_scalar(split[:, 0], v.slot, 127, None, ALU.bitwise_and)
            link(dve.tensor_scalar(split[:, 1], v.slot, 7, None, ALU.logical_shift_right))
            link(dve.tensor_copy(splitf, split))
            for i in range(NT * TOPK):
                tt, k = i // TOPK, i % TOPK
                if i >= 4:
                    dve.wait_ge(s["hot_acc"], i - 3)
                dve.tensor_scalar(hotm[:, i % 4, :], iota, splitf[:, 0, tt, k:k + 1], None, ALU.is_equal)
                dve.tensor_scalar(hotd[:, i % 4, :], iota[:, 0:MAX_BLOCKS + 2], splitf[:, 1, tt, k:k + 1],
                                  v.const[:, C_TOK + tt:C_TOK + tt + 1], ALU.is_equal, ALU.mult
                                  ).then_inc(s["hot_ready"], 1)
            dve.wait_ge(s["hot_acc"], NT * TOPK)
            dve.tensor_copy(v.table, S[2][:, 0:MAX_BLOCKS + 2])


def stage_experts(nc, I, O, v, s, S):
    up = [[v.cut(3000 + (2 * half + par) * 8192, 2, KD, 512) for half in range(2)] for par in range(2)]
    down = v.cut(3000 + 4 * 8192, 2, 4, D)
    xg = v.cut(43960, D)
    xT = v.cut(44984, KD, P)
    bu = v.cut(46008, 2 * FF)
    hid = v.cut(48056, FF)
    hidT = v.cut(49080, 2, 4, P)
    bd = v.cut(50104, 2, D)
    glu, sig, lin = v.cut(128, 512), v.cut(640, 512), v.cut(1152, 512)
    y = v.cut(1664, D)
    idx = v.cut(52152, 1).bitcast(U32)
    w_up = I["w_up"][0].rearrange("e (k p) (g j n) -> e p k g j n", p=P, g=2, j=2)
    w_down = I["w_down"][0].rearrange("e (j p k) n -> e p j (k n)", j=2, k=4)

    def cum(eng, i, least=0):
        return eng.value_load(v.cum[0:1, bass.ds(i, 1)] if not isinstance(i, int) else v.cum[0:1, i:i + 1],
                              min_val=least, max_val=MAX_BLOCKS)

    with nc.Block() as block:
        @block.sync
        def _(sp):
            def load_up(e, par, half):
                for g in range(2):
                    sp.dma_start(up[par][half][:, g], w_up[bass.ds(e, 1), :, :, g, half, :]
                                 .rearrange("e p k n -> p (e k) n")).then_inc(s["up_in"][par][half], 16)

            def load_down(e):
                sp.dma_start(down.rearrange("p j k n -> p j (k n)"),
                             w_down[bass.ds(e, 1)].rearrange("e p j n -> p (e j) n")).then_inc(s["down_in"], 16)

            def load_bias(e, par):
                sp.dma_start(bu, I["b_up"][0][bass.ds(e, 1), :].rearrange("e n -> (e n)").partition_broadcast(P)
                              ).then_inc(s["bias_in"], 16)
                sp.dma_start(bd[:, par], I["b_down"][0][bass.ds(e, 1), :].rearrange("e n -> (e n)")
                             .partition_broadcast(P)).then_inc(s["bias_in"], 16)

            def step(e, par, last=False):
                blocks = cum(sp, e, least=1)
                sp.wait_ge(s["hid_ready"], blocks * 2)
                load_bias(e, par)
                sp.wait_ge(s["y_acc"], blocks)
                load_down(e)
                if not last:
                    load_up(e + 1, 1 - par, 0)
                    load_up(e + 1, 1 - par, 1)

            load_bias(0, 0)
            load_up(0, 0, 1)
            load_down(0)
            load_up(1, 1, 0)
            load_up(1, 1, 1)
            with sp.Fori(0, NE // 2 - 1) as i:
                step(i * 2 + 1, 1)
                step(i * 2 + 2, 0)
            step(NE - 1, 1, last=True)

        @block.gpsimd
        def _(pool):
            def gather(b):
                pool.tensor_copy(idx, v.table[:, bass.ds(b, 1)]).then_inc(s["idx_in"], 1)
                pool.wait_ge(s["idx_in"], b + 1)
                pool.sem_inc(s["idx_seen"], 1)
                pool.indirect_dma_start(out=xg, out_offset=None, in_=v.d_u2,
                                        in_offset=bass.IndirectOffsetOnAxis(ap=idx, axis=0)).then_inc(s["xg_in"], 16)

            pool.sem_inc(s["y_stored"], 1)
            gather(0)
            pool.wait_ge(s["turned"], 2)
            gather(1)
            total = cum(pool, NE, least=NE)
            with pool.Fori(0, total) as b:
                pool.wait_ge(s["turned"], b * 4 + 5)
                gather(b + 2)
                pool.wait_ge(s["y_ready"], b + 2)
                pool.dma_start(v.d_y[bass.ds(b * P, P), :], y).then_inc(s["y_out"], 16)
                pool.wait_ge(s["y_out"], b * 16 + 16)
                pool.sem_inc(s["y_stored"], 1)
            pool.wait_ge(s["xg_in"], total * 16 + 32)
            pool.wait_ge(s["y_stored"], total + 1)

        @block.scalar
        def _(act):
            def x_evac(j):
                act.activation(xT[:, 4 * j:4 * j + 4, :], S[6 + j][:, :].rearrange("p (k n) -> p k n", n=P),
                               ACT.Copy).then_inc(s["turn_out"], 1)

            for j in range(2):
                act.wait_ge(s["turned"], j + 1)
                x_evac(j)

            blocks = cum(act, NE, least=NE)
            with act.Fori(0, blocks) as b:
                n = b * 4
                act.wait_ge(s["glu_ready"], b * 2 + 1)
                act.activation(sig, glu, ACT.Sigmoid, scale=SW_ALPHA).then_inc(s["sig_ready"], 1)
                act.wait_ge(s["turned"], n + 3)
                act.activation(hidT[:, 0], S[6][:, :].rearrange("p (k n) -> p k n", n=P), ACT.Copy
                               ).then_inc(s["turn_out"], 1)
                act.wait_ge(s["turned"], n + 4)
                act.activation(xT[:, 0:4, :], S[7][:, :].rearrange("p (k n) -> p k n", n=P), ACT.Copy
                               ).then_inc(s["turn_out"], 1)
                act.wait_ge(s["turned"], n + 5)
                act.activation(xT[:, 4:8, :], S[6][:, :].rearrange("p (k n) -> p k n", n=P), ACT.Copy
                               ).then_inc(s["turn_out"], 1)
                act.wait_ge(s["glu_ready"], b * 2 + 2)
                act.activation(sig, glu, ACT.Sigmoid, scale=SW_ALPHA).then_inc(s["sig_ready"], 1)
                act.wait_ge(s["turned"], n + 6)
                act.activation(hidT[:, 1], S[7][:, :].rearrange("p (k n) -> p k n", n=P), ACT.Copy
                               ).then_inc(s["turn_out"], 1)


        @block.tensor
        def _(pe):
            def x_turn(j, bank):
                for k in range(4):
                    ins = pe.transpose(bank[:, k * P:(k + 1) * P], xg[:, (4 * j + k) * P:(4 * j + k + 1) * P], v.ident)
                ins.then_inc(s["turned"], 1)

            def h_turn(j, bank):
                for k in range(4):
                    ins = pe.transpose(bank[:, k * P:(k + 1) * P], hid[:, j * 512 + k:(j + 1) * 512:4], v.ident)
                ins.then_inc(s["turned"], 1)

            pe.wait_ge(s["xg_in"], 16)
            for j in range(2):
                x_turn(j, S[6 + j])

            def expert(e, par):
                lo, hi = cum(pe, e), cum(pe, e + 1)
                with pe.Fori(lo, hi) as b:
                    n = b * 4
                    pe.wait_ge(s["turn_out"], n + 2)
                    for half in range(2):
                        pe.wait_ge(s["up_read"][half], b + 1)
                        pe.wait_ge(s["up_in"][par][half], (e - par) * 16 + 32)
                        for g in range(2):
                            for k in range(KD):
                                ins = pe.matmul(S[2 * half + g][:, :], xT[:, k, :], up[par][half][:, g, k, :],
                                                start=(k == 0), stop=(k == KD - 1))
                        ins.then_inc(s["up_acc"], 1)
                    pe.wait_ge(s["hid_ready"], b * 2 + 1)
                    h_turn(0, S[6])
                    pe.wait_ge(s["xg_in"], b * 16 + 32)
                    x_turn(0, S[7])
                    pe.wait_ge(s["turn_out"], n + 3)
                    x_turn(1, S[6])
                    pe.wait_ge(s["y_ready"], b + 1)
                    pe.wait_ge(s["down_in"], e * 16 + 16)

                    def down_half(j, c):
                        for k in range(4):
                            ins = pe.matmul(S[4 + c][:, :], hidT[:, j, k, :], down[:, j, k, c * 512:(c + 1) * 512],
                                            start=(j == 0 and k == 0), stop=(j == 1 and k == 3))
                        return ins
                    down_half(0, 0)
                    pe.wait_ge(s["hid_ready"], b * 2 + 2)
                    pe.wait_ge(s["turn_out"], n + 4)
                    h_turn(1, S[7])
                    down_half(0, 1)
                    pe.wait_ge(s["turn_out"], n + 6)
                    down_half(1, 0)
                    down_half(1, 1).then_inc(s["y_acc"], 1)

            with pe.Fori(0, NE // 2) as i:
                expert(i * 2, 0)
                expert(i * 2 + 1, 1)

        @block.vector
        def _(dve):
            def half_step(b, j):
                dve.wait_ge(s["up_acc"], b * 2 + j + 1)
                dve.tensor_tensor(glu, S[2 * j][:, :], bu[:, j * 512:(j + 1) * 512], ALU.add
                                  ).then_inc(s["glu_sum"], 1)
                dve.tensor_tensor(lin, S[2 * j + 1][:, :], bu[:, FF + j * 512:FF + (j + 1) * 512], ALU.add
                                  ).then_inc(s["up_read"][j], 1)
                dve.wait_ge(s["glu_sum"], b * 2 + j + 1)
                dve.tensor_scalar(glu, glu, LIMIT, None, ALU.min).then_inc(s["glu_ready"], 1)
                dve.wait_ge(s["up_read"][j], b + 2)
                dve.tensor_scalar(lin, lin, LIMIT, -LIMIT, ALU.min, ALU.max).then_inc(s["lin_ready"], 1)
                dve.wait_ge(s["sig_ready"], b * 2 + j + 1)
                dve.tensor_tensor(glu, glu, sig, ALU.mult).then_inc(s["glu_gated"], 1)
                dve.wait_ge(s["glu_gated"], b * 2 + j + 1)
                dve.wait_ge(s["lin_ready"], b * 2 + j + 1)
                dve.scalar_tensor_tensor(hid[:, j * 512:(j + 1) * 512], lin, 1.0, glu, ALU.add, ALU.mult
                                         ).then_inc(s["hid_ready"], 1)
                dve.wait_ge(s["hid_ready"], b * 2 + j + 1)

            def expert(e, par):
                lo, hi = cum(dve, e), cum(dve, e + 1)
                with dve.Fori(lo, hi) as b:
                    dve.wait_ge(s["bias_in"], e * 32 + 32)
                    half_step(b, 0)
                    half_step(b, 1)
                    dve.wait_ge(s["y_acc"], b + 1)
                    dve.wait_ge(s["y_stored"], b + 1)
                    dve.tensor_tensor(y, v.psum[:, 4:6, :].rearrange("p a n -> p (a n)"), bd[:, par], ALU.add
                                      ).then_inc(s["y_ready"], 1)

            dve.sem_inc(s["up_read"][0], 1)
            dve.sem_inc(s["up_read"][1], 1)
            dve.sem_inc(s["y_ready"], 1)
            with dve.Fori(0, NE // 2) as i:
                expert(i * 2, 0)
                expert(i * 2 + 1, 1)


def stage_combine(nc, I, O, v, s, S):
    x1 = v.cut(3000, NT, D)
    G = v.cut(8120, 2, D)
    ln = v.cut(10168, 2, D)
    yg = v.cut(12216, 2 * TOPK, D)
    f = v.cut(20408, 2, D)
    bn = v.cut(22456, 2, 2, 6)
    mv = v.cut(22480, NT, 2)
    rs = v.cut(22490, NT, 2)

    with nc.Block() as block:
        @block.sync
        def _(sp):
            sp.dma_start(x1, v.d_x1.rearrange("(t p) d -> p t d", p=P)).then_inc(s["f_in"], 16)
            sp.dma_start(G, v.d_gate).then_inc(s["f_in"], 16)
            sp.dma_start(ln[:, 0], bcast_rows(I["ln2_g"][0], P)).then_inc(s["f_in"], 16)
            sp.dma_start(ln[:, 1], bcast_rows(I["ln2_b"][0], P)).then_inc(s["f_in"], 16)
            for t in range(NT):
                sp.wait_ge(s["fin_ready"], t + 1)
                if t < NP_T:
                    sp.dma_start(O["y_prompt"][0, t * P:(t + 1) * P, :], x1[:, t]).then_inc(s["fin_out"], 16)
                else:
                    sp.dma_start(O["y_sample"].rearrange("b t d -> (b t) d"), x1[:, t]).then_inc(s["fin_out"], 16)
            sp.wait_ge(s["fin_out"], 16 * NT)

        @block.gpsimd
        def _(pool):
            for t in range(NT):
                if t >= 2:
                    pool.wait_ge(s["yg_read"], t - 1)
                for k in range(TOPK):
                    pool.indirect_dma_start(out=yg[:, (t % 2) * TOPK + k], out_offset=None, in_=v.d_y,
                                            in_offset=bass.IndirectOffsetOnAxis(ap=v.slot[:, t, k:k + 1], axis=0)
                                            ).then_inc(s["yg_in"][t % 2], 16)

            pool.wait_ge(s["f_in"], 64)
            for t in range(NT):
                pool.wait_ge(s["norm2"], t + 1)
                s["pool"](pool, pool.tensor_tensor(x1[:, t], x1[:, t], ln[:, 0], ALU.mult))
                pool.tensor_tensor(x1[:, t], x1[:, t], ln[:, 1], ALU.add).then_inc(s["fin_ready"], 1)

        @block.scalar
        def _(act):
            def first(t):
                act.wait_ge(s["yg_in"][t % 2], 16 * TOPK * (t // 2 + 1))
                if t >= 2:
                    act.wait_ge(s["res2"], t - 1)
                act.activation(f[:, t % 2], yg[:, (t % 2) * TOPK], ACT.Copy, scale=v.wts[:, t, 0:1]
                               ).then_inc(s["f0"], 1)

            first(0)
            for t in range(NT):
                if t + 1 < NT:
                    first(t + 1)
                act.wait_ge(s["var2"], t + 1)
                act.activation(rs[:, t, 1:2], rs[:, t, 0:1], ACT.Sqrt).then_inc(s["root2"], 1)

        @block.vector
        def _(dve):
            link = lambda ins: s["dve"](dve, ins)
            dve.wait_ge(s["f_in"], 64)
            for t in range(NT):
                ins = dve.tensor_scalar(x1[:, t], x1[:, t], ALPHA, None, ALU.mult)
            link(ins)
            for t in range(NT):
                who = 0 if t < NP_T else 1
                a = f[:, t % 2]
                dve.wait_ge(s["f0"], t + 1)
                for k in range(1, TOPK):
                    ins = dve.scalar_tensor_tensor(a, yg[:, (t % 2) * TOPK + k], v.wts[:, t, k:k + 1], a,
                                                   ALU.mult, ALU.add)
                    if k < TOPK - 1:
                        link(ins)
                ins.then_inc(s["yg_read"], 1)
                dve.wait_ge(s["yg_read"], t + 1)
                link(dve.tensor_tensor(a, a, G[:, who], ALU.mult))
                dve.tensor_tensor(x1[:, t], x1[:, t], a, ALU.add).then_inc(s["res2"], 1)
                dve.wait_ge(s["res2"], t + 1)
                for j in range(2):
                    ins = dve.bn_stats(bn[:, t % 2, j, :], x1[:, t, j * 512:(j + 1) * 512])
                link(ins)
                link(dve.bn_aggr(mv[:, t, :], bn[:, t % 2]))
                dve.tensor_scalar(rs[:, t, 0:1], mv[:, t, 1:2], EPS, None, ALU.add).then_inc(s["var2"], 1)
                dve.wait_ge(s["root2"], t + 1)
                link(dve.reciprocal(rs[:, t, 0:1], rs[:, t, 1:2]))
                dve.tensor_scalar(x1[:, t], x1[:, t], mv[:, t, 0:1], rs[:, t, 0:1], ALU.subtract, ALU.mult
                                  ).then_inc(s["norm2"], 1)


SEMS = """const_in crow_in crow_read c_in c_sig c_silu bada_in x_in gq_in cT_acc cT_ready cw_ready ada_acc ada_out
ssT_acc xT_acc uT_out proj_acc proj_out pad_ready conv_done conv_sig ss_ready ss_root C_in out1 tail_ready
tail_acc m_ready C_new nT_ready n_in m0_in row_a act_row cols_acc cols_exp pre_acc W_ready D_ready num_acc
nd_ready tmp_ready var_ready rs_root gate_acc n_acc rows_done kw_ready C_zero n_cols nT_acc wu_in krc_zero
yz_ready yz_out prep_out prep_acc q_rot at_exp at_S at_T at_PT at_out at_O at_max new_in d_O ql_out ql_acc
tr_out tr_acc d_exp d_S p_out p_acc ol_ready ol_T ol_out datt_acc d_max wo_in G_out G_acc st_out x1_ready
u2_ready x2_in rw_in mT_acc mT_out wo_acc wo_read var1 root1 uT2_acc uT2_out lg_acc lg_read top_neg ex_ready
hot_ready hot_acc sc2_ready mask_ready pos_acc down_in y_acc idx_in idx_seen xg_in turned turn_out y_ready
y_out y_stored bias_in glu_ready sig_ready hid_ready up_acc glu_sum lin_ready glu_gated f_in fin_ready fin_out
yg_read var2 root2 f0 res2 norm2""".split()

INPUTS = ("x_prompt x_sample c_prompt c_sample cache_ckv cache_kr state_C state_n state_m state_conv w_ada b_ada "
          "w_in b_if conv_w conv_b q_norm_g w_uq kv_norm_g w_uk w_uv ml_norm_g w_o ln1_g ln1_b router_w router_b "
          "w_up b_up w_down b_down ln2_g ln2_b").split()
OUTPUTS = {
    "y_prompt": (1, SEQ, D), "y_sample": (DEC_B, DEC_T, D),
    "new_ckv_p": (1, 1, SEQ, KV_LORA), "new_kr_p": (1, 1, SEQ, ROPE),
    "new_C_p": (1, 1, MH, MD, MD), "new_n_p": (1, 1, MH, MD), "new_m_p": (1, 1, MH), "new_conv_p": (1, 1, 3, 2 * MW),
    "new_ckv_s": (1, DEC_B, DEC_T, KV_LORA), "new_kr_s": (1, DEC_B, DEC_T, ROPE),
    "new_C_s": (1, DEC_B, MH, MD, MD), "new_n_s": (1, DEC_B, MH, MD), "new_m_s": (1, DEC_B, MH),
    "new_conv_s": (1, DEC_B, 3, 2 * MW),
}


def build(nc, I, O):
    from contextlib import ExitStack
    with ExitStack() as ctx:
        s = {n: ctx.enter_context(nc.semaphore(n)) for n in SEMS}
        s["ring_in"] = [ctx.enter_context(nc.semaphore("ring_in%d" % i)) for i in range(3)]
        s["cache_in"] = [ctx.enter_context(nc.semaphore("cache_in%d" % i)) for i in range(2)]
        s["up_in"] = [[ctx.enter_context(nc.semaphore("up_in%d%d" % (i, j))) for j in range(2)] for i in range(2)]
        s["up_read"] = [ctx.enter_context(nc.semaphore("up_read%d" % i)) for i in range(2)]
        s["yg_in"] = [ctx.enter_context(nc.semaphore("yg_in%d" % i)) for i in range(2)]
        s["x1_out"] = [ctx.enter_context(nc.semaphore("x1_out%d" % i)) for i in range(2)]
        s["u2_out"] = [ctx.enter_context(nc.semaphore("u2_out%d" % i)) for i in range(2)]
        s["dve"] = Chain(ctx.enter_context(nc.semaphore("dve_step")))
        s["pool"] = Chain(ctx.enter_context(nc.semaphore("pool_step")))
        v = make_views(nc, ctx)
        v.psum = ctx.enter_context(nc.psum_tensor("psum", [P, 8, 512], F32))
        S = [v.psum[:, i, :] for i in range(8)]
        v.d_x1 = nc.dram_tensor("d_x1", (TOK, D), F32, kind="Internal").ap()
        v.d_u2 = nc.dram_tensor("d_u2", (TOK, D), F32, kind="Internal").ap()
        v.d_gate = nc.dram_tensor("d_gate", (P, 2, D), F32, kind="Internal").ap()
        v.d_y = nc.dram_tensor("d_y", (MAX_BLOCKS * P, D), F32, kind="Internal").ap()
        stage_project(nc, I, O, v, s, S)
        stage_mlstm(nc, I, O, v, s, S)
        stage_prompt_attention(nc, I, O, v, s, S)
        stage_decode_attention(nc, I, O, v, s, S)
        stage_output_router(nc, I, O, v, s, S)
        stage_experts(nc, I, O, v, s, S)
        stage_combine(nc, I, O, v, s, S)


def kernel(**inputs):
    import concourse.bacc as bacc
    from concourse.bass_utils import run_bass_kernel_spmd

    nc = bacc.Bacc("TRN2", target_bir_lowering=False, num_devices=1)
    arrays = {"in_" + n: np.ascontiguousarray(inputs[n]) for n in INPUTS}
    arrays["in_const"], arrays["in_rows"] = const_tables()
    I = {n[3:]: nc.dram_tensor(n, a.shape, F32, kind="ExternalInput").ap()
                           for n, a in arrays.items()}
    O = {n: nc.dram_tensor("out_" + n, shape, F32, kind="ExternalOutput").ap()
                           for n, shape in OUTPUTS.items()}
    build(nc, I, O)
    r = run_bass_kernel_spmd(nc, [arrays], core_ids=[0])
    return tuple(r.results[0]["out_" + n] for n in OUTPUTS)
```

```python
import numpy as np

import concourse.bass as bass
from concourse import mybir

F32 = mybir.dt.float32
I32 = mybir.dt.int32
U32 = mybir.dt.uint32
ALU = mybir.AluOpType
ACT = mybir.ActivationFunctionType
AX = mybir.AxisListType

P = 128
D = 1024
KD = D // P
SEQ = 512
DEC_B, DEC_T = 8, 16
PAST = 1024
NT = (SEQ + DEC_B * DEC_T) // P
NP_T = SEQ // P
TOK = NT * P
H, NOPE, ROPE, VD = 8, 64, 32, 64
QK = NOPE + ROPE
Q_LORA, KV_LORA = 384, 256
MH, MD = 4, 128
MW = MH * MD
IN_COLS = Q_LORA + KV_LORA + ROPE + 4 * MW + 2 * MH
ZC = Q_LORA + KV_LORA + ROPE
NE, TOPK, FF = 32, 4, 1024
ATTN_SCALE = float((NOPE + ROPE) ** -0.5)
ALPHA = float(2.0 ** 0.25)
EPS = 1e-5
LIMIT, SW_ALPHA = 7.0, 1.702
NEG = -1e30
CB = 3
MAX_BLOCKS = NE + TOK * TOPK // P

C_ID, C_TRI, C_ONE, C_NEGP, C_NEGS, C_NEGA = (i * P for i in range(6))
C_BIND = 6 * P
C_IOTA = C_BIND + DEC_B
C_ROPE = C_IOTA + P
C_TOK = C_ROPE + NT * ROPE
NCONST = C_TOK + NT
R_SEL4, R_RESET, R_SELC = 0, MH * P, MH * P + TOK
NROWS = R_SELC + 2 * P


def const_tables():
    c = np.zeros((P, NCONST), np.float32)
    p = np.arange(P)
    c[:, C_ID:C_ID + P] = np.eye(P)
    c[:, C_TRI:C_TRI + P] = p[:, None] < p[None, :]
    c[:, C_ONE:C_ONE + P] = 1.0
    c[:, C_NEGP:C_NEGP + P] = np.where(p[:, None] > p[None, :], NEG, 0)
    same = p[:, None] // DEC_T == p[None, :] // DEC_T
    c[:, C_NEGS:C_NEGS + P] = np.where(same & (p[:, None] <= p[None, :]), 0, NEG)
    c[:, C_NEGA:C_NEGA + P] = np.where((p[:, None] < 64) & (p[None, :] >= 64), NEG, 0)
    c[:, C_BIND:C_BIND + DEC_B] = p[:, None] // DEC_T == np.arange(DEC_B)
    c[:, C_IOTA:C_IOTA + P] = np.arange(P)
    half = ROPE // 2
    inv = np.float32(10000.0) ** (-np.arange(half, dtype=np.float32) / np.float32(half))
    for t in range(NT):
        pos = (t * P + p if t < NP_T else PAST + p % DEC_T).astype(np.float32)
        ang = pos[:, None] * inv
        c[:, C_ROPE + t * ROPE:C_ROPE + t * ROPE + half] = np.cos(ang)
        c[:, C_ROPE + t * ROPE + half:C_ROPE + (t + 1) * ROPE] = np.sin(ang)
        c[:, C_TOK + t] = t * P + p
    r = np.zeros((1 + DEC_B, NROWS), np.float32)
    for h in range(MH):
        r[h, R_SEL4 + h * P:R_SEL4 + (h + 1) * P] = 1.0
    tok = np.arange(TOK)
    r[:, R_RESET:R_RESET + TOK] = np.where(tok < SEQ, tok % P != 0, tok % DEC_T != 0)
    r[0, R_SELC:R_SELC + P] = 1.0
    for b in range(DEC_B):
        r[1 + b, R_SELC + P + b * DEC_T:R_SELC + P + (b + 1) * DEC_T] = 1.0
    return c, r


class Views:
    pass


class Chain:

    def __init__(self, sem):
        self.sem, self.n = sem, 0

    def __call__(self, eng, ins):
        ins.then_inc(self.sem, 1)
        self.n += 1
        eng.wait_ge(self.sem, self.n)


def spread_rows(eng, dst, v, part, n, sem):
    src = v.d_e9[:, part * D:(part + n) * D]
    eng.dma_start(dst[:, :, 0, :], bcast_rows(src[0].rearrange("(g n) -> g n", g=n), P)).then_inc(sem, 16)
    for b in range(DEC_B):
        eng.dma_start(dst[b * DEC_T:(b + 1) * DEC_T, :, 1, :],
                      bcast_rows(src[1 + b].rearrange("(g n) -> g n", g=n), DEC_T)).then_inc(sem, 16)


def bcast_rows(ap, n):
    return ap.partition_broadcast(n)


def make_views(nc, ctx):
    v = Views()
    arena = ctx.enter_context(nc.sbuf_tensor("arena", [P, 53100], F32))

    def cut(off, *dims):
        n = int(np.prod(dims))
        assert off + n <= 53100, (off, n)
        ap = arena[:, off:off + n]
        if len(dims) == 1:
            return ap
        names = "abcd"[:len(dims)]
        return ap.rearrange("p (%s) -> p %s" % (" ".join(names), " ".join(names)),
                            **{k: d for k, d in zip(names, dims)})
    v.cut = cut
    v.const = cut(0, NCONST)
    v.rows = cut(NCONST, NROWS)
    assert NCONST + NROWS <= 3000
    v.ident = v.const[:, C_ID:C_ID + P]
    v.ones = v.const[:, C_ONE:C_ONE + P]
    v.e9 = cut(3000, 6 * D)
    v.z = cut(9144, NT, ZC)
    v.so = cut(12504, NT, MW)
    v.qk = cut(15064, 8, TOK)
    v.va = cut(20184, NT, MH, MD + 1)
    v.mix = cut(22764, NT, D)
    v.wuq = cut(48492, 3, H * QK)
    v.wuk = cut(50796, 2, H * NOPE)
    v.wuv = cut(51820, 2, H * VD)
    v.row = cut(22764, 8, TOK)
    v.seg = cut(52844, 4, 4 + DEC_B)
    v.gates = cut(52900, NT, 2 * MH)
    return v


IG, LF, T1, T2, FC, M, A, B = range(8)
NM, Q2, IG2, Q3 = T1, T2, T2, LF
Pm, Sm = slice(0, SEQ), slice(SEQ, TOK)


def bat(ap):
    return ap.rearrange("p (b t) -> p b t", b=DEC_B)


def til(ap):
    return ap.rearrange("p (b t) -> p b t", b=NP_T)


def stage_project(nc, I, O, v, s, S):
    x = v.cut(22764, NT, D)
    uT = v.cut(27884, KD, TOK)
    RING = 3
    ring = v.cut(33004, RING, KD, 512)
    xpP = v.cut(45292, 8, SEQ + 3)
    xpS = v.cut(45292 + 8 * (SEQ + 3), 8, DEC_B, DEC_T + 3)
    c9 = v.cut(45292, 2, D)
    m0 = 45292 + 8 * 667
    scT = v.cut(m0, KD, 9)
    ssT = v.cut(m0 + 72, 2, KD, 9)
    cw = v.cut(m0 + 216, KD, 29)
    gq = v.cut(m0 + 448, Q_LORA + KV_LORA)
    bif = v.cut(m0 + 1088, 2 * MH)
    ss = v.cut(m0 + 1096, 4, 2 * NT)
    rt = v.cut(m0 + 1136, 4, NT, ROPE // 2)
    tail = v.tail = v.cut(m0 + 1456, KD, 27)
    assert m0 + 1456 + 216 <= 52900
    crow = ring[:, 2, 0:2, :].rearrange("p a b -> p (a b)")

    wada = I["w_ada"][0].rearrange("(k p) n -> p k n", p=P)
    win = I["w_in"][0].rearrange("(k p) n -> p k n", p=P)
    cut_in = [("q", ZC, 512), ("k", ZC + MW, 512), ("za", 0, 512), ("zb", 512, ZC - 512),
              ("g", IN_COLS - 2 * MH, 2 * MH), ("v", ZC + 2 * MW, 512), ("o", ZC + 3 * MW, 512)]
    stream = [(wada[:, :, n * 512:(n + 1) * 512], 512, "ada%d" % n) for n in range(12)]
    stream += [(win[:, :, a:a + n], n, k) for k, a, n in cut_in]
    accs, last_acc = [], {}
    for i, (kind, a, n) in enumerate(cut_in):
        if kind in "qk":
            accs += [(kind, 12 + i, ct, part) for ct in range(4) for part in ((0, 512), (512, TOK))]
        else:
            accs += [(kind, 12 + i, t, (0, n)) for t in range(NT)]
        last_acc[12 + i] = len(accs)
    NB = 4

    def out_count(kind, tile):
        return 1 + max(i for i, a in enumerate(accs) if a[0] == kind and a[2] == tile)

    def r(i, sl=slice(0, TOK)):
        return v.row[0:4, i, sl]

    def seg12(i, sl=slice(0, 4 + DEC_B)):
        return v.seg[0:4, i, sl]

    with nc.Block() as block:
        @block.sync
        def _(sp):
            sp.dma_start(v.const, I["const"]).then_inc(s["const_in"], 16)
            sp.dma_start(v.rows[0:9, :], I["rows"]).then_inc(s["const_in"], 16)
            for i, (src, n, _) in enumerate(stream):
                if i == 1:
                    sp.wait_ge(s["crow_in"], 48)
                if i == 2:
                    sp.wait_ge(s["crow_read"], 1)
                if RING <= i < 12 + RING:
                    sp.wait_ge(s["ada_acc"], i - RING + 1)
                if i >= 12 + RING:
                    sp.wait_ge(s["proj_acc"], last_acc[i - RING])
                sp.dma_start(ring[:, i % RING, :, 0:n], src).then_inc(s["ring_in"][i % RING], 16)

        @block.scalar
        def _(act):
            act.dma_start(c9[0:1, 0, :], I["c_prompt"]).then_inc(s["c_in"], 16)
            act.dma_start(c9[1:9, 0, :], I["c_sample"]).then_inc(s["c_in"], 16)
            act.dma_start(v.e9[0:9, :], bcast_rows(I["b_ada"][0], 9)).then_inc(s["bada_in"], 16)
            act.dma_start(crow[0:4, :], I["conv_w"][0]).then_inc(s["crow_in"], 16)
            act.dma_start(crow[4:5, :], I["conv_b"]).then_inc(s["crow_in"], 16)
            act.dma_start(crow[5:29, :], I["state_conv"][0].rearrange("b j n -> (b j) n")).then_inc(s["crow_in"], 16)
            act.wait_ge(s["c_in"], 32)
            act.activation(c9[0:9, 1, :], c9[0:9, 0, :], ACT.Sigmoid).then_inc(s["c_sig"], 1)
            act.wait_ge(s["ring_in"][1], 16)
            for t in range(NP_T):
                act.dma_start(x[:, t, :], I["x_prompt"][0, t * P:(t + 1) * P, :]).then_inc(s["x_in"], 16)
            act.dma_start(x[:, NP_T, :], I["x_sample"].rearrange("b t d -> (b t) d")).then_inc(s["x_in"], 16)
            act.dma_start(gq[:, 0:Q_LORA], bcast_rows(I["q_norm_g"][0], P)).then_inc(s["gq_in"], 16)
            act.dma_start(gq[:, Q_LORA:], bcast_rows(I["kv_norm_g"][0], P)).then_inc(s["gq_in"], 16)
            act.dma_start(bif, bcast_rows(I["b_if"][0], P)).then_inc(s["gq_in"], 16)
            act.dma_start(v.seg[0:4, 0, 4:12], I["state_m"][0].rearrange("b h -> h b"),
                          allow_slow_non_contiguous=True).then_inc(s["m0_in"], 16)

            def evac(i):
                kind, _, t, (a, b) = accs[i]
                act.wait_ge(s["proj_acc"], i + 1)
                ps = S[1 + i % NB]
                if kind in "qk":
                    ct = t + (4 if kind == "k" else 0)
                    if i == 0:
                        act.wait_ge(s["pad_ready"], 2)
                    if a == 0:
                        dst, src = xpP[:, ct, 3:3 + SEQ], ps[:, 0:512]
                    else:
                        dst = xpS[:, ct, :, 3:3 + DEC_T]
                        src = ps[:, 0:P].rearrange("p (b t) -> p b t", b=DEC_B)
                elif kind == "za":
                    dst, src = v.z[:, t, 0:512], ps[:, 0:512]
                elif kind == "zb":
                    dst, src = v.z[:, t, 512:ZC], ps[:, 0:ZC - 512]
                elif kind == "g":
                    dst, src = v.gates[:, t, :], ps[:, 0:2 * MH]
                elif kind == "v":
                    dst = v.va[:, t, :, 0:MD]
                    src = ps[:, 0:MW].rearrange("p (h e) -> p h e", h=MH)
                else:
                    dst, src = v.so[:, t, :], ps[:, 0:MW]
                act.activation(dst, src, ACT.Sigmoid if kind == "o" else ACT.Copy).then_inc(s["proj_out"], 1)

            def sigmoids(cts):
                for ct in cts:
                    act.wait_ge(s["conv_done"], ct + 1)
                    act.activation(xpP[:, ct, 0:SEQ], v.qk[:, ct, 0:SEQ], ACT.Sigmoid).then_inc(s["conv_sig"], 1)
                    act.activation(xpS[:, ct, :, 0:DEC_T],
                                   v.qk[:, ct, SEQ:].rearrange("p (b t) -> p b t", b=DEC_B),
                                   ACT.Sigmoid).then_inc(s["conv_sig"], 1)

            n_g = last_acc[12 + 4]
            for i in range(n_g):
                evac(i)
            sigmoids(range(8))
            for i in range(n_g, len(accs)):
                if i == n_g + 3:
                    act.wait_ge(s["row_a"], 1)
                    act.activation(r(T1), r(T2), ACT.Exp, scale=-1.0).then_inc(s["act_row"], 1)
                    act.wait_ge(s["act_row"], 1)
                    act.activation(r(T1), r(T1), ACT.Ln, bias=v.ones[0:4, 0:1]).then_inc(s["act_row"], 1)
                if i == len(accs) - NT:
                    act.wait_ge(s["ss_ready"], 1)
                    act.activation(ss[:, 2, :], ss[:, 1, :], ACT.Sqrt).then_inc(s["ss_root"], 1)
                evac(i)

        @block.tensor
        def _(pe):
            pe.wait_ge(s["const_in"], 32)
            pe.wait_ge(s["c_silu"], 1)
            for k in range(KD):
                ins = pe.transpose(S[0][:, k * 9:(k + 1) * 9], c9[0:9, 0, k * P:(k + 1) * P],
                                   v.ident[0:9, 0:9])
            ins.then_inc(s["cT_acc"], 1)
            pe.wait_ge(s["crow_in"], 48)
            for k in range(KD):
                ins = pe.transpose(S[7][:, k * 29:(k + 1) * 29], crow[0:29, k * P:(k + 1) * P],
                                   v.ident[0:29, 0:29])
            ins.then_inc(s["crow_read"], 1)
            pe.wait_ge(s["cT_ready"], 1)

            def ada(n):
                pe.wait_ge(s["ring_in"][n % RING], 16 * (n // RING + 1))
                if n >= NB:
                    pe.wait_ge(s["ada_out"], n - NB + 1)
                for k in range(KD):
                    ins = pe.matmul(S[1 + n % NB][0:9, :], scT[:, k, :], ring[:, n % RING, k, :],
                                    start=(k == 0), stop=(k == KD - 1))
                ins.then_inc(s["ada_acc"], 1)

            for n in range(5):
                ada(n)
            pe.wait_ge(s["ada_out"], 4)
            for j in range(16):
                ins = pe.transpose(S[0][:, 128 + j * 9:137 + j * 9], v.e9[0:9, j * P:(j + 1) * P],
                                   v.ident[0:9, 0:9])
            ins.then_inc(s["ssT_acc"], 1)
            pe.wait_ge(s["x_in"], 16 * NT)
            for k in range(KD):
                if k >= 2:
                    pe.wait_ge(s["uT_out"], k - 1)
                for t in range(NP_T):
                    ins = pe.transpose(S[5 + k % 2][:, t * P:(t + 1) * P], x[:, t, k * P:(k + 1) * P], v.ident)
                ins.then_inc(s["xT_acc"], 1)
            for g in range(2):
                pe.wait_ge(s["cw_ready"], 1) if g == 0 else pe.wait_ge(s["uT_out"], KD - 1)
                for k in range(4):
                    ins = pe.transpose(S[7 - 2 * g][:, k * P:(k + 1) * P],
                                       x[:, NP_T, (4 * g + k) * P:(4 * g + k + 1) * P], v.ident)
                ins.then_inc(s["xT_acc"], 1)
            for n in range(5, 12):
                ada(n)
            pe.wait_ge(s["uT_out"], KD + 2)
            pe.wait_ge(s["ada_out"], 12)
            for i, (kind, piece, t, (a, b)) in enumerate(accs):
                slot = piece % RING
                if i == last_acc[12 + 4] + 2:
                    pe.wait_ge(s["gates_ready"], 1)
                    for j in range(2):
                        for tt in range(NT):
                            bank, c = (5 + j, tt * P) if tt < NP_T else (7, j * P)
                            ins = pe.transpose(S[bank][0:4, c:c + P], v.gates[:, tt, 4 * j:4 * j + 4], v.ident)
                    ins.then_inc(s["gate_acc"], 1)
                pe.wait_ge(s["ring_in"][slot], 16 * (piece // RING + 1))
                if i >= NB:
                    pe.wait_ge(s["proj_out"], i - NB + 1)
                ps = S[1 + i % NB]
                for k in range(KD):
                    if kind in "qk":
                        ins = pe.matmul(ps[:, 0:b - a], ring[:, slot, k, t * P:(t + 1) * P], uT[:, k, a:b],
                                        start=(k == 0), stop=(k == KD - 1))
                    else:
                        ins = pe.matmul(ps[:, 0:b], uT[:, k, t * P:(t + 1) * P], ring[:, slot, k, 0:b],
                                        start=(k == 0), stop=(k == KD - 1))
                ins.then_inc(s["proj_acc"], 1)

        @block.vector
        def _(dve):
            link = lambda ins: s["dve"](dve, ins)
            dve.memset(v.va[:, :, :, MD:MD + 1], 1.0)
            dve.wait_ge(s["c_sig"], 1)
            dve.tensor_tensor(c9[0:9, 0, :], c9[0:9, 0, :], c9[0:9, 1, :], ALU.mult).then_inc(s["c_silu"], 1)
            dve.wait_ge(s["cT_acc"], 1)
            dve.tensor_copy(scT, S[0][:, 0:KD * 9].rearrange("p (k n) -> p k n", k=KD)).then_inc(s["cT_ready"], 1)
            dve.wait_ge(s["crow_read"], 1)
            dve.tensor_copy(cw, S[7][:, 0:KD * 29].rearrange("p (k n) -> p k n", k=KD)).then_inc(s["cw_ready"], 1)
            dve.memset(xpP[:, :, 0:3], 0.0).then_inc(s["pad_ready"], 1)
            dve.wait_ge(s["cw_ready"], 1)
            dve.tensor_copy(xpS[:, :, :, 0:3], cw[:, :, 5:29].rearrange("p k (b j) -> p k b j", j=3)
                            ).then_inc(s["pad_ready"], 1)
            dve.wait_ge(s["bada_in"], 16)

            def ada_out(n):
                dve.wait_ge(s["ada_acc"], n + 1)
                e = v.e9[0:9, n * 512:(n + 1) * 512]
                dve.tensor_tensor(e, S[1 + n % NB][0:9, :], e, ALU.add).then_inc(s["ada_out"], 1)

            for n in range(4):
                ada_out(n)
            dve.wait_ge(s["ssT_acc"], 1)
            link(dve.tensor_copy(ssT[:, 0], S[0][:, 128:200].rearrange("p (k n) -> p k n", k=KD)))
            link(dve.tensor_scalar(ssT[:, 1], S[0][:, 200:272].rearrange("p (k n) -> p k n", k=KD),
                                   1.0, None, ALU.add))
            ada_out(4)
            for k in range(KD):
                dve.wait_ge(s["xT_acc"], k + 1)
                dve.tensor_scalar(uT[:, k, 0:SEQ], S[5 + k % 2][:, :], ssT[:, 1, k, 0:1], ssT[:, 0, k, 0:1],
                                  ALU.mult, ALU.add).then_inc(s["uT_out"], 1)
            for g in range(2):
                dve.wait_ge(s["xT_acc"], KD + 1 + g)
                dst = uT[:, 4 * g:4 * g + 4, SEQ:].rearrange("p k (b t) -> p k b t", b=DEC_B)

                def per_batch(j):
                    return ssT[:, j, 4 * g:4 * g + 4, 1:9].unsqueeze(3).to_broadcast([P, 4, DEC_B, DEC_T])

                link(dve.tensor_tensor(dst, S[7 - 2 * g][:, :].rearrange("p (k b t) -> p k b t", k=4, b=DEC_B),
                                       per_batch(1), ALU.mult))
                dve.tensor_tensor(dst, dst, per_batch(0), ALU.add).then_inc(s["uT_out"], 1)
            for n in range(5, 12):
                ada_out(n)

            for ct in range(8):
                kind = "q" if ct < 4 else "k"
                dve.wait_ge(s["proj_out"], out_count(kind, ct % 4))
                accP, accS = v.qk[:, ct, 0:SEQ], v.qk[:, ct, SEQ:].rearrange("p (b t) -> p b t", b=DEC_B)
                dve.tensor_scalar(accP, xpP[:, ct, 0:SEQ], cw[:, ct, 0:1], cw[:, ct, 4:5], ALU.mult, ALU.add)
                link(dve.tensor_scalar(accS, xpS[:, ct, :, 0:DEC_T], cw[:, ct, 0:1], cw[:, ct, 4:5],
                                       ALU.mult, ALU.add))
                for j in range(1, 4):
                    dve.scalar_tensor_tensor(accP, xpP[:, ct, j:j + SEQ], cw[:, ct, j:j + 1], accP,
                                             ALU.mult, ALU.add)
                    ins = dve.scalar_tensor_tensor(accS, xpS[:, ct, :, j:j + DEC_T], cw[:, ct, j:j + 1], accS,
                                                   ALU.mult, ALU.add)
                    link(ins)
                dve.tensor_copy(tail[:, ct, 0:3], xpP[:, ct, SEQ:SEQ + 3])
                dve.tensor_copy(tail[:, ct, 3:27].rearrange("p (b j) -> p b j", j=3),
                                xpS[:, ct, :, DEC_T:DEC_T + 3]).then_inc(s["conv_done"], 1)
            sq = x[:, 0, 0:Q_LORA]
            for t in range(NT):
                dve.wait_ge(s["proj_out"], out_count("zb", t))
                link(dve.tensor_tensor_reduce(sq, v.z[:, t, 0:Q_LORA], v.z[:, t, 0:Q_LORA], 1.0, 0.0,
                                              ALU.mult, ALU.add, ss[:, 0, t:t + 1]))
                link(dve.tensor_tensor_reduce(sq[:, 0:KV_LORA], v.z[:, t, Q_LORA:Q_LORA + KV_LORA],
                                              v.z[:, t, Q_LORA:Q_LORA + KV_LORA], 1.0, 0.0,
                                              ALU.mult, ALU.add, ss[:, 0, NT + t:NT + t + 1]))
            link(dve.tensor_scalar(ss[:, 1, 0:NT], ss[:, 0, 0:NT], 1.0 / Q_LORA, EPS, ALU.mult, ALU.add))
            dve.tensor_scalar(ss[:, 1, NT:], ss[:, 0, NT:], 1.0 / KV_LORA, EPS, ALU.mult, ALU.add
                              ).then_inc(s["ss_ready"], 1)
            tab = v.const[:, C_ROPE:C_ROPE + NT * ROPE].rearrange("p (t n) -> p t n", t=NT)
            cos, sin = tab[:, :, 0:16], tab[:, :, 16:32]
            x1, x2 = v.z[:, :, ZC - 32:ZC - 16], v.z[:, :, ZC - 16:ZC]
            dve.tensor_tensor(rt[:, 0], x1, cos, ALU.mult)
            dve.tensor_tensor(rt[:, 1], x2, sin, ALU.mult)
            dve.tensor_tensor(rt[:, 2], x1, sin, ALU.mult)
            link(dve.tensor_tensor(rt[:, 3], x2, cos, ALU.mult))
            dve.tensor_tensor(x1, rt[:, 0], rt[:, 1], ALU.subtract)
            dve.tensor_tensor(x2, rt[:, 2], rt[:, 3], ALU.add)
            for ct in range(8):
                dve.wait_ge(s["conv_sig"], 2 * ct + 2)
                sc = 1.0 if ct < 4 else float(MD ** -0.5)
                dve.scalar_tensor_tensor(v.qk[:, ct, 0:SEQ], v.qk[:, ct, 0:SEQ], sc, xpP[:, ct, 0:SEQ],
                                         ALU.mult, ALU.mult)
                accS = v.qk[:, ct, SEQ:].rearrange("p (b t) -> p b t", b=DEC_B)
                link(dve.scalar_tensor_tensor(accS, accS, sc, xpS[:, ct, :, 0:DEC_T], ALU.mult, ALU.mult))
            dve.wait_ge(s["gq_in"], 48)
            dve.wait_ge(s["proj_out"], out_count("g", NT - 1))
            dve.tensor_tensor(v.gates, v.gates, bif.unsqueeze(1).to_broadcast([P, NT, 2 * MH]), ALU.add
                              ).then_inc(s["gates_ready"], 1)
            dve.memset(seg12(0, slice(0, 1)), 0.0)
            dve.wait_ge(s["gate_acc"], 1)
            for j, dst in ((0, IG), (1, LF)):
                dve.tensor_copy(r(dst, Pm), S[5 + j][0:4, :])
                link(dve.tensor_copy(r(dst, Sm), S[7][0:4, j * P:(j + 1) * P]))
            dve.scalar_tensor_tensor(r(T2), r(LF), -1.0, r(LF), ALU.mult, ALU.max).then_inc(s["row_a"], 1)
            dve.wait_ge(s["act_row"], 2)
            link(dve.scalar_tensor_tensor(r(LF), r(LF), 0.0, r(T1), ALU.min, ALU.subtract))
            link(dve.tensor_tensor_scan(r(FC), v.rows[0:4, R_RESET:R_RESET + TOK], r(LF), 0.0, ALU.mult, ALU.add))
            link(dve.tensor_tensor_scan(r(M, Pm), r(LF, Pm), r(IG, Pm), 0.0, ALU.add, ALU.max))
            dve.tensor_copy(r(IG2, Sm), r(IG, Sm))
            link(dve.tensor_copy(r(T1, Sm), r(LF, Sm)))
            first, firstI = bat(r(T1, Sm))[:, :, 0:1], bat(r(IG2, Sm))[:, :, 0:1]
            dve.wait_ge(s["m0_in"], 16)
            m0c = seg12(0, slice(4, 12)).unsqueeze(2)
            link(dve.tensor_tensor(first, first, m0c, ALU.add))
            link(dve.tensor_tensor(firstI, firstI, first, ALU.max))
            link(dve.memset(first, NEG))
            link(dve.tensor_tensor_scan(r(M, Sm), r(T1, Sm), r(IG2, Sm), 0.0, ALU.add, ALU.max))
            dve.tensor_tensor(r(A), r(FC), r(M), ALU.subtract)
            dve.tensor_tensor(r(B), r(IG), r(FC), ALU.subtract)
            dve.tensor_scalar(r(NM), r(M), -1.0, None, ALU.mult)
            dve.tensor_copy(seg12(0, slice(1, 4)).unsqueeze(2), til(r(M, Pm))[:, 0:3, P - 1:P])
            link(dve.tensor_copy(seg12(3, slice(4, 12)).unsqueeze(2), bat(r(M, Sm))[:, :, DEC_T - 1:DEC_T]))
            dve.tensor_copy(seg12(1, slice(0, 4)).unsqueeze(2), til(r(A, Pm))[:, :, P - 1:P])
            link(dve.tensor_copy(seg12(1, slice(4, 12)).unsqueeze(2), bat(r(A, Sm))[:, :, DEC_T - 1:DEC_T]))
            dve.tensor_tensor(seg12(2), seg12(0), seg12(1), ALU.add).then_inc(s["m_ready"], 1)
            for i, src, dst in ((0, A, Q2), (1, B, Q3)):
                dve.tensor_tensor(til(r(dst, Pm)), til(r(src, Pm)),
                                  seg12(i, slice(0, 4)).unsqueeze(2).to_broadcast([4, NP_T, P]), ALU.add)
                ins = dve.tensor_tensor(bat(r(dst, Sm)), bat(r(src, Sm)),
                                        seg12(i, slice(4, 12)).unsqueeze(2).to_broadcast([4, DEC_B, DEC_T]), ALU.add)
            ins.then_inc(s["rows_done"], 1)
            dve.wait_ge(s["ss_root"], 1)
            link(dve.reciprocal(ss[:, 3, :], ss[:, 2, :]))
            for t in range(NT):
                zq, zk = v.z[:, t, 0:Q_LORA], v.z[:, t, Q_LORA:Q_LORA + KV_LORA]
                dve.scalar_tensor_tensor(zq, zq, ss[:, 3, t:t + 1], gq[:, 0:Q_LORA], ALU.mult, ALU.mult)
                dve.scalar_tensor_tensor(zk, zk, ss[:, 3, NT + t:NT + t + 1], gq[:, Q_LORA:], ALU.mult,
                                         ALU.mult)


def stage_mlstm(nc, I, O, v, s, S):
    W0 = 27884
    C = v.cut(W0, 36, MD + 1)
    QM0 = W0 + 36 * (MD + 1)
    VM0 = QM0 + 2 * DEC_B * (P + DEC_T)
    row, seg = v.row, v.seg
    o = 40256
    assert VM0 + 2 * DEC_B * (MD + 1) <= o
    colv = v.cut(o, NT, 4, MH)
    o += NT * 16
    dec = v.cut(o, MH, 4 + DEC_B)
    o += 48
    Dx = v.cut(o, 2, P)
    Wt = v.cut(o + 256, 2, P)
    kw = v.cut(o + 512, 2, P)
    nd = v.cut(o + 768, 2, MD + 1)
    tmp = v.cut(o + 1026, 2, MD + 1)
    o += 1284
    qm = v.cut(QM0, 2, DEC_B, P + DEC_T)
    vm = v.cut(VM0, 2, DEC_B, MD + 1)
    o = 43724
    h = v.cut(o, NT * MH, MD)
    o += NT * MH * MD
    st = v.cut(o, NT * MH, 6)
    mv = v.cut(o + 120, NT * MH, 2)
    rs = v.cut(o + 160, 2, NT * MH)
    dn = v.cut(o + 200, NT * MH, 2)
    o += 240
    gml = v.cut(o, MW)
    o += MW
    nrow = v.cut(o, 2, MD)
    crow = v.cut(o + 256, D)
    o += 256 + D
    assert o <= 48492
    v.norm = h, st, mv, rs, gml

    def r(i, sl=slice(0, TOK)):
        return row[0:4, i, sl]

    def seg12(i, sl=slice(0, 4 + DEC_B)):
        return seg[0:4, i, sl]

    units = [(t, hh) for t in range(NP_T) for hh in range(MH)] + [(NP_T, hh) for hh in range(MH)]
    NU = len(units)

    with nc.Block() as block:
        @block.sync
        def _(sp):
            for b in range(DEC_B):
                sp.dma_start(C[:, 4 + 4 * b:8 + 4 * b, 0:MD], I["state_C"][0, b].rearrange("h d e -> d h e")
                             ).then_inc(s["C_in"], 16)
            sp.dma_start(v.d_e9, v.e9[0:9, :]).then_inc(s["out1"], 16)
            sp.dma_start(v.wuq, I["w_uq"][0].rearrange("(k p) n -> p k n", p=P)).then_inc(s["wu_in"], 16)
            sp.dma_start(v.wuk, I["w_uk"][0].rearrange("(k p) h n -> p k (h n)", p=P)).then_inc(s["wu_in"], 16)
            sp.wait_ge(s["tail_acc"], 1)
            sp.dma_start(v.wuv, I["w_uv"][0].rearrange("(k p) h n -> p k (h n)", p=P)).then_inc(s["wu_in"], 16)
            sp.dma_start(O["new_ckv_p"][0, 0].rearrange("(t p) n -> p t n", p=P),
                         v.z[:, 0:NP_T, Q_LORA:Q_LORA + KV_LORA]).then_inc(s["out1"], 16)
            sp.dma_start(O["new_ckv_s"][0].rearrange("b t n -> (b t) n"),
                         v.z[:, NP_T, Q_LORA:Q_LORA + KV_LORA]).then_inc(s["out1"], 16)
            sp.dma_start(O["new_kr_p"][0, 0].rearrange("(t p) n -> p t n", p=P),
                         v.z[:, 0:NP_T, ZC - ROPE:ZC]).then_inc(s["out1"], 16)
            sp.dma_start(O["new_kr_s"][0].rearrange("b t n -> (b t) n"), v.z[:, NP_T, ZC - ROPE:ZC]
                         ).then_inc(s["out1"], 16)
            sp.wait_ge(s["tail_ready"], 2)
            sp.dma_start(O["new_conv_p"][0, 0], crow[0:3, :]).then_inc(s["out1"], 16)
            sp.dma_start(O["new_conv_s"][0].rearrange("b j n -> (b j) n"), crow[3:27, :]).then_inc(s["out1"], 16)
            sp.wait_ge(s["m_ready"], 1)
            sp.dma_start(O["new_m_p"][0, 0:1].rearrange("b h -> h b"), row[0:4, M, SEQ - 1:SEQ]).then_inc(s["out1"], 16)
            sp.dma_start(O["new_m_s"][0].rearrange("b h -> h b"), seg[0:4, 3, 4:12],
                         allow_slow_non_contiguous=True).then_inc(s["out1"], 16)
            sp.wait_ge(s["C_new"], MH * NP_T)
            sp.dma_start(O["new_C_p"][0, 0].rearrange("h d e -> d h e"), C[:, 0:4, 0:MD]).then_inc(s["C_out"], 16)
            sp.wait_ge(s["C_new"], MH * NP_T + MH)
            for b in range(DEC_B):
                sp.dma_start(O["new_C_s"][0, b].rearrange("h d e -> d h e"), C[:, 4 + 4 * b:8 + 4 * b, 0:MD]
                             ).then_inc(s["C_out"], 16)
            sp.wait_ge(s["nT_ready"], 1)
            sp.dma_start(O["new_n_p"][0, 0], nrow[0:4, 1, :]).then_inc(s["C_out"], 16)
            sp.dma_start(O["new_n_s"][0].rearrange("b h d -> (b h) d"), nrow[4:36, 1, :]).then_inc(s["C_out"], 16)
            sp.wait_ge(s["out1"], 16 * (1 + 4 + 2 + 2))

        @block.gpsimd
        def _(pool):
            pool.memset(qm, 0.0)
            s["pool"](pool, pool.memset(vm, 0.0))
            for hh in range(MH):
                if hh >= 2:
                    pool.wait_ge(s["num_acc"], MH * NP_T + hh - 1)
                pool.tensor_copy(qm[:, hh % 2, :, 0:DEC_T],
                                 v.qk[:, hh, SEQ:].rearrange("p (b t) -> p b t", b=DEC_B))
                pool.tensor_tensor(vm[:, hh % 2], v.va[:, NP_T, hh, :].unsqueeze(1).to_broadcast([P, DEC_B, MD + 1]),
                                   v.const[:, C_BIND:C_BIND + DEC_B].unsqueeze(2).to_broadcast([P, DEC_B, MD + 1]),
                                   ALU.mult).then_inc(s["masked"], 1)

        @block.scalar
        def _(act):
            act.dma_start(nrow[0:32, 0, :], I["state_n"][0].rearrange("b h d -> (b h) d")).then_inc(s["n_in"], 16)
            act.dma_start(gml, bcast_rows(I["ml_norm_g"][0], P)).then_inc(s["n_in"], 16)
            act.wait_ge(s["cols_acc"], 1)
            act.activation(dec, S[3][:, 0:48].rearrange("p (h n) -> p h n", h=MH), ACT.Exp).then_inc(s["cols_exp"], 1)
            act.activation(colv[:, :, 0, :], S[2][:, 0:80].rearrange("p (t q h) -> p t q h", q=4, h=MH)[:, :, 0],
                           ACT.Copy).then_inc(s["cols_exp"], 1)
            act.activation(colv[:, :, 1:4, :], S[2][:, 0:80].rearrange("p (t q h) -> p t q h", q=4, h=MH)[:, :, 1:4],
                           ACT.Exp).then_inc(s["cols_exp"], 1)
            act.wait_ge(s["cols_exp"], 3)
            for u, (t, hh) in enumerate(units):
                act.wait_ge(s["pre_acc"], u + 1)
                if u >= 2:
                    act.wait_ge(s["W_ready"], u - 1)
                act.activation(Dx[:, u % 2, :], S[u % 2][:, P:2 * P], ACT.Exp,
                               bias=colv[:, t, 0, hh:hh + 1]).then_inc(s["D_ready"], 1)
                act.wait_ge(s["num_acc"], u + 1)
                if u >= 2:
                    act.wait_ge(s["nd_ready"], u - 1)
                act.activation(tmp[:, u % 2, :], S[2 + u % 2][:, 129:258], ACT.Copy,
                               scale=colv[:, t, 1, hh:hh + 1]).then_inc(s["tmp_ready"], 1)

        @block.tensor
        def _(pe):
            for k in range(KD):
                ins = pe.transpose(S[4 + k // 4][0:27, (k % 4) * P:(k % 4 + 1) * P], v.tail[:, k, :], v.ident)
            ins.then_inc(s["tail_acc"], 1)
            pe.wait_ge(s["n_in"], 32)
            pe.transpose(S[6][:, 0:32], nrow[0:32, 0, :], v.ident[0:32, 0:32]).then_inc(s["n_acc"], 1)
            pe.wait_ge(s["rows_done"], 1)
            for hh in range(MH):
                ins = pe.matmul(S[3][:, hh * 12:hh * 12 + 12], v.rows[0:4, R_SEL4 + hh * P:R_SEL4 + (hh + 1) * P],
                                seg12(2), start=True, stop=True)
            for t in range(NT):
                for q, src in enumerate((B, Q2, Q3, NM)):
                    c = (t * 4 + q) * 4
                    ins = pe.transpose(S[2][:, c:c + 4], row[0:4, src, t * P:(t + 1) * P], v.ident[0:4, 0:4])
            ins.then_inc(s["cols_acc"], 1)

            def pre(u):
                t, hh = units[u]
                if u >= 2:
                    pe.wait_ge(s["kw_ready"], u - 1)
                b = S[u % 2]
                pe.matmul(b[:, 0:P], v.qk[:, 4 + hh, t * P:(t + 1) * P], v.qk[:, hh, t * P:(t + 1) * P],
                          start=True, stop=True)
                pe.matmul(b[:, P:2 * P], v.rows[0:4, R_SEL4 + hh * P:R_SEL4 + (hh + 1) * P],
                          r(A, slice(t * P, (t + 1) * P)), start=True, stop=False)
                neg = C_NEGP if t < NP_T else C_NEGS
                pe.matmul(b[:, P:2 * P], v.ident, v.const[:, neg:neg + P], start=False, stop=True)
                pe.transpose(b[:, 2 * P:3 * P], v.qk[:, 4 + hh, t * P:(t + 1) * P], v.ident
                             ).then_inc(s["pre_acc"], 1)

            def products(u):
                t, hh = units[u]
                pe.wait_ge(s["kw_ready"], u + 1)
                if u == 0:
                    pe.wait_ge(s["cols_exp"], 3)
                if u >= 2:
                    pe.wait_ge(s["nd_ready"], u - 1)
                    pe.wait_ge(s["C_new"], u - 1)
                b = S[2 + u % 2]
                pe.matmul(b[:, 0:129], Wt[:, u % 2, :], v.va[:, t, hh, :], start=True, stop=True)
                if t < NP_T:
                    pe.wait_ge(s["C_new"], max(1, u - MH + 1)) if t else pe.wait_ge(s["C_zero"], 1)
                    pe.matmul(b[:, 129:258], v.qk[:, hh, t * P:(t + 1) * P], C[:, hh, :], start=True, stop=True)
                    pe.matmul(b[:, 258:387], kw[:, u % 2, :], v.va[:, t, hh, :], start=True, stop=True
                              ).then_inc(s["num_acc"], 1)
                else:
                    if hh == 0:
                        pe.wait_ge(s["C_in"], 16 * DEC_B)
                    pe.wait_ge(s["masked"], hh + 1)
                    qd = qm[:, hh % 2].rearrange("p b n -> p (b n)")
                    for bb in range(DEC_B):
                        pe.matmul(b[:, 129:258], qd[:, bb * P:(bb + 1) * P], C[:, 4 + 4 * bb + hh, :],
                                  start=(bb == 0), stop=(bb == DEC_B - 1))
                    if hh >= 1:
                        pe.wait_ge(s["C_new"], u)
                    for j, (b0, b1) in enumerate(((0, 3), (3, 6), (6, 8))):
                        ins = pe.matmul(S[4 + j][:, 0:(b1 - b0) * 129], kw[:, u % 2, :], vm[:, hh % 2, b0:b1, :],
                                        start=True, stop=True)
                    ins.then_inc(s["num_acc"], 1)

            pre(0)
            for u in range(NU):
                if u + 1 < NU:
                    pre(u + 1)
                products(u)
            pe.wait_ge(s["n_cols"], 1)
            pe.transpose(S[7][0:36, 0:P], Dx[:, 0, 0:36], v.ident).then_inc(s["nT_acc"], 1)

        @block.vector
        def _(dve):
            link = lambda ins: s["dve"](dve, ins)
            dve.wait_ge(s["tail_acc"], 1)
            dve.tensor_copy(crow[0:27, 0:512], S[4][0:27, :]).then_inc(s["tail_ready"], 1)
            dve.tensor_copy(crow[0:27, 512:], S[5][0:27, :]).then_inc(s["tail_ready"], 1)
            dve.memset(C[:, 0:4, :], 0.0).then_inc(s["C_zero"], 1)
            dve.wait_ge(s["n_acc"], 1)
            link(dve.tensor_copy(C[:, 4:36, MD:MD + 1], S[6][:, 0:32].unsqueeze(2)))
            dve.wait_ge(s["cols_exp"], 3)
            dve.wait_ge(s["C_in"], 16 * DEC_B)

            def weights(u):
                t, hh = units[u]
                dve.wait_ge(s["pre_acc"], u + 1)
                if u >= 2:
                    dve.wait_ge(s["num_acc"], u - 1)
                dve.wait_ge(s["D_ready"], u + 1)
                dve.tensor_tensor(Wt[:, u % 2, :], S[u % 2][:, 0:P], Dx[:, u % 2, :], ALU.mult
                                  ).then_inc(s["W_ready"], 1)
                dve.tensor_scalar(kw[:, u % 2, :], S[u % 2][:, 2 * P:3 * P], colv[:, t, 2, hh:hh + 1], None,
                                  ALU.mult).then_inc(s["kw_ready"], 1)

            def close(u):
                t, hh = units[u]
                dve.wait_ge(s["num_acc"], u + 1)
                dve.wait_ge(s["tmp_ready"], u + 1)
                b = S[2 + u % 2]
                link(dve.tensor_tensor(nd[:, u % 2, :], b[:, 0:129], tmp[:, u % 2, :], ALU.add))
                if t < NP_T:
                    dve.scalar_tensor_tensor(C[:, hh, :], C[:, hh, :], dec[:, hh, t:t + 1], b[:, 258:387],
                                             ALU.mult, ALU.add).then_inc(s["C_new"], 1)
                else:
                    for bb in range(DEC_B):
                        c = C[:, 4 + 4 * bb + hh, :]
                        ins = dve.scalar_tensor_tensor(c, c, dec[:, hh, 4 + bb:5 + bb],
                                                       S[4 + bb // 3][:, (bb % 3) * 129:(bb % 3 + 1) * 129],
                                                       ALU.mult, ALU.add)
                    ins.then_inc(s["C_new"], 1)
                den = nd[:, u % 2, MD:MD + 1]
                d2 = dn[:, 4 * t + hh, :]
                link(dve.scalar_tensor_tensor(d2[:, 0:1], den, -1.0, den, ALU.mult, ALU.max))
                link(dve.tensor_tensor(d2[:, 1:2], d2[:, 0:1], colv[:, t, 3, hh:hh + 1], ALU.max))
                link(dve.reciprocal(d2[:, 0:1], d2[:, 1:2]))
                dve.tensor_scalar(h[:, 4 * t + hh, :], nd[:, u % 2, 0:MD], d2[:, 0:1], None, ALU.mult
                                  ).then_inc(s["nd_ready"], 1)
                dve.wait_ge(s["nd_ready"], u + 1)
                dve.bn_stats(st[:, 4 * t + hh, :], h[:, 4 * t + hh, :])

            weights(0)
            for u in range(NU):
                if u + 1 < NU:
                    weights(u + 1)
                close(u)
            dve.wait_ge(s["D_ready"], NU)
            dve.wait_ge(s["W_ready"], NU)
            dve.wait_ge(s["C_new"], NU)
            dve.tensor_copy(Dx[:, 0, 0:36].unsqueeze(2), C[:, :, MD:MD + 1]).then_inc(s["n_cols"], 1)
            dve.wait_ge(s["nT_acc"], 1)
            dve.tensor_copy(nrow[0:36, 1, :], S[7][0:36, 0:P]).then_inc(s["nT_ready"], 1)


def stage_prompt_attention(nc, I, O, v, s, S):
    v.qT = qT = v.cut(15064, H, TOK)
    wuq, wuk, wuv = v.wuq, v.wuk, v.wuv
    kT = v.cut(27884, H, SEQ)
    vP = v.cut(31980, NP_T, H * VD)
    cqT = v.cut(34028, 3, TOK)
    v.ckT = ckT = v.cut(35948, 2, TOK)
    v.ukT = ukT = v.cut(37228, H, KV_LORA)
    qt = v.cut(39276, 2, H, QK)
    Pr = v.cut(40812, 2, SEQ)
    PT = v.cut(41836, 2, NP_T, P)
    v.cache = [v.cut(42860, KD, KV_LORA), v.cut(44908, KD, KV_LORA), v.cut(12504, KD, KV_LORA)]
    v.krc = [v.cut(46956, KD, QK), v.cut(21208, KD, QK), v.cut(20184, KD, QK)]
    rot = v.cut(21976, 4, H, ROPE // 2)
    mx = v.cut(22488, 4, 2)
    v.newk = v.cut(48492, DEC_B, KV_LORA)
    yz = v.cut(20952, D // 4)
    v.krnew = v.cut(22500, 1, P)
    hml, st, mv, rs, gml = v.norm
    units = [(t, h) for t in range(NP_T) for h in range(H)]
    NU = len(units)
    tab = v.const[:, C_ROPE:C_ROPE + NT * ROPE].rearrange("p (t n) -> p t n", t=NT)
    prep = [("cq", t) for t in range(NT)] + [("uk", j) for j in range(4)] + [("ck", t) for t in range(NT)]
    fill = [("k", h) for h in range(H)] + [("v", t) for t in range(NP_T)]
    for t in range(NT):
        prep += [("q", t, 0), ("q", t, 1)] + fill[3 * t:3 * t + 3] + [("qT", t, 0), ("qT", t, 1)]
    where = {k: i for i, k in enumerate(prep)}

    with nc.Block() as block:
        @block.sync
        def _(sp):
            sp.wait_ge(s["zeros_ready"], 1)
            sp.dma_start(v.d_y[NE * P:, :].rearrange("(p b) (q d) -> p (b q) d", p=P, q=4),
                         yz.unsqueeze(1).to_broadcast([P, 4 * (MAX_BLOCKS - NE), D // 4])).then_inc(s["yz_out"], 16)
            sp.wait_ge(s["zeros_ready"], 2)
            sp.wait_ge(s["ml_ready"], NT)
            for b in range(CB):
                sp.dma_start(v.cache[b], I["cache_ckv"][0, b].rearrange("(k p) n -> p k n", p=P)
                             ).then_inc(s["cache_in"][b], 16)
                sp.dma_start(v.krc[b][:, :, NOPE:], I["cache_kr"][0, b].rearrange("(k p) n -> p k n", p=P)
                             ).then_inc(s["cache_in"][b], 16)

        @block.gpsimd
        def _(pool):
            pool.memset(yz, 0.0).then_inc(s["zeros_ready"], 1)
            pool.memset(v.krc[1][:, :, 0:NOPE], 0.0)
            pool.memset(v.krc[2][:, :, 0:NOPE], 0.0)
            for t in range(NT):
                pool.wait_ge(s["prep_out"], where[("q", t, 1)] + 1)
                x1, x2 = qt[:, t % 2, :, NOPE:NOPE + 16], qt[:, t % 2, :, NOPE + 16:]
                cos = tab[:, t, 0:16].unsqueeze(1).to_broadcast([P, H, 16])
                sin = tab[:, t, 16:32].unsqueeze(1).to_broadcast([P, H, 16])
                pool.tensor_tensor(rot[:, 0], x1, cos, ALU.mult)
                pool.tensor_tensor(rot[:, 1], x2, sin, ALU.mult)
                pool.tensor_tensor(rot[:, 2], x1, sin, ALU.mult)
                s["pool"](pool, pool.tensor_tensor(rot[:, 3], x2, cos, ALU.mult))
                pool.tensor_tensor(x1, rot[:, 0], rot[:, 1], ALU.subtract)
                pool.tensor_tensor(x2, rot[:, 2], rot[:, 3], ALU.add).then_inc(s["q_rot"], 1)
                pool.wait_ge(s["q_rot"], t + 1)
                if t == 0:
                    pool.wait_ge(s["ml_ready"], NT)
                    pool.wait_ge(s["C_out"], 16 * (1 + DEC_B + 2))
                    pool.memset(v.krc[0][:, :, 0:NOPE], 0.0).then_inc(s["zeros_ready"], 1)

        @block.tensor
        def _(pe):
            pe.wait_ge(s["wu_in"], 48)
            for i, it in enumerate(prep):
                if i >= 8:
                    pe.wait_ge(s["prep_out"], i - 7)
                ps = S[i % 8]
                if it[0] == "cq":
                    for k in range(3):
                        ins = pe.transpose(ps[:, k * P:(k + 1) * P], v.z[:, it[1], k * P:(k + 1) * P], v.ident)
                elif it[0] == "ck":
                    for k in range(2):
                        pe.transpose(ps[:, k * P:(k + 1) * P],
                                     v.z[:, it[1], Q_LORA + k * P:Q_LORA + (k + 1) * P], v.ident)
                    ins = pe.transpose(ps[0:QK, 2 * P:3 * P], v.z[:, it[1], ZC - QK:ZC], v.ident)
                elif it[0] == "uk":
                    for h in (2 * it[1], 2 * it[1] + 1):
                        for k in range(2):
                            c = (h % 2) * KV_LORA + k * P
                            ins = pe.transpose(ps[0:NOPE, c:c + P], wuk[:, k, h * NOPE:(h + 1) * NOPE], v.ident)
                elif it[0] == "q":
                    _, t, half = it
                    pe.wait_ge(s["prep_out"], where[("cq", t)] + 1)
                    for k in range(3):
                        ins = pe.matmul(ps[:, 0:384], cqT[:, k, t * P:(t + 1) * P],
                                        wuq[:, k, half * 384:(half + 1) * 384], start=(k == 0), stop=(k == 2))
                elif it[0] == "k":
                    pe.wait_ge(s["prep_out"], where[("ck", NT - 1)] + 1)
                    for k in range(2):
                        ins = pe.matmul(ps[0:NOPE, :], wuk[:, k, it[1] * NOPE:(it[1] + 1) * NOPE],
                                        ckT[:, k, 0:SEQ], start=(k == 0), stop=(k == 1))
                elif it[0] == "v":
                    for k in range(2):
                        ins = pe.matmul(ps[:, :], ckT[:, k, it[1] * P:(it[1] + 1) * P], wuv[:, k, :],
                                        start=(k == 0), stop=(k == 1))
                else:
                    _, t, half = it
                    pe.wait_ge(s["q_rot"], t + 1)
                    for h in range(4):
                        ins = pe.transpose(ps[0:QK, h * P:(h + 1) * P], qt[:, t % 2, 4 * half + h, :], v.ident)
                ins.then_inc(s["prep_acc"], 1)
            pe.wait_ge(s["prep_out"], len(prep))

            def scores(u):
                t, h = units[u]
                n = (t + 1) * P
                if u >= 2:
                    pe.wait_ge(s["at_exp"], u - 1)
                pe.matmul(S[u % 2][:, 0:n], qT[0:QK, h, t * P:n], kT[0:QK, h, 0:n], start=True, stop=False,
                          skip_group_check=True)
                pe.matmul(S[u % 2][:, t * P:n], v.ident, v.const[:, C_NEGA:C_NEGA + P], start=False, stop=True,
                          skip_group_check=True).then_inc(s["at_S"], 1)

            def turn(u):
                t, h = units[u]
                pe.wait_ge(s["at_exp"], u + 1)
                if u >= 2:
                    pe.wait_ge(s["at_PT"], u - 1)
                for k in range(t + 1):
                    ins = pe.transpose(S[2 + u % 2][:, k * P:(k + 1) * P], Pr[:, u % 2, k * P:(k + 1) * P], v.ident)
                ins.then_inc(s["at_T"], 1)

            def weigh(u):
                t, h = units[u]
                pe.wait_ge(s["at_PT"], u + 1)
                if u >= 2:
                    pe.wait_ge(s["at_out"], u - 1)
                for k in range(t + 1):
                    ins = pe.matmul(S[4 + u % 2][:, 0:VD], PT[:, u % 2, k, :], vP[:, k, h * VD:(h + 1) * VD],
                                    start=(k == 0), stop=(k == t))
                ins.then_inc(s["at_O"], 1)

            scores(0)
            for u in range(NU + 1):
                if u + 1 < NU:
                    scores(u + 1)
                if u < NU:
                    turn(u)
                if u >= 1:
                    weigh(u - 1)

        @block.scalar
        def _(act):
            for i, it in enumerate(prep):
                if i == 6:
                    act.wait_ge(s["var_ready"], 1)
                    act.activation(rs[:, 1, :], rs[:, 0, :], ACT.Sqrt).then_inc(s["rs_root"], 1)
                act.wait_ge(s["prep_acc"], i + 1)
                if it == ("ck", 0):
                    act.wait_ge(s["C_out"], 16 * (1 + DEC_B + 2))
                ps = S[i % 8]
                if it[0] == "cq":
                    act.activation(cqT[:, :, it[1] * P:(it[1] + 1) * P],
                                   ps[:, 0:384].rearrange("p (k n) -> p k n", k=3), ACT.Copy).then_inc(s["prep_out"], 1)
                elif it[0] == "ck":
                    act.activation(ckT[:, :, it[1] * P:(it[1] + 1) * P],
                                   ps[:, 0:256].rearrange("p (k n) -> p k n", k=2), ACT.Copy)
                    n = H if it[1] < NP_T else 1
                    dst = kT[NOPE:QK, 0:n, it[1] * P:(it[1] + 1) * P] if it[1] < NP_T else v.krnew[NOPE:QK, :, :]
                    act.activation(dst, ps[NOPE:QK, 256:384].unsqueeze(1).to_broadcast([ROPE, n, P]), ACT.Copy
                                   ).then_inc(s["prep_out"], 1)
                elif it[0] == "uk":
                    act.activation(ukT[0:NOPE, 2 * it[1]:2 * it[1] + 2, :],
                                   ps[0:NOPE, :].rearrange("p (h n) -> p h n", h=2), ACT.Copy).then_inc(s["prep_out"], 1)
                elif it[0] == "q":
                    _, t, half = it
                    if t >= 2:
                        act.wait_ge(s["prep_acc"], where[("qT", t - 2, 1)] + 1)
                    act.activation(qt[:, t % 2, 4 * half:4 * half + 4, :],
                                   ps[:, 0:384].rearrange("p (h n) -> p h n", h=4), ACT.Copy).then_inc(s["prep_out"], 1)
                elif it[0] == "k":
                    act.activation(kT[0:NOPE, it[1], :], ps[0:NOPE, :], ACT.Copy).then_inc(s["prep_out"], 1)
                elif it[0] == "v":
                    act.activation(vP[:, it[1], :], ps[:, :], ACT.Copy).then_inc(s["prep_out"], 1)
                else:
                    _, t, half = it
                    act.activation(qT[0:QK, 4 * half:4 * half + 4, t * P:(t + 1) * P],
                                   ps[0:QK, :].rearrange("p (h n) -> p h n", h=4), ACT.Copy).then_inc(s["prep_out"], 1)

            for u, (t, h) in enumerate(units):
                act.wait_ge(s["at_max"], u + 1)
                if u >= 2:
                    act.wait_ge(s["at_T"], u - 1)
                    act.wait_ge(s["at_out"], u - 1)
                n = (t + 1) * P
                act.activation(Pr[:, u % 2, 0:n], S[u % 2][:, 0:n], ACT.Exp, bias=mx[:, 1, u % 2:u % 2 + 1],
                               scale=ATTN_SCALE, accum_out=mx[:, 2, u % 2:u % 2 + 1]).then_inc(s["at_exp"], 1)

        @block.vector
        def _(dve):
            link = lambda ins: s["dve"](dve, ins)

            def maximum(u):
                t, h = units[u]
                dve.wait_ge(s["at_S"], u + 1)
                link(dve.tensor_reduce(mx[:, 0, u % 2:u % 2 + 1], S[u % 2][:, 0:(t + 1) * P], AX.X, ALU.max))
                if u >= 2:
                    dve.wait_ge(s["at_exp"], u - 1)
                dve.tensor_scalar(mx[:, 1, u % 2:u % 2 + 1], mx[:, 0, u % 2:u % 2 + 1], -ATTN_SCALE, None,
                                  ALU.mult).then_inc(s["at_max"], 1)

            def close(u):
                t, hh = units[u]
                dve.wait_ge(s["at_exp"], u + 1)
                link(dve.reciprocal(mx[:, 3, u % 2:u % 2 + 1], mx[:, 2, u % 2:u % 2 + 1]))
                dve.wait_ge(s["at_O"], u + 1)
                dve.tensor_scalar(v.mix[:, t, hh * VD:(hh + 1) * VD], S[4 + u % 2][:, 0:VD],
                                  mx[:, 3, u % 2:u % 2 + 1], None, ALU.mult).then_inc(s["at_out"], 1)

            for i in range(NT * MH):
                ins = dve.bn_aggr(mv[:, i, :], st[:, i, :])
            link(ins)
            dve.tensor_scalar(rs[:, 0, :], mv[:, :, 1], EPS, None, ALU.add).then_inc(s["var_ready"], 1)
            dve.wait_ge(s["rs_root"], 1)
            link(dve.reciprocal(rs[:, 0, :], rs[:, 1, :]))
            for t in range(NT):
                for hh in range(MH):
                    i = 4 * t + hh
                    dve.tensor_scalar(hml[:, i, :], hml[:, i, :], mv[:, i, 0:1], rs[:, 0, i:i + 1],
                                      ALU.subtract, ALU.mult)
                link(dve.tensor_tensor(v.so[:, t, :], v.so[:, t, :], gml, ALU.mult))
                dve.tensor_tensor(v.mix[:, t, MW:], hml[:, 4 * t:4 * t + 4, :].rearrange("p h e -> p (h e)"),
                                  v.so[:, t, :], ALU.mult).then_inc(s["ml_ready"], 1)

            maximum(0)
            for u in range(NU + 1):
                if u + 1 < NU:
                    maximum(u + 1)
                if u < NU:
                    dve.wait_ge(s["at_T"], u + 1)
                    if u >= 2:
                        dve.wait_ge(s["at_O"], u - 1)
                    n = (units[u][0] + 1) * P
                    dve.tensor_copy(PT[:, u % 2, 0:units[u][0] + 1, :],
                                    S[2 + u % 2][:, 0:n].rearrange("p (k n) -> p k n", n=P)).then_inc(s["at_PT"], 1)
                if u >= 1:
                    close(u - 1)


def stage_decode_attention(nc, I, O, v, s, S):
    KT = PAST // P
    NK = PAST + DEC_T
    cT = v.cut(27884, 2, PAST)
    kT = v.cut(29932, PAST)
    PT = v.cut(30956, KT + 1, P)
    olT = v.cut(32108, 2, H, DEC_B, DEC_T)
    ol = v.cut(34156, 2, KV_LORA)
    mx = v.cut(34668, 8, 2)
    qlT = v.cut(39276, 2, DEC_B, H, DEC_T)
    Pr = v.cut(41324, NK)
    qr = v.cut(34684, DEC_B, H, DEC_T)
    newk, krnew, ckT, qT, ukT, wuv = v.newk, v.krnew, v.ckT, v.qT, v.ukT, v.wuv
    B = DEC_B
    TG = 6

    with nc.Block() as block:
        @block.sync
        def _(sp):
            for b in range(B):
                sp.dma_start(newk[0:DEC_T, b, :],
                             v.z[b * DEC_T:(b + 1) * DEC_T, NP_T, Q_LORA:Q_LORA + KV_LORA]).then_inc(s["new_in"], 16)
            sp.wait_ge(s["yz_out"], 16)
            for b in range(CB, B):
                sp.wait_ge(s["d_O"], b - CB + 1)
                sp.dma_start(v.cache[b % CB], I["cache_ckv"][0, b].rearrange("(k p) n -> p k n", p=P)
                             ).then_inc(s["cache_in"][b % CB], 16)
                sp.dma_start(v.krc[b % CB][:, :, NOPE:], I["cache_kr"][0, b].rearrange("(k p) n -> p k n", p=P)
                             ).then_inc(s["cache_in"][b % CB], 16)

        @block.tensor
        def _(pe):
            n = 0
            for h in range(H):
                for k in range(2):
                    if n >= 4:
                        pe.wait_ge(s["ql_out"], n - 3)
                    pe.matmul(S[n % 4][:, 0:P], ukT[0:NOPE, h, k * P:(k + 1) * P], qT[0:NOPE, h, SEQ:],
                              start=True, stop=True).then_inc(s["ql_acc"], 1)
                    n += 1
            pe.wait_ge(s["ql_out"], n + 1)
            def turn(b, groups):
                slot = b % CB
                if groups[0] == 0:
                    pe.wait_ge(s["cache_in"][slot], 32 * (b // CB + 1))
                for g in groups:
                    if g in (4, 5):
                        pe.wait_ge(s["tr_out_dve"], 2 * b + g - 3)
                    elif g in (2, 3):
                        pe.wait_ge(s["tr_out"], 4 * b + g - 1)
                    elif b >= 1:
                        pe.wait_ge(s["tr_out"], 4 * b + g - 1)
                    bank = S[3 + g % 2]
                    for j in range(4):
                        if g < 4:
                            k, half = (4 * g + j) % KT, (4 * g + j) // KT
                            ins = pe.transpose(bank[:, j * P:(j + 1) * P],
                                               v.cache[slot][:, k, half * P:(half + 1) * P], v.ident)
                        else:
                            ins = pe.transpose(bank[0:QK, j * P:(j + 1) * P],
                                               v.krc[slot][:, 4 * (g - 4) + j, :], v.ident)
                    ins.then_inc(s["tr_acc"], 1)

            def turn_latent(b):
                pe.wait_ge(s["ol_ready"], b + 1)
                for k in range(2):
                    ins = pe.transpose(S[7][:, 256 + k * P:256 + (k + 1) * P], ol[:, b % 2, k * P:(k + 1) * P], v.ident)
                ins.then_inc(s["ol_T"], 1)

            turn(0, range(TG))
            for b in range(B):
                pe.wait_ge(s["tr_out"], 4 * (b + 1))
                pe.wait_ge(s["tr_out_dve"], 2 * (b + 1))
                if b >= 1:
                    pe.wait_ge(s["d_exp"], b)
                for c, (lo, hi) in enumerate(((0, 512), (512, 1024), (1024, NK))):
                    w = hi - lo
                    for k in range(2):
                        rhs = cT[:, k, lo:hi] if c < 2 else ckT[:, k, SEQ + b * DEC_T:SEQ + (b + 1) * DEC_T]
                        pe.matmul(S[c][:, 0:w], qlT[:, k, b, :, :], rhs, start=(k == 0), stop=False)
                    rhs = kT[NOPE:QK, lo:hi] if c < 2 else krnew[NOPE:QK, 0, b * DEC_T:(b + 1) * DEC_T]
                    ins = pe.matmul(S[c][:, 0:w], qr[NOPE:QK, b, :, :], rhs,
                                    start=False, stop=True)
                ins.then_inc(s["d_S"], 1)
                if b >= 1:
                    turn_latent(b - 1)
                if b + 1 < B:
                    turn(b + 1, range(TG))
                pe.wait_ge(s["d_exp"], b + 1)
                for g in range(3):
                    bank = S[5 + g % 2]
                    if g == 2:
                        pe.wait_ge(s["p_out"], 3 * b + 1)
                    elif b >= 1:
                        pe.wait_ge(s["p_out"], 3 * b)
                    if g < 2:
                        for j in range(4):
                            k = 4 * g + j
                            ins = pe.transpose(bank[:, j * P:(j + 1) * P], Pr[:, k * P:(k + 1) * P], v.ident)
                    else:
                        ins = pe.transpose(bank[0:DEC_T, 0:P], Pr[:, PAST:NK], v.ident)
                    ins.then_inc(s["p_acc"], 1)
                if b == 0:
                    pe.wait_ge(s["new_in"], 16 * B)
                else:
                    pe.wait_ge(s["ol_out"], b)
                for k in range(KT + 1):
                    if k % 4 == 0:
                        pe.wait_ge(s["p_out"], 3 * b + k // 4 + 1)
                    if k < KT:
                        pe.matmul(S[7][:, 0:KV_LORA], PT[:, k, :], v.cache[b % CB][:, k, :],
                                  start=(k == 0), stop=False)
                    else:
                        pe.matmul(S[7][:, 0:KV_LORA], PT[0:DEC_T, KT, :], newk[0:DEC_T, b, :], start=False, stop=True
                                  ).then_inc(s["d_O"], 1)
            turn_latent(B - 1)
            pe.wait_ge(s["ol_out"], B)
            for h in range(H):
                for k in range(2):
                    ins = pe.matmul(S[0][:, h * VD:(h + 1) * VD], olT[:, k, h, :, :], wuv[:, k, h * VD:(h + 1) * VD],
                                    start=(k == 0), stop=(k == 1))
            ins.then_inc(s["datt_acc"], 1)

        @block.scalar
        def _(act):
            def evac(b, groups):
                for g in groups:
                    m = TG * b + g
                    act.wait_ge(s["tr_acc"], m + 1)
                    if g == 0 and b >= 1:
                        act.wait_ge(s["d_S"], b)
                    if g < 2:
                        c = g * 512
                        ins = act.activation(cT[:, 0, c:c + 512], S[3 + g % 2][:, :], ACT.Copy)
                    else:
                        c = (g - 4) * 512
                        ins = act.activation(kT[NOPE:QK, c:c + 512], S[3 + g % 2][NOPE:QK, :], ACT.Copy)
                    ins.then_inc(s["tr_out"], 1)

            evac(0, (0, 1, 4, 5))
            for b in range(B):
                if b + 1 < B:
                    evac(b + 1, (0, 1))
                act.wait_ge(s["d_max"], b + 1)
                if b >= 1:
                    act.wait_ge(s["p_acc"], 3 * b)
                for c, (lo, hi) in enumerate(((0, 512), (512, 1024), (1024, NK))):
                    ins = act.activation(Pr[:, lo:hi], S[c][:, 0:hi - lo], ACT.Exp, bias=mx[:, 4, 0:1],
                                         scale=ATTN_SCALE, accum_out=mx[:, 5 + c, 0:1])
                ins.then_inc(s["d_exp"], 1)
                if b + 1 < B:
                    evac(b + 1, (4, 5))

        @block.vector
        def _(dve):
            link = lambda ins: s["dve"](dve, ins)
            n = 0
            for h in range(H):
                for k in range(2):
                    dve.wait_ge(s["ql_acc"], n + 1)
                    dve.tensor_copy(qlT[:, k, :, h, :],
                                    S[n % 4][:, 0:P].rearrange("p (b t) -> p b t", b=B)).then_inc(s["ql_out"], 1)
                    n += 1
            dve.tensor_copy(qr[NOPE:QK].rearrange("p b h t -> p h b t"),
                            qT[NOPE:QK, :, SEQ:].rearrange("p h (b t) -> p h b t", b=B)).then_inc(s["ql_out"], 1)
            def latent_out(b):
                dve.wait_ge(s["ol_T"], b + 1)
                dve.tensor_copy(olT[:, :, :, b, :],
                                S[7][:, 256:512].rearrange("p (k h t) -> p k h t", k=2, h=H)).then_inc(s["ol_out"], 1)

            def evac(b):
                for g in (2, 3):
                    dve.wait_ge(s["tr_acc"], TG * b + g + 1)
                    dve.tensor_copy(cT[:, 1, (g - 2) * 512:(g - 1) * 512], S[3 + g % 2][:, :]
                                    ).then_inc(s["tr_out_dve"], 1)

            evac(0)
            for b in range(B):
                dve.wait_ge(s["d_S"], b + 1)
                for c, w in enumerate((512, 512, DEC_T)):
                    ins = dve.tensor_reduce(mx[:, c, 0:1], S[c][:, 0:w], AX.X, ALU.max)
                link(ins)
                link(dve.tensor_tensor(mx[:, 3, 0:1], mx[:, 0, 0:1], mx[:, 1, 0:1], ALU.max))
                link(dve.tensor_tensor(mx[:, 3, 0:1], mx[:, 3, 0:1], mx[:, 2, 0:1], ALU.max))
                dve.tensor_scalar(mx[:, 4, 0:1], mx[:, 3, 0:1], -ATTN_SCALE, None, ALU.mult).then_inc(s["d_max"], 1)
                if b >= 1:
                    latent_out(b - 1)
                if b + 1 < B:
                    evac(b + 1)
                for g in range(3):
                    dve.wait_ge(s["p_acc"], 3 * b + g + 1)
                    if g < 2:
                        ins = dve.tensor_copy(PT[:, 4 * g:4 * g + 4, :],
                                              S[5 + g % 2][:, :].rearrange("p (k n) -> p k n", n=P))
                    else:
                        ins = dve.tensor_copy(PT[0:DEC_T, KT, :], S[5 + g % 2][0:DEC_T, 0:P])
                    ins.then_inc(s["p_out"], 1)
                dve.wait_ge(s["d_exp"], b + 1)
                link(dve.tensor_tensor(mx[:, 0, 1:2], mx[:, 5, 0:1], mx[:, 6, 0:1], ALU.add))
                link(dve.tensor_tensor(mx[:, 0, 1:2], mx[:, 0, 1:2], mx[:, 7, 0:1], ALU.add))
                link(dve.reciprocal(mx[:, 1, 1:2], mx[:, 0, 1:2]))
                dve.wait_ge(s["d_O"], b + 1)
                dve.tensor_scalar(ol[:, b % 2, :], S[7][:, 0:KV_LORA], mx[:, 1, 1:2], None, ALU.mult
                                  ).then_inc(s["ol_ready"], 1)
            latent_out(B - 1)
            dve.wait_ge(s["datt_acc"], 1)
            dve.tensor_copy(v.mix[:, NP_T, 0:H * VD], S[0][:, :])


def stage_output_router(nc, I, O, v, s, S):
    wo = v.cut(27884, 2, KD, 512)
    x = v.cut(36076, NT, D)
    G = v.cut(41196, 3, 2, D)
    ln = v.cut(49388, 2, D)
    mixT = v.cut(47340, 2, KD, P)
    u2T = v.cut(11192, 2, KD, P)
    rw = v.cut(13240, KD, NE)
    rb = v.cut(13496, NE)
    u2 = v.cut(15064, 2, D)
    x1 = v.cut(17112, 2, D)
    tmp = v.cut(19160, 2, D)
    o = 13528
    bn = v.cut(o, 2, 2, 6)
    mv = v.cut(o + 24, NT, 2)
    rs = v.cut(o + 34, NT, 2)
    lg = v.cut(o + 44, NT, NE)
    mask = v.cut(o + 204, NT, NE)
    top = v.cut(o + 364, NT, 8)
    topf = v.cut(o + 404, NT, 8)
    ex = v.cut(o + 444, NT, TOPK)
    es = v.cut(o + 464, NT, 2)
    oh = v.cut(o + 474, NT, TOPK, NE)
    assert o + 1114 <= 15064
    cnt = v.cut(21208, 6, NE)
    gs = v.cut(21400, NT, NE)
    slotf = v.cut(21560, NT, TOPK)
    dummy = v.cut(21580, 2, NE)
    v.table = v.cut(2800, MAX_BLOCKS + 2).bitcast(U32)
    split = v.cut(21760, 2, NT, TOPK).bitcast(U32)
    splitf = v.cut(21800, 2, NT, TOPK)
    hotm = v.cut(21840, 4, P)
    hotd = v.cut(22352, 4, MAX_BLOCKS + 2)
    topi = v.cut(21720, NT, 8).bitcast(U32)
    v.slot = v.cut(2700, NT, TOPK).bitcast(U32)
    v.wts = v.cut(2720, NT, TOPK)
    v.cum = v.cut(2740, NE + 1).bitcast(I32)
    iota = v.const[:, C_IOTA:C_IOTA + P]
    two = lambda b: v.psum[:, b:b + 2, :].rearrange("p a n -> p (a n)")

    with nc.Block() as block:
        @block.sync
        def _(sp):
            for j in range(2):
                sp.dma_start(wo[:, j], I["w_o"][0][:, j * 512:(j + 1) * 512].rearrange("(k p) n -> p k n", p=P)
                             ).then_inc(s["wo_in"], 16)
            spread_rows(sp, G, v, 2, 3, s["G_in"])
            sp.dma_start(x[:, 0:NP_T, :], I["x_prompt"][0].rearrange("(t p) d -> p t d", p=P)).then_inc(s["x2_in"], 16)
            sp.dma_start(x[:, NP_T, :], I["x_sample"].rearrange("b t d -> (b t) d")).then_inc(s["x2_in"], 16)
            sp.dma_start(ln[:, 0], bcast_rows(I["ln1_g"][0], P)).then_inc(s["x2_in"], 16)
            sp.dma_start(ln[:, 1], bcast_rows(I["ln1_b"][0], P)).then_inc(s["x2_in"], 16)
            sp.dma_start(rw, I["router_w"][0].rearrange("(k p) n -> p k n", p=P)).then_inc(s["rw_in"], 16)
            sp.dma_start(rb, bcast_rows(I["router_b"][0], P)).then_inc(s["rw_in"], 16)
            first_up = v.cut(3000, 2, KD, 512)
            for g in range(2):
                sp.dma_start(first_up[:, g], I["w_up"][0, 0].rearrange("(k p) n -> p k n", p=P)
                             [:, :, g * FF:g * FF + 512]).then_inc(s["up_in"][0][0], 16)
            for t in range(NT):
                if t == NT - 1:
                    sp.wait_ge(s["wo_acc"], NT)
                    next_up = v.cut(27576, 2, KD, 512)
                    for g in range(2):
                        sp.dma_start(next_up[:, g], I["w_up"][0, 1].rearrange("(k p) n -> p k n", p=P)
                                     [:, :, g * FF + 512:(g + 1) * FF]).then_inc(s["up_in"][1][1], 16)
                sp.wait_ge(s["x1_ready"], t + 1)
                sp.dma_start(v.d_x1[t * P:(t + 1) * P, :], x1[:, t % 2]).then_inc(s["x1_out"][t % 2], 16)
                sp.wait_ge(s["u2_ready"], t + 1)
                sp.dma_start(v.d_u2[t * P:(t + 1) * P, :], u2[:, t % 2]).then_inc(s["u2_out"][t % 2], 16)
            sp.dma_start(v.cut(35768, 2, 4 * D), I["w_down"][0, 0].rearrange("(j p k) n -> p j (k n)", j=2, k=4)
                         ).then_inc(s["down_in"], 16)
            for par, n in ((0, (NT + 1) // 2), (1, NT // 2)):
                sp.wait_ge(s["x1_out"][par], 16 * n)
                sp.wait_ge(s["u2_out"][par], 16 * n)

        @block.scalar
        def _(act):
            def mix_T(t):
                for j in range(2):
                    act.wait_ge(s["mT_acc"], 2 * t + j + 1)
                    if t >= 2:
                        act.wait_ge(s["wo_acc"], t - 1)
                    act.activation(mixT[:, t % 2, 4 * j:4 * j + 4, :],
                                   S[j][:, :].rearrange("p (k n) -> p k n", n=P), ACT.Copy).then_inc(s["mT_out"], 1)

            mix_T(0)
            for t in range(NT):
                if t + 1 < NT:
                    mix_T(t + 1)
                act.wait_ge(s["var1"], t + 1)
                act.activation(rs[:, t, 1:2], rs[:, t, 0:1], ACT.Sqrt).then_inc(s["root1"], 1)
                for j in range(2):
                    act.wait_ge(s["uT2_acc"], 2 * t + j + 1)
                    if t >= 2:
                        act.wait_ge(s["lg_acc"], t - 1)
                    act.activation(u2T[:, t % 2, 4 * j:4 * j + 4, :],
                                   S[6 + j][:, :].rearrange("p (k n) -> p k n", n=P), ACT.Copy
                                   ).then_inc(s["uT2_out"], 1)
            for t in range(NT):
                act.wait_ge(s["top_neg"], t + 1)
                act.activation(ex[:, t, :], top[:, t, 0:TOPK], ACT.Exp, bias=es[:, t, 0:1],
                               accum_out=es[:, t, 1:2]).then_inc(s["ex_ready"], 1)

        @block.gpsimd
        def _(pool):
            pool.wait_ge(s["G_in"], 16 * (1 + DEC_B))
            pool.tensor_scalar(G[:, 2], G[:, 2], 1.0, None, ALU.add).then_inc(s["sc2_ready"], 1)
            pool.wait_ge(s["sc2_ready"], 1)
            for t in range(NT - 1):
                who = 0 if t < NP_T else 1
                pool.wait_ge(s["x1_ready"], t + 1)
                if t >= 2:
                    pool.wait_ge(s["u2_out"][t % 2], 16 * (t // 2))
                    pool.wait_ge(s["uT2_acc"], 2 * (t - 1))
                s["pool"](pool, pool.tensor_tensor(u2[:, t % 2], x1[:, t % 2], G[:, 2, who], ALU.mult))
                pool.tensor_tensor(u2[:, t % 2], u2[:, t % 2], G[:, 1, who], ALU.add).then_inc(s["u2_ready"], 1)

        @block.tensor
        def _(pe):
            def mix_T(t):
                for j in range(2):
                    if t:
                        pe.wait_ge(s["mT_out"], 2 * t - 1 + j)
                    for k in range(4):
                        ins = pe.transpose(S[j][:, k * P:(k + 1) * P], v.mix[:, t, (4 * j + k) * P:(4 * j + k + 1) * P],
                                           v.ident)
                    ins.then_inc(s["mT_acc"], 1)

            def project(t):
                pe.wait_ge(s["mT_out"], 2 * t + 2)
                if t == 0:
                    pe.wait_ge(s["wo_in"], 32)
                if t >= 2:
                    pe.wait_ge(s["wo_read"], t - 1)
                for n in range(2):
                    for k in range(KD):
                        ins = pe.matmul(S[2 + 2 * (t % 2) + n][:, :], mixT[:, t % 2, k, :], wo[:, n, k, :],
                                        start=(k == 0), stop=(k == KD - 1))
                ins.then_inc(s["wo_acc"], 1)

            def router(t):
                pe.wait_ge(s["u2_ready"], t + 1)
                for j in range(2):
                    if t:
                        pe.wait_ge(s["lg_read"], t) if j == 0 else pe.wait_ge(s["uT2_out"], 2 * t)
                    for k in range(4):
                        ins = pe.transpose(S[6 + j][:, k * P:(k + 1) * P],
                                           u2[:, t % 2, (4 * j + k) * P:(4 * j + k + 1) * P], v.ident)
                    ins.then_inc(s["uT2_acc"], 1)
                pe.wait_ge(s["uT2_out"], 2 * t + 2)
                if t == 0:
                    pe.wait_ge(s["rw_in"], 32)
                for k in range(KD):
                    ins = pe.matmul(S[6][:, 0:NE], u2T[:, t % 2, k, :], rw[:, k, :], start=(k == 0), stop=(k == KD - 1))
                ins.then_inc(s["lg_acc"], 1)

            mix_T(0)
            for t in range(NT):
                if t + 1 < NT:
                    mix_T(t + 1)
                project(t)
                if t >= 1:
                    router(t - 1)
            router(NT - 1)
            pe.wait_ge(s["mask_ready"], NT)
            for t in range(NT):
                for tt in range(t):
                    pe.matmul(S[0][:, t * NE:(t + 1) * NE], v.ones, mask[:, tt, :], start=(tt == 0), stop=False)
                pe.matmul(S[0][:, t * NE:(t + 1) * NE], v.const[:, C_TRI:C_TRI + P], mask[:, t, :],
                          start=(t == 0), stop=True)
            for t in range(NT):
                ins = pe.matmul(S[1][:, 0:NE], v.ones, mask[:, t, :], start=(t == 0), stop=(t == NT - 1))
            ins.then_inc(s["pos_acc"], 1)
            for i in range(NT * TOPK):
                pe.wait_ge(s["hot_ready"], i + 1)
                ins = pe.matmul(S[2][:, 0:MAX_BLOCKS + 2], hotm[:, i % 4, :], hotd[:, i % 4, :],
                                start=(i == 0), stop=(i == NT * TOPK - 1))
                ins.then_inc(s["hot_acc"], 1)

        @block.vector
        def _(dve):
            link = lambda ins: s["dve"](dve, ins)
            dve.wait_ge(s["x2_in"], 64)
            dve.wait_ge(s["G_in"], 16 * (1 + DEC_B))
            def norm(t):
                who = 0 if t < NP_T else 1
                dve.wait_ge(s["wo_acc"], t + 1)
                tm = tmp[:, t % 2]
                dve.tensor_tensor(tm, two(2 + 2 * (t % 2)), G[:, 0, who], ALU.mult).then_inc(s["wo_read"], 1)
                dve.wait_ge(s["wo_read"], t + 1)
                link(dve.scalar_tensor_tensor(x[:, t], x[:, t], ALPHA, tm, ALU.mult, ALU.add))
                for j in range(2):
                    ins = dve.bn_stats(bn[:, t % 2, j, :], x[:, t, j * 512:(j + 1) * 512])
                link(ins)
                link(dve.bn_aggr(mv[:, t, :], bn[:, t % 2]))
                dve.tensor_scalar(rs[:, t, 0:1], mv[:, t, 1:2], EPS, None, ALU.add).then_inc(s["var1"], 1)
                dve.wait_ge(s["root1"], t + 1)
                link(dve.reciprocal(rs[:, t, 0:1], rs[:, t, 1:2]))
                if t >= 2:
                    dve.wait_ge(s["x1_out"][t % 2], 16 * (t // 2))
                    dve.wait_ge(s["u2_ready"], t - 1)
                xo = x1[:, t % 2]
                link(dve.tensor_scalar(xo, x[:, t], mv[:, t, 0:1], rs[:, t, 0:1], ALU.subtract, ALU.mult))
                link(dve.tensor_tensor(xo, xo, ln[:, 0], ALU.mult))
                dve.tensor_tensor(xo, xo, ln[:, 1], ALU.add).then_inc(s["x1_ready"], 1)
                if t == NT - 1:
                    dve.wait_ge(s["x1_ready"], NT)
                    dve.wait_ge(s["sc2_ready"], 1)
                    dve.wait_ge(s["u2_ready"], NT - 1)
                    dve.wait_ge(s["u2_out"][t % 2], 16 * (t // 2))
                    dve.wait_ge(s["uT2_acc"], 2 * (t - 1))
                    link(dve.tensor_tensor(u2[:, t % 2], xo, G[:, 2, who], ALU.mult))
                    dve.tensor_tensor(u2[:, t % 2], u2[:, t % 2], G[:, 1, who], ALU.add).then_inc(s["u2_ready"], 1)

            def choose(t):
                dve.wait_ge(s["lg_acc"], t + 1)
                dve.tensor_tensor(lg[:, t, :], S[6][:, 0:NE], rb, ALU.add).then_inc(s["lg_read"], 1)
                dve.wait_ge(s["lg_read"], t + 1)
                link(dve.max(top[:, t, :], lg[:, t, :]))
                dve.tensor_scalar(es[:, t, 0:1], top[:, t, 0:1], -1.0, None, ALU.mult).then_inc(s["top_neg"], 1)
                link(dve.max_index(topi[:, t, :], top[:, t, :], lg[:, t, :]))
                link(dve.tensor_copy(topf[:, t, :], topi[:, t, :]))
                link(dve.tensor_tensor(oh[:, t], iota[:, 0:NE].unsqueeze(1).to_broadcast([P, TOPK, NE]),
                                       topf[:, t, 0:TOPK].unsqueeze(2).to_broadcast([P, TOPK, NE]), ALU.is_equal))
                dve.tensor_tensor(dummy[:, 0], oh[:, t, 0], oh[:, t, 1], ALU.add)
                link(dve.tensor_tensor(dummy[:, 1], oh[:, t, 2], oh[:, t, 3], ALU.add))
                dve.tensor_tensor(mask[:, t, :], dummy[:, 0], dummy[:, 1], ALU.add).then_inc(s["mask_ready"], 1)
                dve.wait_ge(s["mask_ready"], t + 1)

            for t in range(NT):
                norm(t)
                if t >= 1:
                    choose(t - 1)
            choose(NT - 1)
            for t in range(NT):
                dve.wait_ge(s["ex_ready"], t + 1)
                link(dve.reciprocal(es[:, t, 0:1], es[:, t, 1:2]))
                dve.tensor_scalar(v.wts[:, t, :], ex[:, t, :], es[:, t, 0:1], None, ALU.mult)
            dve.wait_ge(s["pos_acc"], 1)
            c, nb, ns, inc = cnt[:, 0], cnt[:, 1], cnt[:, 2], cnt[:, 3]
            dve.memset(cnt[:, 4], 1.0)
            link(dve.tensor_copy(c, S[1][:, 0:NE]))
            link(dve.tensor_scalar(nb, c, float(P), 1.0, ALU.is_gt, ALU.add))
            for j in range(2, NT):
                link(dve.tensor_scalar(ns, c, float(P * j), None, ALU.is_gt))
                link(dve.tensor_tensor(nb, nb, ns, ALU.add))
            link(dve.tensor_tensor_scan(inc, cnt[:, 4], nb, 0.0, ALU.mult, ALU.add))
            link(dve.tensor_tensor(ns, inc, nb, ALU.subtract))
            link(dve.tensor_scalar(cnt[:, 5], ns, float(P), None, ALU.mult))
            dve.memset(v.cum[0:1, 0:1], 0)
            dve.tensor_copy(v.cum[0:1, 1:NE + 1], inc[0:1, :])
            for t in range(NT):
                ins = dve.tensor_tensor(gs[:, t, :], S[0][:, t * NE:(t + 1) * NE], cnt[:, 5], ALU.add)
            link(ins)
            link(dve.tensor_tensor(oh, oh, gs.unsqueeze(2).to_broadcast([P, NT, TOPK, NE]), ALU.mult))
            link(dve.tensor_reduce(slotf, oh, AX.X, ALU.add))
            link(dve.tensor_copy(v.slot, slotf))
            dve.tensor_scalar(split[:, 0], v.slot, 127, None, ALU.bitwise_and)
            link(dve.tensor_scalar(split[:, 1], v.slot, 7, None, ALU.logical_shift_right))
            link(dve.tensor_copy(splitf, split))
            for i in range(NT * TOPK):
                tt, k = i // TOPK, i % TOPK
                if i >= 4:
                    dve.wait_ge(s["hot_acc"], i - 3)
                dve.tensor_scalar(hotm[:, i % 4, :], iota, splitf[:, 0, tt, k:k + 1], None, ALU.is_equal)
                dve.tensor_scalar(hotd[:, i % 4, :], iota[:, 0:MAX_BLOCKS + 2], splitf[:, 1, tt, k:k + 1],
                                  v.const[:, C_TOK + tt:C_TOK + tt + 1], ALU.is_equal, ALU.mult
                                  ).then_inc(s["hot_ready"], 1)
            dve.wait_ge(s["hot_acc"], NT * TOPK)
            dve.tensor_copy(v.table, S[2][:, 0:MAX_BLOCKS + 2])


def stage_experts(nc, I, O, v, s, S):
    up = [[v.cut(3000 + (2 * half + par) * 8192, 2, KD, 512) for half in range(2)] for par in range(2)]
    down = v.cut(3000 + 4 * 8192, 2, 4, D)
    xg = v.cut(43960, D)
    xT = v.cut(44984, KD, P)
    bu = v.cut(46008, 2 * FF)
    hid = v.cut(48056, FF)
    hidT = v.cut(49080, 2, 4, P)
    bd = v.cut(50104, 2, D)
    glu, sig, lin = v.cut(128, 512), v.cut(640, 512), v.cut(1152, 512)
    y = v.cut(1664, D)
    idx = v.cut(52152, 1).bitcast(U32)
    v.x1_res, v.gate2 = v.cut(3000, NT, D), v.cut(8120, 1, 2, D)
    v.ln2 = v.cut(19384, 2, D)
    w_up = I["w_up"][0].rearrange("e (k p) (g j n) -> e p k g j n", p=P, g=2, j=2)
    w_down = I["w_down"][0].rearrange("e (j p k) n -> e p j (k n)", j=2, k=4)

    def cum(eng, i, least=0):
        return eng.value_load(v.cum[0:1, bass.ds(i, 1)] if not isinstance(i, int) else v.cum[0:1, i:i + 1],
                              min_val=least, max_val=MAX_BLOCKS)

    with nc.Block() as block:
        @block.sync
        def _(sp):
            def load_up(e, par, half):
                for g in range(2):
                    sp.dma_start(up[par][half][:, g], w_up[bass.ds(e, 1), :, :, g, half, :]
                                 .rearrange("e p k n -> p (e k) n")).then_inc(s["up_in"][par][half], 16)

            def load_down(e):
                sp.dma_start(down.rearrange("p j k n -> p j (k n)"),
                             w_down[bass.ds(e, 1)].rearrange("e p j n -> p (e j) n")).then_inc(s["down_in"], 16)

            def load_bias(e, par):
                sp.dma_start(bu, I["b_up"][0][bass.ds(e, 1), :].rearrange("e n -> (e n)").partition_broadcast(P)
                              ).then_inc(s["bias_in"], 16)
                sp.dma_start(bd[:, par], I["b_down"][0][bass.ds(e, 1), :].rearrange("e n -> (e n)")
                             .partition_broadcast(P)).then_inc(s["bias_in"], 16)

            def step(e, par, last=False):
                blocks = cum(sp, e, least=1)
                sp.wait_ge(s["hid_ready"], blocks * 2)
                load_bias(e, par)
                sp.wait_ge(s["y_acc"], blocks)
                load_down(e)
                if not last:
                    load_up(e + 1, 1 - par, 0)
                    load_up(e + 1, 1 - par, 1)
                else:
                    sp.dma_start(v.x1_res, v.d_x1.rearrange("(t p) d -> p t d", p=P)).then_inc(s["f_in"], 16)
                    spread_rows(sp, v.gate2, v, 5, 1, s["f_in"])
                    sp.dma_start(v.ln2[:, 0], bcast_rows(I["ln2_g"][0], P)).then_inc(s["f_in"], 16)
                    sp.dma_start(v.ln2[:, 1], bcast_rows(I["ln2_b"][0], P)).then_inc(s["f_in"], 16)

            load_bias(0, 0)
            sp.wait_ge(s["xg_in"], 16)
            load_up(0, 0, 1)
            sp.wait_ge(s["turned"], 2)
            load_up(1, 1, 0)
            with sp.Fori(0, NE // 2 - 1) as i:
                step(i * 2 + 1, 1)
                step(i * 2 + 2, 0)
            step(NE - 1, 1, last=True)

        @block.gpsimd
        def _(pool):
            def gather(b):
                pool.tensor_copy(idx, v.table[:, bass.ds(b, 1)]).then_inc(s["idx_in"], 1)
                pool.wait_ge(s["idx_in"], b + 1)
                pool.sem_inc(s["idx_seen"], 1)
                pool.indirect_dma_start(out=xg, out_offset=None, in_=v.d_u2,
                                        in_offset=bass.IndirectOffsetOnAxis(ap=idx, axis=0)).then_inc(s["xg_in"], 16)

            pool.sem_inc(s["y_stored"], 1)
            gather(0)
            pool.wait_ge(s["turned"], 2)
            gather(1)
            total = cum(pool, NE, least=NE)
            with pool.Fori(0, total) as b:
                pool.wait_ge(s["turned"], b * 4 + 5)
                gather(b + 2)
                pool.wait_ge(s["y_ready"], b + 2)
                pool.dma_start(v.d_y[bass.ds(b * P, P), :], y).then_inc(s["y_out"], 16)
                pool.wait_ge(s["y_out"], b * 16 + 16)
                pool.sem_inc(s["y_stored"], 1)
            pool.wait_ge(s["xg_in"], total * 16 + 32)
            pool.wait_ge(s["y_stored"], total + 1)

        @block.scalar
        def _(act):
            def x_evac(j):
                act.activation(xT[:, 4 * j:4 * j + 4, :], S[6 + j][:, :].rearrange("p (k n) -> p k n", n=P),
                               ACT.Copy).then_inc(s["turn_out"], 1)

            for j in range(2):
                act.wait_ge(s["turned"], j + 1)
                x_evac(j)

            blocks = cum(act, NE, least=NE)
            with act.Fori(0, blocks) as b:
                n = b * 4
                act.wait_ge(s["glu_ready"], b * 2 + 1)
                act.activation(sig, glu, ACT.Sigmoid, scale=SW_ALPHA).then_inc(s["sig_ready"], 1)
                act.wait_ge(s["turned"], n + 3)
                act.activation(hidT[:, 0], S[6][:, :].rearrange("p (k n) -> p k n", n=P), ACT.Copy
                               ).then_inc(s["turn_out"], 1)
                act.wait_ge(s["turned"], n + 4)
                act.activation(xT[:, 0:4, :], S[7][:, :].rearrange("p (k n) -> p k n", n=P), ACT.Copy
                               ).then_inc(s["turn_out"], 1)
                act.wait_ge(s["turned"], n + 5)
                act.activation(xT[:, 4:8, :], S[6][:, :].rearrange("p (k n) -> p k n", n=P), ACT.Copy
                               ).then_inc(s["turn_out"], 1)
                act.wait_ge(s["glu_ready"], b * 2 + 2)
                act.activation(sig, glu, ACT.Sigmoid, scale=SW_ALPHA).then_inc(s["sig_ready"], 1)
                act.wait_ge(s["turned"], n + 6)
                act.activation(hidT[:, 1], S[7][:, :].rearrange("p (k n) -> p k n", n=P), ACT.Copy
                               ).then_inc(s["turn_out"], 1)


        @block.tensor
        def _(pe):
            def x_turn(j, bank):
                for k in range(4):
                    ins = pe.transpose(bank[:, k * P:(k + 1) * P], xg[:, (4 * j + k) * P:(4 * j + k + 1) * P], v.ident)
                ins.then_inc(s["turned"], 1)

            def h_turn(j, bank):
                for k in range(4):
                    ins = pe.transpose(bank[:, k * P:(k + 1) * P], hid[:, j * 512 + k:(j + 1) * 512:4], v.ident)
                ins.then_inc(s["turned"], 1)

            pe.wait_ge(s["xg_in"], 16)
            for j in range(2):
                x_turn(j, S[6 + j])

            def expert(e, par):
                lo, hi = cum(pe, e), cum(pe, e + 1)
                with pe.Fori(lo, hi) as b:
                    n = b * 4
                    pe.wait_ge(s["turn_out"], n + 2)
                    for half in range(2):
                        pe.wait_ge(s["up_read"][half], b + 1)
                        pe.wait_ge(s["up_in"][par][half], (e - par) * 16 + 32)
                        for g in range(2):
                            for k in range(KD):
                                ins = pe.matmul(S[2 * half + g][:, :], xT[:, k, :], up[par][half][:, g, k, :],
                                                start=(k == 0), stop=(k == KD - 1))
                        ins.then_inc(s["up_acc"], 1)
                    pe.wait_ge(s["hid_ready"], b * 2 + 1)
                    h_turn(0, S[6])
                    pe.wait_ge(s["xg_in"], b * 16 + 32)
                    x_turn(0, S[7])
                    pe.wait_ge(s["turn_out"], n + 3)
                    x_turn(1, S[6])
                    pe.wait_ge(s["y_ready"], b + 1)
                    pe.wait_ge(s["down_in"], e * 16 + 16)

                    def down_half(j, c):
                        for k in range(4):
                            ins = pe.matmul(S[4 + c][:, :], hidT[:, j, k, :], down[:, j, k, c * 512:(c + 1) * 512],
                                            start=(j == 0 and k == 0), stop=(j == 1 and k == 3))
                        return ins
                    down_half(0, 0)
                    pe.wait_ge(s["hid_ready"], b * 2 + 2)
                    pe.wait_ge(s["turn_out"], n + 4)
                    h_turn(1, S[7])
                    down_half(0, 1)
                    pe.wait_ge(s["turn_out"], n + 6)
                    down_half(1, 0)
                    down_half(1, 1).then_inc(s["y_acc"], 1)

            with pe.Fori(0, NE // 2) as i:
                expert(i * 2, 0)
                expert(i * 2 + 1, 1)

        @block.vector
        def _(dve):
            def half_step(b, j):
                dve.wait_ge(s["up_acc"], b * 2 + j + 1)
                dve.tensor_tensor(glu, S[2 * j][:, :], bu[:, j * 512:(j + 1) * 512], ALU.add
                                  ).then_inc(s["glu_sum"], 1)
                dve.tensor_tensor(lin, S[2 * j + 1][:, :], bu[:, FF + j * 512:FF + (j + 1) * 512], ALU.add
                                  ).then_inc(s["up_read"][j], 1)
                dve.wait_ge(s["glu_sum"], b * 2 + j + 1)
                dve.tensor_scalar(glu, glu, LIMIT, None, ALU.min).then_inc(s["glu_ready"], 1)
                dve.wait_ge(s["up_read"][j], b + 2)
                dve.tensor_scalar(lin, lin, LIMIT, -LIMIT, ALU.min, ALU.max).then_inc(s["lin_ready"], 1)
                dve.wait_ge(s["sig_ready"], b * 2 + j + 1)
                dve.tensor_tensor(glu, glu, sig, ALU.mult).then_inc(s["glu_gated"], 1)
                dve.wait_ge(s["glu_gated"], b * 2 + j + 1)
                dve.wait_ge(s["lin_ready"], b * 2 + j + 1)
                dve.scalar_tensor_tensor(hid[:, j * 512:(j + 1) * 512], lin, 1.0, glu, ALU.add, ALU.mult
                                         ).then_inc(s["hid_ready"], 1)
                dve.wait_ge(s["hid_ready"], b * 2 + j + 1)

            def expert(e, par):
                lo, hi = cum(dve, e), cum(dve, e + 1)
                with dve.Fori(lo, hi) as b:
                    dve.wait_ge(s["bias_in"], e * 32 + 32)
                    half_step(b, 0)
                    half_step(b, 1)
                    dve.wait_ge(s["y_acc"], b + 1)
                    dve.wait_ge(s["y_stored"], b + 1)
                    dve.tensor_tensor(y, v.psum[:, 4:6, :].rearrange("p a n -> p (a n)"), bd[:, par], ALU.add
                                      ).then_inc(s["y_ready"], 1)

            dve.sem_inc(s["up_read"][0], 1)
            dve.sem_inc(s["up_read"][1], 1)
            dve.sem_inc(s["y_ready"], 1)
            with dve.Fori(0, NE // 2) as i:
                expert(i * 2, 0)
                expert(i * 2 + 1, 1)


def stage_combine(nc, I, O, v, s, S):
    x1, G, ln = v.x1_res, v.gate2[:, 0], v.ln2
    BUF = 3
    yg = v.cut(27576, BUF * TOPK, D)
    f = v.cut(21432, 2, D)
    bn = v.cut(23480, 2, 2, 6)
    mv = v.cut(23504, NT, 2)
    rs = v.cut(23514, NT, 2)
    dg = v.cut(23600, NT, TOPK, P)

    with nc.Block() as block:
        @block.sync
        def _(sp):
            for t in range(NT):
                sp.wait_ge(s["fin_ready"], t + 1) if t < NT - 1 else sp.wait_ge(s["norm2"], NT)
                if t < NP_T:
                    sp.dma_start(O["y_prompt"][0, t * P:(t + 1) * P, :], x1[:, t]).then_inc(s["fin_out"], 16)
                else:
                    sp.dma_start(O["y_sample"].rearrange("b t d -> (b t) d"), x1[:, t]).then_inc(s["fin_out"], 16)
            sp.wait_ge(s["fin_out"], 16 * NT)

        @block.gpsimd
        def _(pool):
            for t in range(NT):
                if t >= BUF:
                    pool.wait_ge(s["yg_read"], t - BUF + 1)
                for k in range(TOPK):
                    pool.indirect_dma_start(out=yg[:, (t % BUF) * TOPK + k], out_offset=None, in_=v.d_y,
                                            in_offset=bass.IndirectOffsetOnAxis(ap=v.slot[:, t, k:k + 1], axis=0)
                                            ).then_inc(s["yg_in"][t % BUF], 16)

            pool.wait_ge(s["f_in"], 16 * (3 + 1 + DEC_B))
            for t in range(NT - 1):
                pool.wait_ge(s["norm2"], t + 1)
                s["pool"](pool, pool.tensor_tensor(x1[:, t], x1[:, t], ln[:, 0], ALU.mult))
                pool.tensor_tensor(x1[:, t], x1[:, t], ln[:, 1], ALU.add).then_inc(s["fin_ready"], 1)

        @block.tensor
        def _(pe):
            for t in range(NT):
                pe.wait_ge(s["dg_ready"], t + 1)
                pe.wait_ge(s["yg_in"][t % BUF], 16 * TOPK * (t // BUF + 1))
                if t >= 4:
                    pe.wait_ge(s["gated"], t - 3)
                for k in range(TOPK):
                    for c in range(2):
                        ins = pe.matmul(S[2 * (t % 4) + c], dg[:, t, k, :],
                                        yg[:, (t % BUF) * TOPK + k, c * 512:(c + 1) * 512],
                                        start=(k == 0), stop=(k == TOPK - 1))
                ins.then_inc(s["yg_read"], 1)

        @block.scalar
        def _(act):
            for t in range(NT):
                act.wait_ge(s["var2"], t + 1)
                act.activation(rs[:, t, 1:2], rs[:, t, 0:1], ACT.Sqrt).then_inc(s["root2"], 1)

        @block.vector
        def _(dve):
            link = lambda ins: s["dve"](dve, ins)
            for t in range(NT):
                dve.tensor_tensor(dg[:, t], v.ident.unsqueeze(1).to_broadcast([P, TOPK, P]),
                                  v.wts[:, t, :].unsqueeze(2).to_broadcast([P, TOPK, P]), ALU.mult
                                  ).then_inc(s["dg_ready"], 1)
            dve.wait_ge(s["f_in"], 16 * (3 + 1 + DEC_B))
            for t in range(NT):
                who = 0 if t < NP_T else 1
                a = f[:, t % 2]
                dve.wait_ge(s["yg_read"], t + 1)
                b = 2 * (t % 4)
                dve.tensor_tensor(a, v.psum[:, b:b + 2, :].rearrange("p a n -> p (a n)"), G[:, who], ALU.mult
                                  ).then_inc(s["gated"], 1)
                dve.wait_ge(s["gated"], t + 1)
                link(dve.scalar_tensor_tensor(x1[:, t], x1[:, t], ALPHA, a, ALU.mult, ALU.add))
                for j in range(2):
                    ins = dve.bn_stats(bn[:, t % 2, j, :], x1[:, t, j * 512:(j + 1) * 512])
                link(ins)
                link(dve.bn_aggr(mv[:, t, :], bn[:, t % 2]))
                dve.tensor_scalar(rs[:, t, 0:1], mv[:, t, 1:2], EPS, None, ALU.add).then_inc(s["var2"], 1)
                dve.wait_ge(s["root2"], t + 1)
                link(dve.reciprocal(rs[:, t, 0:1], rs[:, t, 1:2]))
                ins = dve.tensor_scalar(x1[:, t], x1[:, t], mv[:, t, 0:1], rs[:, t, 0:1], ALU.subtract, ALU.mult)
                if t < NT - 1:
                    ins.then_inc(s["norm2"], 1)
            link(ins)
            link(dve.tensor_tensor(x1[:, NT - 1], x1[:, NT - 1], ln[:, 0], ALU.mult))
            dve.tensor_tensor(x1[:, NT - 1], x1[:, NT - 1], ln[:, 1], ALU.add).then_inc(s["norm2"], 1)


SEMS = """tr_out_dve G_in zeros_ready masked dg_ready gated C_out ml_ready gates_ready const_in crow_in crow_read
c_in c_sig c_silu bada_in x_in gq_in cT_acc cT_ready cw_ready ada_acc ada_out ssT_acc xT_acc uT_out
proj_acc proj_out pad_ready conv_done conv_sig ss_ready ss_root C_in out1 tail_ready tail_acc m_ready
C_new nT_ready n_in m0_in row_a act_row cols_acc cols_exp pre_acc W_ready D_ready num_acc nd_ready
tmp_ready var_ready rs_root gate_acc n_acc rows_done kw_ready C_zero n_cols nT_acc wu_in yz_out prep_out
prep_acc q_rot at_exp at_S at_T at_PT at_out at_O at_max new_in d_O ql_out ql_acc tr_out tr_acc d_exp d_S
p_out p_acc ol_ready ol_T ol_out datt_acc d_max wo_in x1_ready u2_ready x2_in rw_in mT_acc mT_out wo_acc
wo_read var1 root1 uT2_acc uT2_out lg_acc lg_read top_neg ex_ready hot_ready hot_acc sc2_ready mask_ready
pos_acc down_in y_acc idx_in idx_seen xg_in turned turn_out y_ready y_out y_stored bias_in glu_ready
sig_ready hid_ready up_acc glu_sum lin_ready glu_gated f_in fin_ready fin_out yg_read var2 root2 norm2""".split()

INPUTS = ("x_prompt x_sample c_prompt c_sample cache_ckv cache_kr state_C state_n state_m state_conv w_ada b_ada "
          "w_in b_if conv_w conv_b q_norm_g w_uq kv_norm_g w_uk w_uv ml_norm_g w_o ln1_g ln1_b router_w router_b "
          "w_up b_up w_down b_down ln2_g ln2_b").split()
OUTPUTS = {
    "y_prompt": (1, SEQ, D), "y_sample": (DEC_B, DEC_T, D),
    "new_ckv_p": (1, 1, SEQ, KV_LORA), "new_kr_p": (1, 1, SEQ, ROPE),
    "new_C_p": (1, 1, MH, MD, MD), "new_n_p": (1, 1, MH, MD), "new_m_p": (1, 1, MH), "new_conv_p": (1, 1, 3, 2 * MW),
    "new_ckv_s": (1, DEC_B, DEC_T, KV_LORA), "new_kr_s": (1, DEC_B, DEC_T, ROPE),
    "new_C_s": (1, DEC_B, MH, MD, MD), "new_n_s": (1, DEC_B, MH, MD), "new_m_s": (1, DEC_B, MH),
    "new_conv_s": (1, DEC_B, 3, 2 * MW),
}


def build(nc, I, O):
    from contextlib import ExitStack
    with ExitStack() as ctx:
        s = {n: ctx.enter_context(nc.semaphore(n)) for n in SEMS}
        s["ring_in"] = [ctx.enter_context(nc.semaphore("ring_in%d" % i)) for i in range(3)]
        s["cache_in"] = [ctx.enter_context(nc.semaphore("cache_in%d" % i)) for i in range(CB)]
        s["up_in"] = [[ctx.enter_context(nc.semaphore("up_in%d%d" % (i, j))) for j in range(2)] for i in range(2)]
        s["up_read"] = [ctx.enter_context(nc.semaphore("up_read%d" % i)) for i in range(2)]
        s["yg_in"] = [ctx.enter_context(nc.semaphore("yg_in%d" % i)) for i in range(3)]
        s["x1_out"] = [ctx.enter_context(nc.semaphore("x1_out%d" % i)) for i in range(2)]
        s["u2_out"] = [ctx.enter_context(nc.semaphore("u2_out%d" % i)) for i in range(2)]
        s["dve"] = Chain(ctx.enter_context(nc.semaphore("dve_step")))
        s["pool"] = Chain(ctx.enter_context(nc.semaphore("pool_step")))
        v = make_views(nc, ctx)
        v.psum = ctx.enter_context(nc.psum_tensor("psum", [P, 8, 512], F32))
        S = [v.psum[:, i, :] for i in range(8)]
        v.d_x1 = nc.dram_tensor("d_x1", (TOK, D), F32, kind="Internal").ap()
        v.d_u2 = nc.dram_tensor("d_u2", (TOK, D), F32, kind="Internal").ap()
        v.d_e9 = nc.dram_tensor("d_e9", (9, 6 * D), F32, kind="Internal").ap()
        v.d_y = nc.dram_tensor("d_y", (MAX_BLOCKS * P, D), F32, kind="Internal").ap()
        stage_project(nc, I, O, v, s, S)
        stage_mlstm(nc, I, O, v, s, S)
        stage_prompt_attention(nc, I, O, v, s, S)
        stage_decode_attention(nc, I, O, v, s, S)
        stage_output_router(nc, I, O, v, s, S)
        stage_experts(nc, I, O, v, s, S)
        stage_combine(nc, I, O, v, s, S)


def kernel(**inputs):
    import concourse.bacc as bacc
    from concourse.bass_utils import run_bass_kernel_spmd

    nc = bacc.Bacc("TRN2", target_bir_lowering=False, num_devices=1)
    arrays = {"in_" + n: np.ascontiguousarray(inputs[n]) for n in INPUTS}
    arrays["in_const"], arrays["in_rows"] = const_tables()
    I = {n[3:]: nc.dram_tensor(n, a.shape, F32, kind="ExternalInput").ap()
                           for n, a in arrays.items()}
    O = {n: nc.dram_tensor("out_" + n, shape, F32, kind="ExternalOutput").ap()
                           for n, shape in OUTPUTS.items()}
    build(nc, I, O)
    r = run_bass_kernel_spmd(nc, [arrays], core_ids=[0])
    return tuple(r.results[0]["out_" + n] for n in OUTPUTS)
```
